# Optimizing a Trainium2 kernel written in Bass

```python
import jax, jax.numpy as jnp
from jax import lax
import numpy as np
import math

D_MODEL = 1024
BATCH = 1
SEQ = 512
DEPTH = 1

N_MIXERS = 2
D_FF = 4 * D_MODEL
EPS = 1e-6

GLA_HEADS = 4
GLA_DK = D_MODEL // 2
GLA_DV = D_MODEL
GLA_HEAD_K = GLA_DK // GLA_HEADS
GLA_HEAD_V = GLA_DV // GLA_HEADS
GLA_GATE_RANK = 16
GLA_GATE_NORM = 16.0
GLA_CHUNK = 64
GLA_IN = 2 * GLA_DK + 2 * GLA_DV + GLA_GATE_RANK

FOX_HEADS = 16
FOX_HEAD_DIM = D_MODEL // FOX_HEADS
FOX_BLOCK = 128
FOX_IN = 3 * D_MODEL + FOX_HEADS + D_MODEL


def rms_norm(x, g):
    xf = x.astype(jnp.float32)
    y = xf * lax.rsqrt(jnp.mean(xf * xf, axis=-1, keepdims=True) + EPS)
    return (y * g.astype(jnp.float32)).astype(x.dtype)

def sqrelu_mlp(h, w1, w2):
    return jnp.square(jax.nn.relu(h @ w1)) @ w2

def gla_mixer(h, w_in, w_gk_up, b_gk, g_onorm, w_out):
    B, S, _ = h.shape
    C = GLA_CHUNK
    N = S // C
    proj = h @ w_in
    q, k, v, r, gk_low = jnp.split(
        proj, [GLA_DK, 2 * GLA_DK, 2 * GLA_DK + GLA_DV, 2 * GLA_DK + 2 * GLA_DV], axis=-1)
    log_a = jax.nn.log_sigmoid((gk_low @ w_gk_up + b_gk).astype(jnp.float32)) / GLA_GATE_NORM

    def to_chunks(t, dh):
        return t.astype(jnp.float32).reshape(B, N, C, GLA_HEADS, dh).transpose(1, 0, 3, 2, 4)

    qc = to_chunks(q, GLA_HEAD_K) * (GLA_HEAD_K ** -0.5)
    kc = to_chunks(k, GLA_HEAD_K)
    vc = to_chunks(v, GLA_HEAD_V)
    gc = to_chunks(log_a, GLA_HEAD_K)
    causal = jnp.tril(jnp.ones((C, C), dtype=bool))

    def step(state, inp):
        qb, kb, vb, gb = inp
        b = jnp.cumsum(gb, axis=-2)
        o_inter = jnp.einsum('bhck,bhkv->bhcv', qb * jnp.exp(b), state)
        diff = b[:, :, :, None, :] - b[:, :, None, :, :]
        decay = jnp.exp(jnp.where(causal[:, :, None], diff, -jnp.inf))
        attn = jnp.einsum('bhik,bhjk,bhijk->bhij', qb, kb, decay)
        o_intra = jnp.einsum('bhij,bhjv->bhiv', attn, vb)
        b_last = b[:, :, -1:, :]
        k_dec = kb * jnp.exp(b_last - b)
        state = state * jnp.exp(b_last[:, :, 0, :])[..., None] + jnp.einsum('bhck,bhcv->bhkv', k_dec, vb)
        return state, o_inter + o_intra

    state0 = jnp.zeros((B, GLA_HEADS, GLA_HEAD_K, GLA_HEAD_V), jnp.float32)
    _, o = lax.scan(step, state0, (qc, kc, vc, gc))
    o = o.transpose(1, 0, 3, 2, 4).reshape(B, S, GLA_HEADS, GLA_HEAD_V).astype(h.dtype)
    o = rms_norm(o, g_onorm).reshape(B, S, GLA_DV)
    return (o * jax.nn.silu(r)) @ w_out

def fox_mixer(h, w_in, b_f, g_q, g_k, w_out):
    B, S, _ = h.shape
    H, Dh = FOX_HEADS, FOX_HEAD_DIM
    nb = S // FOX_BLOCK
    proj = h @ w_in
    q, k, v, f_logit, o_gate = jnp.split(
        proj, [D_MODEL, 2 * D_MODEL, 3 * D_MODEL, 3 * D_MODEL + H], axis=-1)
    q = rms_norm(q.reshape(B, S, H, Dh), g_q).transpose(0, 2, 1, 3)
    k = rms_norm(k.reshape(B, S, H, Dh), g_k).transpose(0, 2, 1, 3)
    v = v.reshape(B, S, H, Dh).transpose(0, 2, 1, 3)
    log_f = jax.nn.log_sigmoid((f_logit + b_f).astype(jnp.float32))
    c = jnp.cumsum(log_f, axis=1).transpose(0, 2, 1)
    scale = Dh ** -0.5
    key_pos = jnp.arange(S)
    q_blocks = q.reshape(B, H, nb, FOX_BLOCK, Dh).transpose(2, 0, 1, 3, 4)
    c_blocks = c.reshape(B, H, nb, FOX_BLOCK).transpose(2, 0, 1, 3)

    def attend(args):
        qb, cq, blk = args
        s = jnp.einsum('bhqd,bhkd->bhqk', qb, k).astype(jnp.float32) * scale
        s = s + cq[..., None] - c[:, :, None, :]
        q_pos = blk * FOX_BLOCK + jnp.arange(FOX_BLOCK)
        s = jnp.where(key_pos[None, :] <= q_pos[:, None], s, -jnp.inf)
        p = jax.nn.softmax(s, axis=-1)
        return jnp.einsum('bhqk,bhkd->bhqd', p.astype(v.dtype), v)

    o = lax.map(attend, (q_blocks, c_blocks, jnp.arange(nb)))
    o = o.transpose(1, 0, 3, 2, 4).reshape(B, S, D_MODEL)
    return (o * jax.nn.sigmoid(o_gate)) @ w_out

def first_inputs(seed: int = 0) -> dict:
    key = jax.random.key(seed)
    ks = jax.random.split(key, 24)
    f32 = jnp.float32
    nrm = lambda k, shape, fan_in: jax.random.normal(k, shape, f32) * (fan_in ** -0.5)
    gain = lambda k, n: 1.0 + 0.05 * jax.random.normal(k, (n,), f32)
    return {
        "x": jax.random.normal(ks[0], (BATCH, SEQ, D_MODEL), f32),
        "l0_norm_mix": gain(ks[1], D_MODEL),
        "l0_w_in": nrm(ks[2], (D_MODEL, GLA_IN), D_MODEL),
        "l0_w_gk_up": nrm(ks[3], (GLA_GATE_RANK, GLA_DK), GLA_GATE_RANK),
        "l0_b_gk": 0.1 * jax.random.normal(ks[4], (GLA_DK,), f32),
        "l0_g_onorm": gain(ks[5], GLA_HEAD_V),
        "l0_w_out": nrm(ks[6], (GLA_DV, D_MODEL), GLA_DV),
        "l0_norm_ffn": gain(ks[7], D_MODEL),
        "l0_w_ff1": nrm(ks[8], (D_MODEL, D_FF), D_MODEL),
        "l0_w_ff2": nrm(ks[9], (D_FF, D_MODEL), D_FF),
        "l1_norm_mix": gain(ks[10], D_MODEL),
        "l1_w_in": nrm(ks[11], (D_MODEL, FOX_IN), D_MODEL),
        "l1_b_f": jax.random.uniform(ks[12], (FOX_HEADS,), f32, 1.0, 5.0),
        "l1_g_q": gain(ks[13], FOX_HEAD_DIM),
        "l1_g_k": gain(ks[14], FOX_HEAD_DIM),
        "l1_w_out": nrm(ks[15], (D_MODEL, D_MODEL), D_MODEL),
        "l1_norm_ffn": gain(ks[16], D_MODEL),
        "l1_w_ff1": nrm(ks[17], (D_MODEL, D_FF), D_MODEL),
        "l1_w_ff2": nrm(ks[18], (D_FF, D_MODEL), D_FF),
        "final_norm": gain(ks[19], D_MODEL),
    }

def first_block(x, l0_norm_mix, l0_w_in, l0_w_gk_up, l0_b_gk, l0_g_onorm, l0_w_out,
              l0_norm_ffn, l0_w_ff1, l0_w_ff2,
              l1_norm_mix, l1_w_in, l1_b_f, l1_g_q, l1_g_k, l1_w_out,
              l1_norm_ffn, l1_w_ff1, l1_w_ff2, final_norm):
    layers = (
        (l0_norm_mix, (l0_w_in, l0_w_gk_up, l0_b_gk, l0_g_onorm, l0_w_out), l0_norm_ffn, l0_w_ff1, l0_w_ff2),
        (l1_norm_mix, (l1_w_in, l1_b_f, l1_g_q, l1_g_k, l1_w_out), l1_norm_ffn, l1_w_ff1, l1_w_ff2),
    )
    mixers = (gla_mixer, fox_mixer)
    for i in range(DEPTH):
        norm_mix, mix_params, norm_ffn, w1, w2 = layers[i]
        x = x + mixers[i % N_MIXERS](rms_norm(x, norm_mix), *mix_params)
        x = x + sqrelu_mlp(rms_norm(x, norm_ffn), w1, w2)
    return rms_norm(x, final_norm)


GDN_HEAD_K = 128
GDN_HEAD_V = 128
GDN_HEADS = D_MODEL // GDN_HEAD_V
GDN_CONV = 4
GDN_CHUNK = 64
GDN_QK_DIM = GDN_HEADS * GDN_HEAD_K
GDN_V_DIM = GDN_HEADS * GDN_HEAD_V
GDN_CONV_DIM = 2 * GDN_QK_DIM + GDN_V_DIM

ATT_HEAD_DIM = 128
ATT_HEADS = D_MODEL // ATT_HEAD_DIM
ATT_KV_HEADS = 2
ATT_Q_DIM = ATT_HEADS * ATT_HEAD_DIM
ATT_KV_DIM = ATT_KV_HEADS * ATT_HEAD_DIM
IDX_HEADS = 8
IDX_DIM = 64
TOPK_MAX = 256
Q_BLOCK = 128

ROPE_THETA = 500000.0
ROPE_FRACTION = 4
D_FF_2 = 4 * D_MODEL

IN_SPLITS = (GDN_CONV_DIM, GDN_V_DIM, GDN_HEADS, GDN_HEADS,
             ATT_Q_DIM, ATT_KV_DIM, ATT_KV_DIM,
             IDX_HEADS * IDX_DIM, IDX_DIM, IDX_HEADS,
             D_MODEL, D_MODEL)
IN_PROJ_DIM = (GDN_CONV_DIM + GDN_V_DIM + 2 * GDN_HEADS + ATT_Q_DIM + 2 * ATT_KV_DIM
               + IDX_HEADS * IDX_DIM + IDX_DIM + IDX_HEADS + 2 * D_MODEL)


def rms_norm_2(x, g):
    xf = x.astype(jnp.float32)
    y = xf * lax.rsqrt(jnp.mean(xf * xf, axis=-1, keepdims=True) + EPS)
    return (y * g.astype(jnp.float32)).astype(x.dtype)

def l2_normalize(x):
    xf = x.astype(jnp.float32)
    return xf * lax.rsqrt(jnp.sum(xf * xf, axis=-1, keepdims=True) + EPS)

def rope_tables(seq, rot_dim):
    inv_freq = ROPE_THETA ** (-jnp.arange(0, rot_dim, 2, dtype=jnp.float32) / rot_dim)
    ang = jnp.arange(seq, dtype=jnp.float32)[:, None] * inv_freq[None, :]
    return jnp.cos(ang), jnp.sin(ang)

def apply_partial_rope(t, cos, sin):
    half = cos.shape[-1]
    shape = (t.shape[1],) + (1,) * (t.ndim - 3) + (half,)
    c, s = cos.reshape(shape), sin.reshape(shape)
    tf = t.astype(jnp.float32)
    x1, x2 = tf[..., :half], tf[..., half:2 * half]
    out = jnp.concatenate([x1 * c - x2 * s, x2 * c + x1 * s, tf[..., 2 * half:]], axis=-1)
    return out.astype(t.dtype)

def causal_short_conv(u, w):
    k = w.shape[0]
    s = u.shape[1]
    up = jnp.pad(u, ((0, 0), (k - 1, 0), (0, 0)))
    y = up[:, 0:s] * w[0]
    for j in range(1, k):
        y = y + up[:, j:j + s] * w[j]
    return y

def gated_delta_rule_chunked(q, k, v, g, beta):
    B, S, H, dk = q.shape
    dv = v.shape[-1]
    C = GDN_CHUNK
    N = S // C
    f32 = jnp.float32

    def chunks(t):
        t = jnp.swapaxes(t.astype(f32), 1, 2)
        return t.reshape((B, H, N, C) + t.shape[3:])

    q, k, v, g, beta = chunks(q), chunks(k), chunks(v), chunks(g), chunks(beta)
    g_cum = jnp.cumsum(g, axis=-1)
    pos = jnp.arange(C)
    incl = pos[:, None] >= pos[None, :]
    strict = pos[:, None] > pos[None, :]
    diff = g_cum[..., :, None] - g_cum[..., None, :]
    decay = jnp.where(incl, jnp.exp(jnp.where(incl, diff, 0.0)), 0.0)
    k_beta = k * beta[..., None]
    a_mat = jnp.where(strict, jnp.einsum('bhnid,bhnjd->bhnij', k_beta, k) * decay, 0.0)
    lhs = a_mat + jnp.eye(C, dtype=f32)
    rhs = jnp.concatenate([v * beta[..., None], k_beta * jnp.exp(g_cum)[..., None]], axis=-1)
    sol = lax.linalg.triangular_solve(lhs, rhs, left_side=True, lower=True, unit_diagonal=True)
    u, w = sol[..., :dv], sol[..., dv:]
    qk = jnp.where(incl, jnp.einsum('bhnid,bhnjd->bhnij', q, k) * decay, 0.0)
    q_dec = q * jnp.exp(g_cum)[..., None]
    g_last = g_cum[..., -1]
    k_dec = k * jnp.exp(g_last[..., None] - g_cum)[..., None]

    def step(state, xs):
        u_n, w_n, qk_n, q_n, k_n, gl_n = xs
        v_new = u_n - jnp.einsum('bhcd,bhde->bhce', w_n, state)
        o_n = (jnp.einsum('bhcd,bhde->bhce', q_n, state)
               + jnp.einsum('bhij,bhje->bhie', qk_n, v_new))
        state = state * jnp.exp(gl_n)[..., None, None] + jnp.einsum('bhcd,bhce->bhde', k_n, v_new)
        return state, o_n

    xs = tuple(jnp.moveaxis(t, 2, 0) for t in (u, w, qk, q_dec, k_dec, g_last))
    state0 = jnp.zeros((B, H, dk, dv), f32)
    _, o = lax.scan(step, state0, xs)
    o = jnp.moveaxis(o, 0, 2).reshape(B, H, S, dv)
    return jnp.swapaxes(o, 1, 2)

def dsa_sparse_attention(q, k, v, q_idx, k_idx, w_idx):
    B, S, H, hd = q.shape
    kvh = k.shape[2]
    grp = H // kvh
    n_blk = S // Q_BLOCK
    k_sel = min(TOPK_MAX, S // 4)
    scale = hd ** -0.5
    key_pos = jnp.arange(S, dtype=jnp.int32)
    k_idx_f = k_idx.astype(jnp.float32)

    def to_blocks(t):
        return jnp.moveaxis(t.reshape((B, n_blk, Q_BLOCK) + t.shape[2:]), 1, 0)

    def block(args):
        blk, qb, qib, wb = args
        t = blk * Q_BLOCK + jnp.arange(Q_BLOCK, dtype=jnp.int32)
        logits = jnp.einsum('bqhd,bsd->bqhs', qib.astype(jnp.float32), k_idx_f)
        score = jnp.einsum('bqh,bqhs->bqs', wb.astype(jnp.float32), jax.nn.relu(logits))
        causal = key_pos[None, :] <= t[:, None]
        score = jnp.where(causal[None], score, -jnp.inf)
        _, sel = lax.top_k(score, k_sel)
        valid = sel <= t[None, :, None]
        k_g = jax.vmap(lambda kb, ib: kb[ib])(k, sel)
        v_g = jax.vmap(lambda vb, ib: vb[ib])(v, sel)
        qg = qb.reshape(B, Q_BLOCK, kvh, grp, hd)
        s = jnp.einsum('bqcgd,bqncd->bqcgn', qg, k_g).astype(jnp.float32) * scale
        s = jnp.where(valid[:, :, None, None, :], s, -jnp.inf)
        p = jax.nn.softmax(s, axis=-1).astype(v_g.dtype)
        o = jnp.einsum('bqcgn,bqncd->bqcgd', p, v_g)
        return o.reshape(B, Q_BLOCK, H * hd)

    o = lax.map(block, (jnp.arange(n_blk, dtype=jnp.int32), to_blocks(q),
                        to_blocks(q_idx), to_blocks(w_idx)))
    return jnp.moveaxis(o, 0, 1).reshape(B, S, H * hd)

def hybrid_layer(x, norm_mix_g, w_in, conv_w, a_log, dt_bias, gdn_norm_g,
                 q_norm_g, k_norm_g, w_out, norm_mlp_g, w_mlp_up, w_mlp_down):
    B, S, _ = x.shape
    h = rms_norm_2(x, norm_mix_g)
    proj = h @ w_in
    points = np.cumsum(np.array(IN_SPLITS))[:-1].tolist()
    (g_qkv, g_z, g_a, g_b, a_q, a_k, a_v,
     i_q, i_k, i_w, gate_a, gate_b) = jnp.split(proj, points, axis=-1)

    qkv = jax.nn.silu(causal_short_conv(g_qkv, conv_w))
    gq, gk, gv = jnp.split(qkv, [GDN_QK_DIM, 2 * GDN_QK_DIM], axis=-1)
    gq = l2_normalize(gq.reshape(B, S, GDN_HEADS, GDN_HEAD_K)) * (GDN_HEAD_K ** -0.5)
    gk = l2_normalize(gk.reshape(B, S, GDN_HEADS, GDN_HEAD_K))
    gv = gv.reshape(B, S, GDN_HEADS, GDN_HEAD_V)
    beta = jax.nn.sigmoid(g_b.astype(jnp.float32))
    g = -jnp.exp(a_log.astype(jnp.float32)) * jax.nn.softplus(
        g_a.astype(jnp.float32) + dt_bias.astype(jnp.float32))
    o_gdn = gated_delta_rule_chunked(gq, gk, gv, g, beta)
    z = jax.nn.silu(g_z.reshape(B, S, GDN_HEADS, GDN_HEAD_V).astype(jnp.float32))
    o_gdn = (rms_norm_2(o_gdn, gdn_norm_g) * z).reshape(B, S, GDN_V_DIM).astype(x.dtype)

    cos, sin = rope_tables(S, ATT_HEAD_DIM // ROPE_FRACTION)
    a_q = apply_partial_rope(rms_norm_2(a_q.reshape(B, S, ATT_HEADS, ATT_HEAD_DIM), q_norm_g), cos, sin)
    a_k = apply_partial_rope(rms_norm_2(a_k.reshape(B, S, ATT_KV_HEADS, ATT_HEAD_DIM), k_norm_g), cos, sin)
    a_v = a_v.reshape(B, S, ATT_KV_HEADS, ATT_HEAD_DIM)
    cos_i, sin_i = rope_tables(S, IDX_DIM // ROPE_FRACTION)
    i_q = apply_partial_rope(i_q.reshape(B, S, IDX_HEADS, IDX_DIM), cos_i, sin_i)
    i_k = apply_partial_rope(i_k, cos_i, sin_i)
    i_w = i_w * (IDX_HEADS ** -0.5 * IDX_DIM ** -0.5)
    o_att = dsa_sparse_attention(a_q, a_k, a_v, i_q, i_k, i_w).astype(x.dtype)

    merged = jax.nn.sigmoid(gate_a) * o_gdn + jax.nn.sigmoid(gate_b) * o_att
    x = x + merged @ w_out

    h2 = rms_norm_2(x, norm_mlp_g)
    x = x + jnp.square(jax.nn.relu(h2 @ w_mlp_up)) @ w_mlp_down
    return x

def second_inputs(seed: int = 0) -> dict:
    key = jax.random.key(seed)
    ks = jax.random.split(key, 14)
    f32 = jnp.float32

    def gain(k, n):
        return 1.0 + 0.02 * jax.random.normal(k, (DEPTH, n), f32)

    x = jax.random.normal(ks[0], (BATCH, SEQ, D_MODEL), f32)
    norm_mix_g = gain(ks[1], D_MODEL)
    w_in = jax.random.normal(ks[2], (DEPTH, D_MODEL, IN_PROJ_DIM), f32) * D_MODEL ** -0.5
    conv_w = jax.random.normal(ks[3], (DEPTH, GDN_CONV, GDN_CONV_DIM), f32) * GDN_CONV ** -0.5
    a_log = jnp.log(jax.random.uniform(ks[4], (DEPTH, GDN_HEADS), f32, 1.0, 16.0))
    dt = jnp.exp(jax.random.uniform(ks[5], (DEPTH, GDN_HEADS), f32, math.log(1e-3), math.log(1e-1)))
    dt_bias = dt + jnp.log(-jnp.expm1(-dt))
    gdn_norm_g = gain(ks[6], GDN_HEAD_V)
    q_norm_g = gain(ks[7], ATT_HEAD_DIM)
    k_norm_g = gain(ks[8], ATT_HEAD_DIM)
    w_out = jax.random.normal(ks[9], (DEPTH, D_MODEL, D_MODEL), f32) * D_MODEL ** -0.5
    norm_mlp_g = gain(ks[10], D_MODEL)
    w_mlp_up = jax.random.normal(ks[11], (DEPTH, D_MODEL, D_FF_2), f32) * D_MODEL ** -0.5
    w_mlp_down = jax.random.normal(ks[12], (DEPTH, D_FF_2, D_MODEL), f32) * D_FF_2 ** -0.5
    return {"x": x, "norm_mix_g": norm_mix_g, "w_in": w_in, "conv_w": conv_w,
            "a_log": a_log, "dt_bias": dt_bias, "gdn_norm_g": gdn_norm_g,
            "q_norm_g": q_norm_g, "k_norm_g": k_norm_g, "w_out": w_out,
            "norm_mlp_g": norm_mlp_g, "w_mlp_up": w_mlp_up, "w_mlp_down": w_mlp_down}

def second_block(x, norm_mix_g, w_in, conv_w, a_log, dt_bias, gdn_norm_g, q_norm_g, k_norm_g,
              w_out, norm_mlp_g, w_mlp_up, w_mlp_down):
    for layer in range(DEPTH):
        x = hybrid_layer(x, norm_mix_g[layer], w_in[layer], conv_w[layer], a_log[layer],
                         dt_bias[layer], gdn_norm_g[layer], q_norm_g[layer], k_norm_g[layer],
                         w_out[layer], norm_mlp_g[layer], w_mlp_up[layer], w_mlp_down[layer])
    return x


def setup_inputs(seed=0):
    out = dict(first_inputs(seed))
    for name, value in second_inputs(seed + 1).items():
        if name != "x":
            out[name + "_2"] = value
    return out


def reference(
    x, l0_norm_mix, l0_w_in, l0_w_gk_up, l0_b_gk, l0_g_onorm, l0_w_out, l0_norm_ffn, l0_w_ff1,
    l0_w_ff2, l1_norm_mix, l1_w_in, l1_b_f, l1_g_q, l1_g_k, l1_w_out, l1_norm_ffn, l1_w_ff1,
    l1_w_ff2, final_norm, norm_mix_g_2, w_in_2, conv_w_2, a_log_2, dt_bias_2, gdn_norm_g_2,
    q_norm_g_2, k_norm_g_2, w_out_2, norm_mlp_g_2, w_mlp_up_2, w_mlp_down_2,
):
    x = first_block(
        x, l0_norm_mix, l0_w_in, l0_w_gk_up, l0_b_gk, l0_g_onorm, l0_w_out, l0_norm_ffn,
        l0_w_ff1, l0_w_ff2, l1_norm_mix, l1_w_in, l1_b_f, l1_g_q, l1_g_k, l1_w_out, l1_norm_ffn,
        l1_w_ff1, l1_w_ff2, final_norm,
    )
    return second_block(
        x, norm_mix_g_2, w_in_2, conv_w_2, a_log_2, dt_bias_2, gdn_norm_g_2, q_norm_g_2,
        k_norm_g_2, w_out_2, norm_mlp_g_2, w_mlp_up_2, w_mlp_down_2,
    )


_drawn_inputs = setup_inputs


def setup_inputs(seed=0):
    import zlib

    import numpy as np

    out = dict(_drawn_inputs(seed))
    spreads = {}
    factors = {'norm_mix_g_2': 3.689,
     'gdn_norm_g_2': 7.784,
     'q_norm_g_2': 8.0,
     'k_norm_g_2': 8.0,
     'norm_mlp_g_2': 11.252}
    for name, (base, spread) in spreads.items():
        noise = np.random.default_rng([zlib.crc32(name.encode()), seed]).standard_normal(out[name].shape)
        drawn = base * np.exp(spread * noise) if base else spread * noise
        out[name] = __import__('jax').numpy.asarray(drawn.astype(out[name].dtype))
    for name, factor in factors.items():
        out[name] = (out[name] * factor).astype(out[name].dtype)
    return out
```

```python
from contextlib import ExitStack

import numpy as np

import concourse.bass as bass
from concourse import mybir

F32 = mybir.dt.float32
F32R = mybir.dt.float32r
U32 = mybir.dt.uint32
ALU = mybir.AluOpType
ACT = mybir.ActivationFunctionType
AX = mybir.AxisListType

P = 128
SEQ, D, DFF = 512, 1024, 4096
KT = D // P
TT = SEQ // P
EPS = 1e-6
CHUNK = 64
NCH = SEQ // CHUNK
LEVELS = 6

GLA_H, GLA_K, GLA_V = 4, 128, 256
GLA_RANK = 16
GLA_GATE_NORM = 16.0
GLA_Q0, GLA_K0, GLA_V0, GLA_R0, GLA_G0 = 0, 512, 1024, 2048, 3072

GDN_H = 8
QKV0, Z0 = 0, 3072
GA0 = 4096
GB0 = GA0 + GDN_H
AQ0 = GB0 + GDN_H
AK0 = AQ0 + D
AV0 = AK0 + 256
IQ0 = AV0 + 256
IK0 = IQ0 + 512
IW0 = IK0 + 64
GTA0 = IW0 + 8
GTB0 = GTA0 + D
CONV = 4
ATT_H, ATT_KV = 8, 2
IDX_H, IDX_D = 8, 64
TOPK = min(256, SEQ // 4)
NOT_CAUSAL = -3.0e38
TAKEN = -3.4e38
BIG = 1.0e30

G_MIX0, G_FFN0, G_FINAL, G_MIX1, G_MLP1 = 0, 8, 16, 24, 32
G_BGK, G_ON, G_GDN, G_QN, G_KN = 40, 44, 46, 47, 48
N_GAIN = 49


def host_constants():
    j, i = np.meshgrid(np.arange(P), np.arange(P), indexing="ij")
    same = (j // CHUNK) == (i // CHUNK)
    masks = [(j == i)]
    for lv in range(LEVELS):
        s = 1 << lv
        masks.append((j // (2 * s) == i // (2 * s)) & (j % (2 * s) < s) & (i % (2 * s) >= s))
    masks.append(same & (j <= i))
    masks = np.stack(masks, 1).astype(np.float32)
    ident = np.eye(P, dtype=np.float32)

    def rope(seq, rot, width):
        inv = (np.float32(500000.0) ** (-np.arange(0, rot, 2, dtype=np.float32) / np.float32(rot))).astype(np.float32)
        ang = (np.arange(seq, dtype=np.float32)[:, None] * inv[None, :]).astype(np.float32)
        half = rot // 2
        c = np.ones((P, seq), np.float32)
        s = np.zeros((P, seq), np.float32)
        swap = np.zeros((P, P), np.float32)
        for b in range(0, P, width):
            for f in range(half):
                c[b + f] = c[b + half + f] = np.cos(ang[:, f])
                s[b + f] = s[b + half + f] = np.sin(ang[:, f])
                swap[b + half + f, b + f] = -1.0
                swap[b + f, b + half + f] = 1.0
        return c, s, swap

    ca, sa, pa = rope(SEQ, 32, P)
    ci, si, pi = rope(SEQ, 16, IDX_D)
    keep = np.ones((P, SEQ), np.float32)
    keep[:, ::CHUNK] = 0.0
    square = np.concatenate([ident, masks.reshape(P, -1), pa, pi], axis=1)
    wide = np.stack([ca, sa, ci, si, keep], 0)
    return square, wide


def build(nc, t, out, const_square, const_wide, upto=99):
    with ExitStack() as ctx:
        def sb(name, shape, dt=F32):
            return ctx.enter_context(nc.sbuf_tensor(name, shape, dt))

        def sem(name):
            return ctx.enter_context(nc.semaphore(name))

        s = {}

        cleared = []

        def sems(names, reuse=False):
            got = []
            for name in names.split():
                s[name] = cleared.pop() if reuse and cleared else sem(name)
                got.append(s[name])
            return got

        raw = [sb(f"raw{b}", [P, KT, P]) for b in range(2)]
        w_hi = [sb(f"w_hi{b}", [P, KT, P], F32R) for b in range(2)]
        w_lo = [sb(f"w_lo{b}", [P, KT, P], F32R) for b in range(2)]
        h_hi, h_lo = sb("h_hi", [P, KT, SEQ], F32R), sb("h_lo", [P, KT, SEQ], F32R)
        m_hi, m_lo = sb("m_hi", [P, KT, SEQ], F32R), sb("m_lo", [P, KT, SEQ], F32R)
        x = sb("x", [P, KT, SEQ])
        ident = sb("ident", [P, P])
        masks = sb("masks", [P, LEVELS + 2, P])
        swap_a, swap_i = sb("swap_a", [P, P]), sb("swap_i", [P, P])
        ones = sb("ones", [P, P])
        gains = sb("gains", [P, N_GAIN])
        conv_w = sb("conv_w", [P, CONV * 3 * GDN_H])
        eps = sb("eps", [P, 1])
        arena = sb("arena", [P, 22400])
        at = [0]

        def take(*shape):
            n = int(np.prod(shape))
            v = arena[:, at[0]:at[0] + n]
            at[0] += n
            assert at[0] <= 22400, at[0]
            if len(shape) == 2:
                v = v.rearrange("p (a b) -> p a b", a=shape[0])
            if len(shape) == 3:
                v = v.rearrange("p (a b c) -> p a b c", a=shape[0], b=shape[1])
            return v

        bank = [ctx.enter_context(nc.psum_tensor(f"bank{i}", [P, SEQ], F32)) for i in range(8)]
        g_bank, b = bank[0:2], bank[2:8]

        def tiles(ap, n=TT):
            return ap.rearrange("p (t c) -> p t c", t=n)

        def mask(lv):
            return masks[:, lv, :].unsqueeze(1).broadcast_to([P, TT, P])

        sems("piece_in w_hi_ready w_ready phase_done x_in params_in consts_in out_done")
        raw_in = [sem(f"raw_in{i}") for i in range(2)]
        mm_done = [sem(f"mm_done{i}") for i in range(2)]
        bank_free = [sem(f"bank_free{i}") for i in range(2)]
        pieces_sent = [0]

        class Panel:

            def __init__(self, base, per, h, u):
                self.par = (base + u) % 2
                self.n = base + u + per * h
                self.k = (base + u - self.par) // 2 + (per // 2) * h
                self.key = (base, per, h, u)

            def next(self):
                base, per, h, u = self.key
                return Panel(base, per, h, u + 1)

        def load(sp, q, pieces):
            sp.wait_ge(s["w_ready"], q.n + 1)
            for i, (src, c) in enumerate(pieces):
                if i == len(pieces) - 1:
                    if i:
                        sp.wait_ge(s["piece_in"], 16 * pieces_sent[0])
                    sp.dma_start(raw[q.par][:, :, c:c + src.shape[2]], src).then_inc(raw_in[q.par], 16)
                else:
                    sp.dma_start(raw[q.par][:, :, c:c + src.shape[2]], src).then_inc(s["piece_in"], 16)
                    pieces_sent[0] += 1

        def act_split(act, q):
            act.wait_ge(raw_in[q.par], 16 * (q.k + 1))
            act.wait_ge(mm_done[q.par], q.k + 1)
            act.copy(w_hi[q.par][:], raw[q.par][:]).then_inc(s["w_hi_ready"], 1)

        def dve_split(dve, q):
            dve.wait_ge(s["w_hi_ready"], q.n + 1)
            dve.tensor_tensor(w_lo[q.par][:], raw[q.par][:], w_hi[q.par][:].bitcast(F32),
                              ALU.subtract).then_inc(s["w_ready"], 1)

        def pe_panel(pe, q, hi, lo, ready=None, count=0):
            pe.wait_ge(s["w_ready"], q.n + 3)
            pe.wait_ge(bank_free[q.par], q.k + 1)
            for k in range(KT):
                if ready is not None:
                    pe.wait_ge(ready, count + k + 1)
                pe.matmul(g_bank[q.par][:], w_hi[q.par][:, k], hi[:, k], start=(k == 0), stop=False)
                pe.matmul(g_bank[q.par][:], w_hi[q.par][:, k], lo[:, k], start=False, stop=False)
                last = pe.matmul(g_bank[q.par][:], w_lo[q.par][:, k], hi[:, k], start=False, stop=(k == KT - 1))
            last.then_inc(mm_done[q.par], 1)

        def wait_panel(eng, q):
            eng.wait_ge(mm_done[q.par], q.k + 2)

        N_GK = 0
        N_GLA = 1
        N_WO0 = N_GLA + 6 * GLA_H
        N_FF0 = N_WO0 + KT
        GROUPS = DFF // D
        N_IN1 = N_FF0 + 16 * GROUPS
        N_ATT = N_IN1 + 10
        N_GDN = N_ATT + 2 * ATT_H
        N_WO1 = N_GDN + 5 * GDN_H
        N_FF1 = N_WO1 + KT
        N_END = N_FF1 + 16 * GROUPS

        def rows(w):
            return w.rearrange("(k p) c -> p k c", p=P)

        def fence(eng, p):
            eng.drain().then_inc(s["phase_done"], 1)
            eng.wait_ge(s["phase_done"], 4 * p)

        at[0] = 0
        x_tok = take(TT, D)
        par_rows = take(2, P)
        sems("x_t x_s memsets par_t par_s")

        def sp_start(sp):
            gain_rows = [("l0_norm_mix", G_MIX0, 8), ("l0_norm_ffn", G_FFN0, 8), ("final_norm", G_FINAL, 8),
                         ("norm_mix_g_2", G_MIX1, 8), ("norm_mlp_g_2", G_MLP1, 8), ("l0_b_gk", G_BGK, 4),
                         ("l0_g_onorm", G_ON, 2), ("gdn_norm_g_2", G_GDN, 1), ("q_norm_g_2", G_QN, 1),
                         ("k_norm_g_2", G_KN, 1)]
            xv = t["x"].rearrange("b (t p) d -> p (b t) d", p=P)
            sp.dma_start(x_tok, xv).then_inc(s["x_in"], 16)
            sp.dma_start(ident[:], const_square[:, 0:P]).then_inc(s["x_in"], 16)
            load(sp, Panel(N_GK, 0, 0, 0), [(rows(t["l0_w_in"])[:, :, GLA_G0:GLA_G0 + 16], 0),
                                            (rows(t["l0_w_in"])[:, :, 0:P - 16], 16)])
            for name, r, n in gain_rows:
                a = t[name]
                if len(a.shape) == 2:
                    a = a.rearrange("a d -> (a d)")
                sp.dma_start(par_rows[r:r + n, 0, :], a.rearrange("(k p) -> k p", p=P)).then_inc(s["params_in"], 16)
            sp.dma_start(par_rows[0:CONV * 24, 1, :],
                         t["conv_w_2"].rearrange("a j (c p) -> (a j c) p", p=P)).then_inc(s["params_in"], 16)
            c0 = P
            sp.dma_start(masks[:], const_square[:, c0:c0 + 8 * P].rearrange("p (l c) -> p l c", c=P)).then_inc(s["consts_in"], 16)
            sp.dma_start(swap_a[:], const_square[:, c0 + 8 * P:c0 + 9 * P]).then_inc(s["consts_in"], 16)
            sp.dma_start(swap_i[:], const_square[:, c0 + 9 * P:c0 + 10 * P]).then_inc(s["consts_in"], 16)

        PARAM_DMAS = 11

        def pe_start(pe):
            pe.sem_inc(mm_done[0], 1)
            pe.sem_inc(mm_done[1], 1)
            pe.wait_ge(s["x_in"], 32)
            for k in range(KT):
                if k >= 2:
                    pe.wait_ge(s["x_s"], k - 1)
                for tt in range(TT):
                    last = pe.transpose(b[k % 2][:, tt * P:(tt + 1) * P], x_tok[:, tt, k * P:(k + 1) * P], ident[:])
                last.then_inc(s["x_t"], 1)
            pe.wait_ge(s["params_in"], 16 * PARAM_DMAS)
            pe.transpose(b[2][:, 0:N_GAIN], par_rows[0:N_GAIN, 0, :], ident[0:N_GAIN, 0:N_GAIN]).then_inc(s["par_t"], 1)
            n = CONV * 24
            pe.transpose(b[3][:, 0:n], par_rows[0:n, 1, :], ident[0:n, 0:n]).then_inc(s["par_t"], 1)

        def act_start(act):
            for k in range(KT):
                act.wait_ge(s["x_t"], k + 1)
                act.copy(x[:, k], b[k % 2][:]).then_inc(s["x_s"], 1)
            act.wait_ge(s["par_t"], 1)
            act.copy(gains[:], b[2][:, 0:N_GAIN]).then_inc(s["par_s"], 1)
            act.wait_ge(s["par_t"], 2)
            act.copy(conv_w[:], b[3][:, 0:CONV * 24]).then_inc(s["par_s"], 1)

        def dve_start(dve):
            dve.sem_inc(s["w_ready"], 2)
            dve.sem_inc(bank_free[0], 1)
            dve.sem_inc(bank_free[1], 1)
            dve.memset(ones[:], 1.0).then_inc(s["memsets"], 1)
            dve.memset(eps[:], EPS).then_inc(s["memsets"], 1)
            dve.wait_ge(s["par_s"], 2)
            dve.tensor_scalar(gains[:, G_ON:G_ON + 3], gains[:, G_ON:G_ON + 3], 0.5, None, ALU.mult).then_inc(s["memsets"], 1)

        sems("n_sq n_acc n_ss n_ln n_r n_h n_hi h_ready")
        norm_uses = [0]

        class Norm:
            def __init__(self, gain, split):
                self.i, self.gain, self.split = norm_uses[0], gain, split
                self.j = sum(1 for q in norm_list if q.split)
                norm_uses[0] += 1
                norm_list.append(self)

        norm_list = []

        def norm_bufs():
            return take(2, SEQ), take(SEQ), take(SEQ), take(2, SEQ)

        def act_norm(act, nm, bufs):
            sq, acc, r, hb = bufs
            i = nm.i
            for k in range(KT):
                if k >= 2:
                    act.wait_ge(s["n_acc"], KT * i + k - 1)
                act.activation(sq[:, k % 2], x[:, k], ACT.Square).then_inc(s["n_sq"], 1)
            act.wait_ge(s["n_ss"], i + 1)
            act.activation(r, b[0][:], ACT.Ln, scale=1.0 / D, bias=eps[:]).then_inc(s["n_ln"], 1)
            act.wait_ge(s["n_ln"], i + 1)
            act.activation(r, r, ACT.Exp, scale=-0.5).then_inc(s["n_r"], 1)
            if nm.split:
                for k in range(KT):
                    act.wait_ge(s["n_h"], KT * i + k + 1)
                    act.copy(h_hi[:, k], hb[:, k % 2]).then_inc(s["n_hi"], 1)

        def dve_norm(dve, nm, bufs):
            sq, acc, r, hb = bufs
            i = nm.i
            for k in range(KT):
                dve.wait_ge(s["n_sq"], KT * i + k + 1)
                if k == 0:
                    dve.tensor_copy(acc, sq[:, 0]).then_inc(s["n_acc"], 1)
                else:
                    dve.wait_ge(s["n_acc"], KT * i + k)
                    dve.tensor_tensor(acc, acc, sq[:, k % 2], ALU.add).then_inc(s["n_acc"], 1)
            dve.wait_ge(s["n_r"], i + 1)
            for k in range(KT):
                g = gains[:, nm.gain + k:nm.gain + k + 1]
                if nm.split:
                    if k >= 2:
                        dve.wait_ge(s["h_ready"], KT * nm.j + k - 1)
                    dve.scalar_tensor_tensor(hb[:, k % 2], x[:, k], g, r, ALU.mult, ALU.mult).then_inc(s["n_h"], 1)
                    if k >= 1:
                        dve_norm_lo(dve, nm, hb, k - 1)
                else:
                    dve.scalar_tensor_tensor(x[:, k], x[:, k], g, r, ALU.mult, ALU.mult).then_inc(s["n_h"], 1)
            if nm.split:
                dve_norm_lo(dve, nm, hb, KT - 1)
            else:
                dve.wait_ge(s["n_h"], KT * (i + 1))

        def dve_norm_lo(dve, nm, hb, k):
            dve.wait_ge(s["n_hi"], KT * nm.j + k + 1)
            dve.tensor_tensor(h_lo[:, k], hb[:, k % 2], h_hi[:, k].bitcast(F32), ALU.subtract).then_inc(s["h_ready"], 1)

        def pe_norm(pe, nm, bufs):
            sq, acc, r, hb = bufs
            pe.wait_ge(s["n_acc"], KT * (nm.i + 1))
            pe.matmul(b[0][:], ones[:], acc, start=True, stop=True).then_inc(s["n_ss"], 1)

        at[0] = 0
        nb0 = norm_bufs()
        nm0 = Norm(G_MIX0, True)
        keep = take(SEQ)
        gk_up = take(512)
        gk_low = take(SEQ)
        b_all = take(GLA_H, SEQ)
        gt = take(2, SEQ)
        qf, kf = take(SEQ), take(SEQ)
        vf = take(2, SEQ)
        v_tok = take(TT, GLA_V)
        gate = take(2, SEQ)
        arg = take(2, SEQ)
        ex = take(2, SEQ)
        mlev = take(2, SEQ)
        sm = take(2, SEQ)
        a_t = take(TT, P)
        eb, qe, kd = take(SEQ), take(SEQ), take(SEQ)
        kd_tok = take(TT, P)
        state = take(NCH, GLA_V)
        osq, yb = ex, vf
        rb = take(SEQ)
        sems("gk_in")
        gate_sems = sems("gkl gk_ps ga ge gl gm gd gscan gbs")
        gla_sems = sems("q_in k_in v_in vt_ps vt_sb tg gate_r arg_r ab_r ex_r mlev_r slev at_r eb_r qe_r kd_r kdt_ps kdt_sb "
             "u_ps sm_r st_r o_ps osq_r osum on_ps oln or_r y1 y2 y_hi gla_done")

        def u_at(c):
            o = (c // 2 % 2) * GLA_V
            return b[2 + 2 * (c % 2) + c // 4][:, o:o + GLA_V]

        def sp_gla(sp):
            sp.wait_ge(s["phase_done"], 4)
            sp.dma_start(keep, const_wide[4]).then_inc(s["gk_in"], 16)
            sp.dma_start(gk_up[0:GLA_RANK, :], t["l0_w_gk_up"]).then_inc(s["gk_in"], 16)
            w = rows(t["l0_w_in"])
            with sp.Fori(0, GLA_H) as h:
                starts = [GLA_Q0 + P * h, GLA_K0 + P * h, GLA_V0 + 2 * P * h, GLA_V0 + P + 2 * P * h,
                          GLA_R0 + 2 * P * h, GLA_R0 + P + 2 * P * h]
                for u, c in enumerate(starts):
                    load(sp, Panel(N_GLA, 6, h, u), [(w[:, :, bass.ds(c, P)], 0)])

        def pe_gates(pe):
            pe_panel(pe, Panel(N_GK, 0, 0, 0), h_hi, h_lo, s["h_ready"], 0)
            pe.wait_ge(s["gk_in"], 32)
            pe.wait_ge(s["gkl"], 1)
            for h in range(GLA_H):
                if h >= 2:
                    pe.wait_ge(s["gm"], h - 1)
                    pe.wait_ge(s["ga"], h - 1)
                pe.matmul(b[h % 2][:], gk_up[0:GLA_RANK, h * P:(h + 1) * P], gk_low[0:GLA_RANK, :],
                          start=True, stop=True).then_inc(s["gk_ps"], 1)

        def act_gates(act):
            q = Panel(N_GK, 0, 0, 0)
            act_split(act, q.next())
            wait_panel(act, q)
            act.copy(gk_low[0:GLA_RANK, :], g_bank[q.par][0:GLA_RANK, :]).then_inc(s["gkl"], 1)
            for h in range(GLA_H):
                act.wait_ge(s["gk_ps"], h + 1)
                if h >= 2:
                    act.wait_ge(s["gd"], h - 1)
                act.activation(gt[:, h % 2], b[h % 2][:], ACT.Abs,
                               bias=gains[:, G_BGK + h:G_BGK + h + 1]).then_inc(s["ga"], 1)
                act.wait_ge(s["ga"], h + 1)
                act.activation(gt[:, h % 2], gt[:, h % 2], ACT.Exp, scale=-1.0).then_inc(s["ge"], 1)
                act.wait_ge(s["ge"], h + 1)
                act.activation(gt[:, h % 2], gt[:, h % 2], ACT.Ln, bias=1.0).then_inc(s["gl"], 1)

        def dve_gates(dve):
            q = Panel(N_GK, 0, 0, 0)
            dve_split(dve, q.next())
            dve.wait_ge(s["gkl"], 1)
            dve.sem_inc(bank_free[q.par], 1)
            dve.wait_ge(s["gk_in"], 32)
            for h in range(GLA_H):
                dve.wait_ge(s["ga"], h + 1)
                dve.tensor_scalar(arg[:, h % 2], b[h % 2][:], gains[:, G_BGK + h:G_BGK + h + 1], 0.0,
                                  ALU.add, ALU.min).then_inc(s["gm"], 1)
                dve.wait_ge(s["gm"], h + 1)
                dve.wait_ge(s["gl"], h + 1)
                dve.tensor_tensor(arg[:, h % 2], arg[:, h % 2], gt[:, h % 2], ALU.subtract).then_inc(s["gd"], 1)
                dve.wait_ge(s["gd"], h + 1)
                dve.tensor_tensor_scan(b_all[:, h], keep, arg[:, h % 2], 0.0, ALU.mult, ALU.add).then_inc(s["gscan"], 1)
                dve.wait_ge(s["gscan"], h + 1)
                dve.tensor_scalar(b_all[:, h], b_all[:, h], 1.0 / GLA_GATE_NORM, None, ALU.mult).then_inc(s["gbs"], 1)
            dve.sem_inc(s["gla_done"], 1)

        def pe_gla(pe):
            with pe.Fori(0, GLA_H) as h:
                for u in range(6):
                    pe_panel(pe, Panel(N_GLA, 6, h, u), h_hi, h_lo)
                pe.wait_ge(s["gla_done"], h + 1)
                for xh in range(2):
                    pe.wait_ge(s["v_in"], 2 * h + xh + 1)
                    for tt in range(TT):
                        last = pe.transpose(b[4 + xh][:, tt * P:(tt + 1) * P], vf[:, xh, tt * P:(tt + 1) * P], ident[:])
                    last.then_inc(s["vt_ps"], 1)
                pe.wait_ge(s["q_in"], h + 1)
                pe.wait_ge(s["k_in"], h + 1)
                for tt in range(TT):
                    c = slice(tt * P, (tt + 1) * P)
                    last = pe.matmul(b[0][:, c], kf[:, c], qf[:, c], start=True, stop=True)
                last.then_inc(s["slev"], 1)
                for lv in range(LEVELS):
                    pe.wait_ge(s["mlev_r"], LEVELS * h + lv + 1)
                    if lv >= 1:
                        pe.wait_ge(s["at_r"] if lv == 1 else s["sm_r"], (LEVELS + 1) * h + 1 if lv == 1 else LEVELS * h + lv - 1)
                    for tt in range(TT):
                        c = slice(tt * P, (tt + 1) * P)
                        last = pe.matmul(b[(lv + 1) % 2][:, c], mlev[:, lv % 2, c], mlev[:, lv % 2, c],
                                         start=True, stop=True)
                    last.then_inc(s["slev"], 1)
                pe.wait_ge(s["kd_r"], h + 1)
                for tt in range(TT):
                    c = slice(tt * P, (tt + 1) * P)
                    last = pe.transpose(b[2][:, c], kd[:, c], ident[:])
                last.then_inc(s["kdt_ps"], 1)
                pe.wait_ge(s["kdt_sb"], h + 1)
                pe.wait_ge(s["vt_sb"], 2 * h + 2)
                for c in range(NCH - 1):
                    r = slice(CHUNK * (c % 2), CHUNK * (c % 2) + CHUNK)
                    o = u_at(c)
                    last = pe.matmul(o, kd_tok[r, c // 2, :], v_tok[r, c // 2, :], start=True, stop=True)
                last.then_inc(s["u_ps"], 1)
                pe.wait_ge(s["at_r"], (LEVELS + 1) * (h + 1))
                pe.wait_ge(s["st_r"], (NCH - 1) * (h + 1))
                pe.wait_ge(s["qe_r"], h + 1)
                for xh in range(2):
                    vc = slice(xh * P, (xh + 1) * P)
                    for tt in range(TT):
                        pe.matmul(b[2 + xh][:, tt * P:(tt + 1) * P], v_tok[:, tt, vc], a_t[:, tt, :],
                                  start=True, stop=False, skip_group_check=True)
                        for c in (2 * tt, 2 * tt + 1):
                            if c:
                                cc = slice(CHUNK * c, CHUNK * (c + 1))
                                last = pe.matmul(b[2 + xh][:, cc], state[:, c, vc], qe[:, cc],
                                                 start=False, stop=True, skip_group_check=True)
                    last.then_inc(s["o_ps"], 1)
                pe.wait_ge(s["osum"], h + 1)
                pe.matmul(b[4][:], ones[:], osq[:, 0], start=True, stop=True).then_inc(s["on_ps"], 1)

        def act_gla(act):
            with act.Fori(0, GLA_H) as h:
                for u in range(6):
                    q = Panel(N_GLA, 6, h, u)
                    act_split(act, q.next())
                    if u == 0:
                        act.wait_ge(s["gla_done"], h + 1)
                        wait_panel(act, q)
                        act.mul(qf, g_bank[q.par][:], GLA_K ** -0.5).then_inc(s["q_in"], 1)
                    if u == 1:
                        wait_panel(act, q)
                        act.copy(kf, g_bank[q.par][:]).then_inc(s["k_in"], 1)
                    if u >= 4:
                        wait_panel(act, q)
                        act.activation(gate[:, u - 4], g_bank[q.par][:], ACT.Tanh, scale=0.5).then_inc(s["tg"], 1)
                for xh in range(2):
                    act.wait_ge(s["vt_ps"], 2 * h + xh + 1)
                    act.copy(v_tok[:, :, xh * P:(xh + 1) * P], tiles(b[4 + xh][:])).then_inc(s["vt_sb"], 1)
                act.activation(eb, b_all[:, bass.ds(h, 1)].rearrange("p a t -> p (a t)"), ACT.Exp).then_inc(s["eb_r"], 1)
                for lv in range(LEVELS + 1):
                    act.wait_ge(s["arg_r"], (LEVELS + 1) * h + lv + 1)
                    if lv == 0:
                        act.activation(arg[:, 0], arg[:, 0], ACT.Abs).then_inc(s["ab_r"], 1)
                    else:
                        act.activation(arg[:, lv % 2], arg[:, lv % 2], ACT.Abs).then_inc(s["ab_r"], 1)
                    act.wait_ge(s["ab_r"], (LEVELS + 1) * h + lv + 1)
                    if lv == 2:
                        act.wait_ge(s["kd_r"], h + 1)
                    if lv >= 3:
                        act.wait_ge(s["mlev_r"], LEVELS * h + lv - 2)
                    act.activation(ex[:, lv % 2], arg[:, lv % 2], ACT.Exp, scale=-1.0).then_inc(s["ex_r"], 1)
                act.wait_ge(s["kdt_ps"], h + 1)
                act.copy(kd_tok, tiles(b[2][:])).then_inc(s["kdt_sb"], 1)
                for xh in range(2):
                    act.wait_ge(s["o_ps"], 2 * h + xh + 1)
                    act.activation(osq[:, xh], b[2 + xh][:], ACT.Square).then_inc(s["osq_r"], 1)
                act.wait_ge(s["on_ps"], h + 1)
                act.activation(rb, b[4][:], ACT.Ln, scale=1.0 / GLA_V, bias=eps[:]).then_inc(s["oln"], 1)
                act.wait_ge(s["oln"], h + 1)
                act.activation(rb, rb, ACT.Exp, scale=-0.5).then_inc(s["or_r"], 1)
                for xh in range(2):
                    act.wait_ge(s["y2"], 2 * h + xh + 1)
                    act.copy(m_hi[:, bass.ds(2 * h + xh, 1)].rearrange("p a t -> p (a t)"), yb[:, xh]).then_inc(s["y_hi"], 1)

        def dve_gla(dve):
            with dve.Fori(0, GLA_H) as h:
                bh = b_all[:, bass.ds(h, 1)].rearrange("p a t -> p (a t)")
                for u in range(6):
                    q = Panel(N_GLA, 6, h, u)
                    dve_split(dve, q.next())
                    if u < 2:
                        dve.wait_ge((s["q_in"], s["k_in"])[u], h + 1)
                        dve.sem_inc(bank_free[q.par], 1)
                    elif u < 4:
                        wait_panel(dve, q)
                        dve.tensor_copy(vf[:, u - 2], g_bank[q.par][:]).then_inc(s["v_in"], 1)
                        dve.wait_ge(s["v_in"], 2 * h + u - 1)
                        dve.sem_inc(bank_free[q.par], 1)
                    else:
                        dve.wait_ge(s["tg"], 2 * h + u - 3)
                        dve.scalar_tensor_tensor(gate[:, u - 4], gate[:, u - 4], 1.0, g_bank[q.par][:],
                                                 ALU.add, ALU.mult).then_inc(bank_free[q.par], 1)
                ends = bh.rearrange("p (c t) -> p c t", t=CHUNK)
                dve.tensor_tensor(arg[:, 0].rearrange("p (c t) -> p c t", t=CHUNK), ends,
                                  ends[:, :, CHUNK - 1:CHUNK].broadcast_to([P, NCH, CHUNK]),
                                  ALU.subtract).then_inc(s["arg_r"], 1)
                for lv in range(LEVELS):
                    w = 2 << lv
                    v = bh.rearrange("p (c t) -> p c t", t=w)
                    if lv >= 1:
                        dve.wait_ge(s["ex_r"], (LEVELS + 1) * h + lv)
                    dve.tensor_tensor(arg[:, (lv + 1) % 2].rearrange("p (c t) -> p c t", t=w), v,
                                      v[:, :, w // 2 - 1:w // 2].broadcast_to([P, SEQ // w, w]),
                                      ALU.subtract).then_inc(s["arg_r"], 1)
                dve.wait_ge(s["slev"], (LEVELS + 1) * h + 1)
                dve.tensor_tensor(a_t, tiles(b[0][:]), mask(0), ALU.mult).then_inc(s["at_r"], 1)
                for lv in range(LEVELS):
                    dve.wait_ge(s["slev"], (LEVELS + 1) * h + lv + 2)
                    if lv >= 2:
                        dve.wait_ge(s["at_r"], (LEVELS + 1) * h + lv)
                    dve.tensor_tensor(tiles(sm[:, lv % 2]), tiles(b[(lv + 1) % 2][:]), mask(lv + 1),
                                      ALU.mult).then_inc(s["sm_r"], 1)
                for c in range(NCH - 1):
                    dve.wait_ge(s["u_ps"], h + 1)
                    u = u_at(c)
                    if c == 0:
                        dve.wait_ge(s["eb_r"], h + 1)
                        dve.tensor_copy(state[:, 1], u).then_inc(s["st_r"], 1)
                    else:
                        dve.wait_ge(s["st_r"], (NCH - 1) * h + c)
                        e = CHUNK * (c + 1) - 1
                        dve.scalar_tensor_tensor(state[:, c + 1], state[:, c], eb[:, e:e + 1], u,
                                                 ALU.mult, ALU.add).then_inc(s["st_r"], 1)
                dve.wait_ge(s["osq_r"], 2 * h + 2)
                dve.tensor_tensor(osq[:, 0], osq[:, 0], osq[:, 1], ALU.add).then_inc(s["osum"], 1)
                for xh in range(2):
                    dve.scalar_tensor_tensor(yb[:, xh], b[2 + xh][:], gains[:, G_ON + xh:G_ON + xh + 1],
                                             gate[:, xh], ALU.mult, ALU.mult).then_inc(s["y1"], 1)
                dve.wait_ge(s["or_r"], h + 1)
                dve.wait_ge(s["y1"], 2 * h + 2)
                for xh in range(2):
                    dve.tensor_tensor(yb[:, xh], yb[:, xh], rb, ALU.mult).then_inc(s["y2"], 1)
                for xh in range(2):
                    dve.wait_ge(s["y_hi"], 2 * h + xh + 1)
                    i = bass.ds(2 * h + xh, 1)
                    last = dve.tensor_tensor(m_lo[:, i].rearrange("p a t -> p (a t)"), yb[:, xh],
                                             m_hi[:, i].rearrange("p a t -> p (a t)").bitcast(F32), ALU.subtract)
                last.then_inc(s["gla_done"], 1)

        def pool_gla(pool):
            with pool.Fori(0, GLA_H) as h:
                pool.wait_ge(s["q_in"], h + 1)
                pool.wait_ge(s["k_in"], h + 1)
                pool.wait_ge(s["ex_r"], (LEVELS + 1) * h + 1)
                pool.tensor_tensor(kd, kf, ex[:, 0], ALU.mult).then_inc(s["kd_r"], 1)
                for lv in range(LEVELS):
                    w = 1 << lv
                    pool.wait_ge(s["ex_r"], (LEVELS + 1) * h + lv + 2)
                    if lv >= 2:
                        pool.wait_ge(s["slev"], (LEVELS + 1) * h + lv)

                    def half(ap, i):
                        return ap.rearrange("p (c i t) -> p c i t", i=2, t=w)[:, :, i, :]

                    e = ex[:, (lv + 1) % 2]
                    pool.tensor_tensor(half(mlev[:, lv % 2], 0), half(kf, 0), half(e, 0), ALU.mult)
                    pool.tensor_tensor(half(mlev[:, lv % 2], 1), half(qf, 1), half(e, 1), ALU.mult).then_inc(s["mlev_r"], 1)
                for lv in range(LEVELS):
                    pool.wait_ge(s["sm_r"], LEVELS * h + lv + 1)
                    pool.wait_ge(s["at_r"], (LEVELS + 1) * h + lv + 1)
                    pool.tensor_tensor(a_t, a_t, tiles(sm[:, lv % 2]), ALU.add).then_inc(s["at_r"], 1)
                pool.wait_ge(s["eb_r"], h + 1)
                pool.tensor_tensor(qe, qf, eb, ALU.mult).then_inc(s["qe_r"], 1)

        sems("x_add")
        adds = [0]

        def sp_panels(sp, base, w):
            with sp.Fori(0, KT // 2) as m:
                for u in range(2):
                    load(sp, Panel(base, 2, m, u), [(w[:, :, bass.ds(2 * P * m + P * u, P)], 0)])

        def pe_wout(pe, base):
            with pe.Fori(0, KT // 2) as m:
                for u in range(2):
                    pe_panel(pe, Panel(base, 2, m, u), m_hi, m_lo)

        def act_wout(act, base):
            with act.Fori(0, KT // 2) as m:
                for u in range(2):
                    act_split(act, Panel(base, 2, m, u).next())

        def dve_wout(dve, base):
            with dve.Fori(0, KT // 2) as m:
                for u in range(2):
                    q = Panel(base, 2, m, u)
                    dve_split(dve, q.next())
                    wait_panel(dve, q)
                    xm = x[:, bass.ds(2 * m + u, 1)].rearrange("p a t -> p (a t)")
                    dve.tensor_tensor(xm, xm, g_bank[q.par][:], ALU.add).then_inc(bank_free[q.par], 1)

        sems("rl sqr hid_hi hid_ready down_done")

        def sp_mlp(sp, base, w1, w2):
            with sp.Fori(0, GROUPS) as g:
                for u in range(8):
                    load(sp, Panel(base, 16, g, u), [(rows(w1)[:, :, bass.ds(D * g + P * u, P)], 0)])
                w2g = w2.rearrange("(g k p) c -> p (g k) c", p=P, k=KT)
                for u in range(8):
                    load(sp, Panel(base, 16, g, 8 + u), [(w2g[:, bass.ds(KT * g, KT), P * u:P * (u + 1)], 0)])

        def pe_mlp(pe, base, i, first):
            with pe.Fori(0, GROUPS) as g:
                for u in range(8):
                    pe_panel(pe, Panel(base, 16, g, u), h_hi, h_lo, s["h_ready"] if u == 0 else None, first)
                for u in range(8):
                    pe_panel(pe, Panel(base, 16, g, 8 + u), m_hi, m_lo, s["hid_ready"] if u == 0 else None,
                             KT * GROUPS * i + KT * g + 2)

        def act_mlp(act, base, i, bufs, ends):
            rl, sq = bufs
            n = KT * GROUPS * i

            def group(g, no_next):
                for u in range(16):
                    q = Panel(base, 16, g, u)
                    if not (no_next and u == 15):
                        act_split(act, q.next())
                    if u < 8:
                        wait_panel(act, q)
                        act.wait_ge(s["hid_ready"], n + KT * g + u + 1)
                        act.activation(rl[:, u % 2], g_bank[q.par][:], ACT.Relu).then_inc(s["rl"], 1)
                        if u == 0:
                            act.wait_ge(s["down_done"], GROUPS * i + g + 1)
                        act.wait_ge(s["sqr"], n + KT * g + u + 1)
                        act.copy(m_hi[:, u], sq[:, u % 2]).then_inc(s["hid_hi"], 1)

            with act.Fori(0, GROUPS - ends) as g:
                group(g, False)
            if ends:
                group(GROUPS - 1, True)

        def dve_mlp(dve, base, i, bufs, ends):
            rl, sq = bufs
            n = KT * GROUPS * i

            def group(g, no_next):
                for u in range(16):
                    q = Panel(base, 16, g, u)
                    if not (no_next and u == 15):
                        dve_split(dve, q.next())
                    if u < 8:
                        dve.wait_ge(s["rl"], n + KT * g + u + 1)
                        dve.tensor_tensor(sq[:, u % 2], rl[:, u % 2], rl[:, u % 2], ALU.mult).then_inc(s["sqr"], 1)
                        dve.sem_inc(bank_free[q.par], 1)
                        dve.wait_ge(s["sqr"], n + KT * g + u + 1)
                        dve.wait_ge(s["hid_hi"], n + KT * g + u + 1)
                        dve.tensor_tensor(m_lo[:, u], sq[:, u % 2], m_hi[:, u].bitcast(F32),
                                          ALU.subtract).then_inc(s["hid_ready"], 1)
                    else:
                        wait_panel(dve, q)
                        dve.tensor_tensor(x[:, u - 8], x[:, u - 8], g_bank[q.par][:], ALU.add).then_inc(bank_free[q.par], 1)
                dve.sem_inc(s["down_done"], 1)

            with dve.Fori(0, GROUPS - ends) as g:
                group(g, False)
            if ends:
                group(GROUPS - 1, True)

        sems("y_ps y_sb")
        at_out = [0]

        def pe_out(pe, y_tok):
            for tt in range(TT):
                for hf in range(2):
                    i = 2 * tt + hf
                    if i >= 2:
                        pe.wait_ge(s["y_sb"], i - 1)
                    for k in range(4):
                        last = pe.transpose(b[i % 2][:, k * P:(k + 1) * P], x[:, 4 * hf + k, tt * P:(tt + 1) * P], ident[:])
                    last.then_inc(s["y_ps"], 1)

        def act_out(act, y_tok):
            for i in range(2 * TT):
                act.wait_ge(s["y_ps"], i + 1)
                act.copy(y_tok[:, i // 2, (i % 2) * 512:(i % 2 + 1) * 512], b[i % 2][:]).then_inc(s["y_sb"], 1)

        def sp_out(sp, y_tok):
            ov = out.rearrange("b (t p) d -> p (b t) d", p=P)
            for tt in range(TT):
                sp.wait_ge(s["y_sb"], 2 * tt + 2)
                sp.dma_start(ov[:, tt], y_tok[:, tt]).then_inc(s["out_done"], 16)
            sp.wait_ge(s["out_done"], 16 * TT)

        at[0] = 22400 - (SEQ + TT * 40 + ATT_H * SEQ)
        kept0 = at[0]
        gb = take(SEQ)
        gb_tok = take(TT, 40)
        o_att = take(ATT_H, SEQ)

        at[0] = 0
        ca, sa, ci, si = take(SEQ), take(SEQ), take(SEQ), take(SEQ)
        keep2 = take(SEQ)
        ak = take(2, SEQ)
        v_key = [take(TT, P) for _ in range(ATT_KV)]
        sel = take(1280)
        r0 = at[0]
        ms = take(1280)
        p_t = take(1280)
        aq = take(SEQ)
        r1, at[0] = at[0], r0
        iqs = take(4, SEQ)
        at[0] = r0
        nb2 = norm_bufs()
        assert at[0] <= r1
        at[0] = r1
        gtb = take(SEQ)
        rp_c, rp_s = take(SEQ), take(SEQ)
        r128, sq128 = take(SEQ), take(SEQ)
        w_tok = take(TT, IDX_H)
        n_max, r_sum = take(TT), take(TT)
        hp = take(4)
        small = take(SEQ)
        ik = take(SEQ)
        sc = take(1152)
        av = take(2, SEQ)
        gtmp = take(3, SEQ)
        lg = gtmp[:, 0:2]
        top8 = take(3, 8)
        assert at[0] <= kept0, (at[0], kept0)
        off = [0, 128, 384, 768]
        koff = [0, 512, 896, 1152]

        sems("t_in in1 z_ga z_ge z_gl z_gt z_mx z_sp z_g z_gb z_ea z_b wt_ps wt_sb gbt_ps gbt_sb "
             "r_sq r_ss r_ln r_r r_y rp_ps rp_cc rp_ss rp_out av_ps av_sb lg_ps lg_r lg_a sc_m mx8 rp8 sel_r zsel "
             "aq_in gtb_in s_ps ms_r nm_r nms ex_a rs_r pn_r pt_ps pt_sb pv_ps att_done")

        def sp_in1(sp):
            w = rows(t["w_in_2"][0])
            first = Panel(N_IN1, 0, 0, 0)
            load(sp, first, [(w[:, :, c:c + 32], d) for c, d in ((GA0, 0), (GB0, 32), (IW0, 64), (GTA0, 96))])
            load(sp, Panel(N_IN1, 0, 0, 1), [(w[:, :, IK0:IK0 + IDX_D], 0), (w[:, :, IK0:IK0 + IDX_D], IDX_D)])
            cols = [IQ0 + P * i for i in range(4)] + [AK0, AK0 + P, AV0, AV0 + P]
            for i, c in enumerate(cols):
                load(sp, Panel(N_IN1, 0, 0, 2 + i), [(w[:, :, c:c + P], 0)])
                if i == 0:
                    sp.wait_ge(s["phase_done"], 16)
                    for j, dst in enumerate((ca, sa, ci, si, keep2)):
                        sp.dma_start(dst, const_wide[j]).then_inc(s["t_in"], 16)
                    for j, n in enumerate(("dt_bias_2", "a_log_2")):
                        sp.dma_start(hp[0:GDN_H, j:j + 1], t[n].rearrange("a d -> d a")).then_inc(s["t_in"], 16)

        def pe_rms(pe, c, bk):
            pe.wait_ge(s["r_sq"], c + 1)
            pe.matmul(bk[:], ones[:], sq128, start=True, stop=True).then_inc(s["r_ss"], 1)

        def act_rms(act, c, src, bk):
            if isinstance(c, int) and c == 0:
                pass
            else:
                act.wait_ge(s["r_ss"], c)
                act.wait_ge(s["r_y"], c)
            act.activation(sq128, src, ACT.Square).then_inc(s["r_sq"], 1)
            act.wait_ge(s["r_ss"], c + 1)
            act.activation(r128, bk[:], ACT.Ln, scale=1.0 / P, bias=eps[:]).then_inc(s["r_ln"], 1)
            act.wait_ge(s["r_ln"], c + 1)
            act.activation(r128, r128, ACT.Exp, scale=-0.5).then_inc(s["r_r"], 1)

        def dve_rms(dve, c, src, gain):
            dve.wait_ge(s["r_r"], c + 1)
            dve.scalar_tensor_tensor(src, src, gains[:, gain:gain + 1], r128, ALU.mult, ALU.mult).then_inc(s["r_y"], 1)

        def pe_rope(pe, c, src, swap):
            if not (isinstance(c, int) and c == 0):
                pe.wait_ge(s["rp_ss"], c)
            pe.matmul(b[5][:], swap[:], src, start=True, stop=True).then_inc(s["rp_ps"], 1)

        def pool_rope(pool, c, src, cos):
            if not (isinstance(c, int) and c == 0):
                pool.wait_ge(s["rp_out"], c)
            pool.tensor_tensor(rp_c, src, cos, ALU.mult).then_inc(s["rp_cc"], 1)

        def dve_rope(dve, c, src, sin):
            if not (isinstance(c, int) and c == 0):
                dve.wait_ge(s["rp_out"], c)
            dve.wait_ge(s["rp_ps"], c + 1)
            dve.tensor_tensor(rp_s, b[5][:], sin, ALU.mult).then_inc(s["rp_ss"], 1)
            dve.wait_ge(s["rp_cc"], c + 1)
            dve.wait_ge(s["rp_ss"], c + 1)
            dve.tensor_tensor(src, rp_c, rp_s, ALU.add).then_inc(s["rp_out"], 1)

        idx_ropes = [(0, ik)] + [(1 + j, iqs[:, j]) for j in range(4)]

        def pe_in1(pe):
            for u in range(10):
                pe_panel(pe, Panel(N_IN1, 0, 0, u), h_hi, h_lo, s["h_ready"] if u == 0 else None, 2 * KT)
                if u == 1:
                    pe.wait_ge(s["in1"], 1)
                    for tt in range(TT):
                        last = pe.transpose(b[0][:, tt * P:(tt + 1) * P], small[:, tt * P:(tt + 1) * P], ident[:])
                    last.then_inc(s["wt_ps"], 1)
            pe.wait_ge(s["z_gb"], 2)
            pe.wait_ge(s["z_b"], 2)
            for tt in range(TT):
                last = pe.transpose(b[1][:, tt * 40:(tt + 1) * 40], gb[0:40, tt * P:(tt + 1) * P], ident[0:40, 0:40])
            last.then_inc(s["gbt_ps"], 1)
            pe.wait_ge(s["t_in"], 16 * 7)
            pe.wait_ge(s["consts_in"], 48)
            pe.wait_ge(s["in1"], 6)
            for c, src in idx_ropes:
                pe_rope(pe, c, src, swap_i)
            for i in range(2):
                pe_rms(pe, i, b[4])
            for i in range(2):
                pe.wait_ge(s["r_y"], i + 1)
                pe_rope(pe, 5 + i, ak[:, i], swap_a)
            for i in range(2):
                pe.wait_ge(s["in1"], 9 + i)
                for tt in range(TT):
                    last = pe.transpose(b[2 + i][:, tt * P:(tt + 1) * P], av[:, i, tt * P:(tt + 1) * P], ident[:])
                last.then_inc(s["av_ps"], 1)
            pe.wait_ge(s["wt_sb"], 1)
            pe.wait_ge(s["rp_out"], 5)
            i = 0
            for q in range(1, TT):
                for hh in range(IDX_H):
                    if i >= 2:
                        pe.wait_ge(s["lg_r"], i - 1)
                    else:
                        pe.wait_ge(s["gbt_sb"], 1)
                    r = slice(IDX_D * (hh % 2), IDX_D * (hh % 2) + IDX_D)
                    pe.matmul(b[i % 2][:, 0:P * (q + 1)], iqs[r, hh // 2, q * P:(q + 1) * P], ik[r, 0:P * (q + 1)],
                              start=True, stop=True).then_inc(s["lg_ps"], 1)
                    i += 1

        def act_in1(act):
            dst = [small, ik] + [iqs[:, j] for j in range(4)] + [ak[:, 0], ak[:, 1], av[:, 0], av[:, 1]]
            for u in range(10):
                q = Panel(N_IN1, 0, 0, u)
                act_split(act, q.next())
                wait_panel(act, q)
                act.copy(dst[u], g_bank[q.par][:]).then_inc(s["in1"], 1)
                act.wait_ge(s["in1"], u + 1)
                act.sem_inc(bank_free[q.par], 1)
                if u == 1:
                    act.wait_ge(s["wt_ps"], 1)
                    act.mul(w_tok, tiles(b[0][:])[:, :, 64:64 + IDX_H], (IDX_H * IDX_D) ** -0.5).then_inc(s["wt_sb"], 1)
                    act.wait_ge(s["t_in"], 16 * 7)
                    g = gtmp[0:GDN_H, 0]
                    act.activation(g, small[0:GDN_H, :], ACT.Abs, bias=hp[0:GDN_H, 0:1]).then_inc(s["z_ga"], 1)
                    act.activation(hp[0:GDN_H, 2:3], hp[0:GDN_H, 1:2], ACT.Exp).then_inc(s["z_ea"], 1)
                    act.wait_ge(s["z_ga"], 1)
                    act.activation(g, g, ACT.Exp, scale=-1.0).then_inc(s["z_ge"], 1)
                    act.wait_ge(s["z_ge"], 1)
                    act.activation(g, g, ACT.Ln, bias=1.0).then_inc(s["z_gl"], 1)
                    act.wait_ge(s["z_b"], 1)
                    act.activation(gb[32:32 + GDN_H, :], small[32:32 + GDN_H, :], ACT.Tanh, scale=0.5).then_inc(s["z_gt"], 1)
            act.wait_ge(s["gbt_ps"], 1)
            act.copy(gb_tok, b[1][:, 0:TT * 40].rearrange("p (t c) -> p t c", t=TT)).then_inc(s["gbt_sb"], 1)
            for i in range(2):
                act_rms(act, i, ak[:, i], b[4])
            for i in range(2):
                act.wait_ge(s["av_ps"], i + 1)
                act.copy(v_key[i], tiles(b[2 + i][:])).then_inc(s["av_sb"], 1)

        def dve_in1(dve):
            dve.memset(gb[0:64, :], 0.0).then_inc(s["z_b"], 1)
            for u in range(10):
                dve_split(dve, Panel(N_IN1, 0, 0, u).next())
                if u == 1:
                    g, m = gtmp[0:GDN_H, 0], gtmp[0:GDN_H, 1]
                    dve.wait_ge(s["in1"], 1)
                    dve.wait_ge(s["t_in"], 16 * 7)
                    dve.tensor_scalar(m, small[0:GDN_H, :], hp[0:GDN_H, 0:1], 0.0, ALU.add, ALU.max).then_inc(s["z_mx"], 1)
                    dve.wait_ge(s["z_mx"], 1)
                    dve.wait_ge(s["z_gl"], 1)
                    dve.tensor_tensor(m, m, g, ALU.add).then_inc(s["z_sp"], 1)
                    dve.wait_ge(s["z_sp"], 1)
                    dve.wait_ge(s["z_ea"], 1)
                    dve.tensor_scalar(m, m, hp[0:GDN_H, 2:3], -1.0, ALU.mult, ALU.mult).then_inc(s["z_g"], 1)
                    dve.wait_ge(s["z_g"], 1)
                    dve.wait_ge(s["z_b"], 1)
                    dve.tensor_tensor_scan(gb[0:GDN_H, :], keep2[0:GDN_H, :], m, 0.0, ALU.mult, ALU.add).then_inc(s["z_gb"], 1)
                    dve.wait_ge(s["z_gt"], 1)
                    bt = gb[32:32 + GDN_H, :]
                    dve.tensor_scalar(bt, bt, 1.0, 0.5, ALU.add, ALU.mult).then_inc(s["z_gb"], 1)
                    dve.sem_inc(s["z_b"], 1)
            for c, src in idx_ropes:
                dve_rope(dve, c, src, si)
            for i in range(2):
                dve_rms(dve, i, ak[:, i], G_KN)
            for i in range(2):
                dve_rope(dve, 5 + i, ak[:, i], sa)
            sco = [None, 0, 256, 640]
            dve.wait_ge(s["wt_sb"], 1)
            i = 0
            for q in range(1, TT):
                n = P * (q + 1)
                acc = sc[:, sco[q]:sco[q] + n]
                for hh in range(IDX_H):
                    dve.wait_ge(s["lg_ps"], i + 1)
                    w = w_tok[:, q, hh:hh + 1]
                    if hh == 0:
                        dve.tensor_scalar(acc, b[i % 2][:, 0:n], 0.0, w, ALU.max, ALU.mult).then_inc(s["lg_r"], 1)
                        dve.wait_ge(s["lg_r"], i + 1)
                        if i:
                            dve.wait_ge(s["lg_a"], i)
                        dve.sem_inc(s["lg_a"], 1)
                    else:
                        lgt = lg[:, i % 2, 0:n]
                        dve.tensor_scalar(lgt, b[i % 2][:, 0:n], 0.0, w, ALU.max, ALU.mult).then_inc(s["lg_r"], 1)
                        dve.wait_ge(s["lg_r"], i + 1)
                        dve.wait_ge(s["lg_a"], i)
                        dve.tensor_tensor(acc, acc, lgt, ALU.add).then_inc(s["lg_a"], 1)
                    i += 1
            dve.wait_ge(s["sc_m"], 3)
            with dve.Fori(0, TOPK // 8):
                for q in range(1, TT):
                    dve.max(out=top8[:, q - 1], in_=sc[:, sco[q]:sco[q] + P * (q + 1)])
                dve.drain()
                for q in range(1, TT):
                    acc = sc[:, sco[q]:sco[q] + P * (q + 1)]
                    dve.match_replace(out=acc, in_to_replace=top8[:, q - 1], in_values=acc, imm_value=TAKEN)
                dve.drain()
            for q in range(1, TT):
                n = P * (q + 1)
                dve.tensor_scalar(sel[:, off[q]:off[q] + n], sc[:, sco[q]:sco[q] + n], TAKEN, 1.0,
                                  ALU.is_equal, ALU.subtract).then_inc(s["sel_r"], 1)
            dve.wait_ge(s["sel_r"], 3)
            dve.wait_ge(s["zsel"], 2)

        def pool_in1(pool):
            pool.wait_ge(s["t_in"], 16 * 7)
            pool.wait_ge(s["in1"], 6)
            for c, src in idx_ropes:
                pool_rope(pool, c, src, ci)
            for i in range(2):
                pool.wait_ge(s["r_y"], i + 1)
                pool_rope(pool, 5 + i, ak[:, i], ca)
            pool.memset(sel[:, 0:P], 0.0).then_inc(s["zsel"], 1)
            pool.wait_ge(s["zsel"], 1)
            pool.affine_select(out=sel[:, 0:P], in_=sel[:, 0:P], compare_op=ALU.is_ge, fill=-1.0, base=0,
                               pattern=[[-1, P]], channel_multiplier=1).then_inc(s["zsel"], 1)
            sco = [None, 0, 256, 640]
            for q in range(1, TT):
                pool.wait_ge(s["lg_a"], IDX_H * q)
                d = sc[:, sco[q] + P * q:sco[q] + P * (q + 1)]
                pool.affine_select(out=d, in_=d, compare_op=ALU.is_ge, fill=NOT_CAUSAL, base=0,
                                   pattern=[[-1, P]], channel_multiplier=1).then_inc(s["sc_m"], 1)

        HPK = ATT_H // ATT_KV

        def sp_att(sp):
            w = rows(t["w_in_2"][0])
            for kv in range(ATT_KV):
                with sp.Fori(0, HPK) as j:
                    for u, c in enumerate((AQ0, GTB0)):
                        load(sp, Panel(N_ATT + 2 * HPK * kv, 2, j, u), [(w[:, :, bass.ds(c + HPK * kv * P + P * j, P)], 0)])

        def pe_att(pe):
            for kv in range(ATT_KV):
                with pe.Fori(0, HPK) as j:
                    h = j + HPK * kv
                    for u in range(2):
                        pe_panel(pe, Panel(N_ATT + 2 * HPK * kv, 2, j, u), h_hi, h_lo)
                    pe.wait_ge(s["att_done"], h + 1)
                    pe_rms(pe, h + 2, b[4])
                    pe.wait_ge(s["r_y"], h + 3)
                    pe_rope(pe, h + 7, aq, swap_a)
                    pe.wait_ge(s["rp_out"], h + 8)
                    for q in range(TT):
                        pe.matmul(b[q][:, 0:P * (q + 1)], aq[:, q * P:(q + 1) * P], ak[:, kv, 0:P * (q + 1)],
                                  start=True, stop=True).then_inc(s["s_ps"], 1)
                    pe.wait_ge(s["pn_r"], TT * h + TT)
                    for k in range(TT):
                        for q in range(k, TT):
                            last = pe.transpose(b[k][:, (q - k) * P:(q - k + 1) * P],
                                                ms[:, off[q] + k * P:off[q] + (k + 1) * P], ident[:])
                        last.then_inc(s["pt_ps"], 1)
                    for k in range(TT):
                        pe.wait_ge(s["pt_sb"], TT * h + k + 1)
                        last = pe.matmul(b[4][:, k * P:SEQ], v_key[kv][:, k, :], p_t[:, koff[k]:koff[k] + SEQ - k * P],
                                         start=(k == 0), stop=(k == TT - 1), skip_group_check=True)
                    last.then_inc(s["pv_ps"], 1)

        def act_att(act):
            for kv in range(ATT_KV):
                with act.Fori(0, HPK) as j:
                    h = j + HPK * kv
                    for u in range(2):
                        q = Panel(N_ATT + 2 * HPK * kv, 2, j, u)
                        act_split(act, q.next())
                        wait_panel(act, q)
                        if u == 0:
                            act.wait_ge(s["att_done"], h + 1)
                            act.copy(aq, g_bank[q.par][:]).then_inc(s["aq_in"], 1)
                            act.wait_ge(s["aq_in"], h + 1)
                        else:
                            act.activation(gtb, g_bank[q.par][:], ACT.Tanh, scale=0.5).then_inc(s["gtb_in"], 1)
                            act.wait_ge(s["gtb_in"], h + 1)
                        act.sem_inc(bank_free[q.par], 1)
                    act_rms(act, h + 2, aq, b[4])
                    for q in range(TT):
                        act.wait_ge(s["nms"], h + 1)
                        m = ms[:, off[q]:off[q] + P * (q + 1)]
                        act.activation(m, m, ACT.Exp, scale=P ** -0.5, bias=n_max[:, q:q + 1],
                                       accum_out=r_sum[:, q:q + 1]).then_inc(s["ex_a"], 1)
                    for k in range(TT):
                        act.wait_ge(s["pt_ps"], TT * h + k + 1)
                        act.copy(p_t[:, koff[k]:koff[k] + SEQ - k * P], b[k][:, 0:SEQ - k * P]).then_inc(s["pt_sb"], 1)

        def dve_att(dve):
            for kv in range(ATT_KV):
                with dve.Fori(0, HPK) as j:
                    h = j + HPK * kv
                    for u in range(2):
                        dve_split(dve, Panel(N_ATT + 2 * HPK * kv, 2, j, u).next())
                    dve_rms(dve, h + 2, aq, G_QN)
                    dve_rope(dve, h + 7, aq, sa)
                    for q in range(TT):
                        dve.wait_ge(s["s_ps"], TT * h + q + 1)
                        n = P * (q + 1)
                        m = ms[:, off[q]:off[q] + n]
                        dve.scalar_tensor_tensor(m, sel[:, off[q]:off[q] + n], BIG, b[q][:, 0:n],
                                                 ALU.mult, ALU.add).then_inc(s["ms_r"], 1)
                    for q in range(TT):
                        dve.wait_ge(s["ms_r"], TT * h + q + 1)
                        dve.tensor_reduce(n_max[:, q:q + 1], ms[:, off[q]:off[q] + P * (q + 1)], AX.X, ALU.max,
                                          negate=True).then_inc(s["nm_r"], 1)
                    dve.wait_ge(s["nm_r"], TT * h + TT)
                    dve.tensor_scalar(n_max, n_max, P ** -0.5, None, ALU.mult).then_inc(s["nms"], 1)
                    dve.wait_ge(s["ex_a"], TT * h + TT)
                    dve.reciprocal(r_sum, r_sum).then_inc(s["rs_r"], 1)
                    dve.wait_ge(s["rs_r"], h + 1)
                    for q in range(TT):
                        m = ms[:, off[q]:off[q] + P * (q + 1)]
                        dve.tensor_scalar(m, m, r_sum[:, q:q + 1], None, ALU.mult).then_inc(s["pn_r"], 1)
                    dve.wait_ge(s["pv_ps"], h + 1)
                    dve.wait_ge(s["gtb_in"], h + 1)
                    dve.scalar_tensor_tensor(o_att[:, bass.ds(h, 1)].rearrange("p a t -> p (a t)"), gtb, 1.0, b[4][:],
                                             ALU.add, ALU.mult).then_inc(s["att_done"], 1)

        def pool_att(pool):
            with pool.Fori(0, ATT_H) as h:
                pool.wait_ge(s["r_y"], h + 3)
                pool_rope(pool, h + 7, aq, ca)

        at[0] = 0
        ub = take(SEQ + CONV)
        qkv = take(3, SEQ)
        tz = take(2, SEQ)
        zs, ga = take(SEQ), take(SEQ)
        pick = take(2, P)
        gc_b, be_b, eg_b = take(SEQ), take(SEQ), take(SEQ)
        sq2, rr = take(2, SEQ), take(2, SEQ)
        kb = take(SEQ)
        dec = take(TT, P)
        ek = take(SEQ)
        a_tr = take(TT, P)
        a_lv = take(2, SEQ)
        t_m, t_t = take(TT, P), take(TT, P)
        y_m = take(TT, P)
        vb_tok, kbe_tok, kdec_tok = take(TT, P), take(TT, P), take(TT, P)
        u_m, w_t, v_new = take(TT, P), take(SEQ), take(TT, P)
        st = take(2, P)
        assert at[0] <= kept0, (at[0], kept0)
        qn, kn, vn = qkv[:, 0], qkv[:, 1], qkv[:, 2]
        kbe, q_dec = tz[:, 0], tz[:, 1]
        o_sq, r_o, y_o = sq2[:, 0], rr[:, 0], sq2[:, 1]

        cleared += gla_sems + gate_sems
        sems("c_chain oo_c ub0 c_in c_y c_t c_s z_in z_s ga_in pick_r bc_ps bc_sb eg_r l_sq l_ss l_ln l_r l_y kb_r vb_r "
             "dm_a dm_b dm_c dec_r ek_a ek_b ek_c kk_ps kk_r qk_ps qk_r kbe_r qd_r tok_ps tok_sb al_r yy_ps y_sb2 "
             "z_ps t_r u_ps2 u_sb ws_ps vn_r kv_ps st2 oo_ps oo_sq oo_ss oo_ln oo_r oo_y1 oo_y2 oo_y3 oo_y4 oo_hi gdn_done", reuse=True)

        def sp_gdn(sp):
            w = rows(t["w_in_2"][0])
            with sp.Fori(0, GDN_H // 2) as hp2:
                for e in range(2):
                    for u, c in enumerate((QKV0, QKV0 + 1024, QKV0 + 2048, Z0, GTA0)):
                        load(sp, Panel(N_GDN, 10, hp2, 5 * e + u), [(w[:, :, bass.ds(c + P * e + 2 * P * hp2, P)], 0)])

        def pe_gdn(pe):
            with pe.Fori(0, GDN_H // 2) as hp2:
                for e in range(2):
                    h = 2 * hp2 + e
                    for u in range(5):
                        pe_panel(pe, Panel(N_GDN, 10, hp2, 5 * e + u), h_hi, h_lo)
                    pe.wait_ge(s["gdn_done"], h + 1)
                    pe.wait_ge(s["pick_r"], 2 * h + 2)
                    pe.matmul(b[0][:], pick[0:40, 0], gb[0:40, :], start=True, stop=True).then_inc(s["bc_ps"], 1)
                    pe.matmul(b[1][:], pick[0:40, 1], gb[0:40, :], start=True, stop=True).then_inc(s["bc_ps"], 1)
                    for i in range(2):
                        pe.wait_ge(s["l_sq"], 2 * h + i + 1)
                        pe.matmul(b[2 + i][:], ones[:], sq2[:, i], start=True, stop=True).then_inc(s["l_ss"], 1)
                    pe.wait_ge(s["l_y"], 2 * h + 2)
                    pe.wait_ge(s["kb_r"], h + 1)
                    for bk, rhs, done in ((b[4], kb, s["kk_ps"]), (b[5], qn, s["qk_ps"])):
                        for tt in range(TT):
                            c = slice(tt * P, (tt + 1) * P)
                            last = pe.matmul(bk[:, c], kn[:, c], rhs[:, c], start=True, stop=True)
                        last.then_inc(done, 1)
                    pe.wait_ge(s["bc_sb"], 2 * h + 2)
                    pe.wait_ge(s["eg_r"], h + 1)
                    for i, (src, ready) in enumerate(((vn, s["vb_r"]), (kbe, s["kbe_r"]), (ek, s["ek_c"]))):
                        pe.wait_ge(ready, h + 1)
                        bk = b[(2, 3, 0)[i]]
                        for tt in range(TT):
                            c = slice(tt * P, (tt + 1) * P)
                            last = pe.transpose(bk[:, c], src[:, c], ident[:])
                        last.then_inc(s["tok_ps"], 1)
                    for lv in range(LEVELS):
                        pe.wait_ge(s["al_r"], LEVELS * h + lv + 1)
                        al = a_lv[:, lv % 2]
                        pe.wait_ge(s["tok_sb"], 3 * h + 3)
                        if lv:
                            pe.wait_ge(s["t_r"], (2 * LEVELS - 1) * h + 2 * lv)
                        for tt in range(TT):
                            c = slice(tt * P, (tt + 1) * P)
                            rhs = t_m[:, tt, :] if lv else ident[:]
                            last = pe.matmul(b[0][:, c], al[:, c], rhs, start=True, stop=True)
                        last.then_inc(s["yy_ps"], 1)
                        if lv == 0:
                            continue
                        pe.wait_ge(s["y_sb2"], (LEVELS - 1) * h + lv)
                        for side in ((0, 1) if lv < LEVELS - 1 else (1,)):
                            for tt in range(TT):
                                c = slice(tt * P, (tt + 1) * P)
                                if side == 0:
                                    last = pe.matmul(b[1][:, c], t_t[:, tt, :], y_m[:, tt, :], start=True, stop=True)
                                else:
                                    last = pe.matmul(b[2][:, c], y_m[:, tt, :], t_t[:, tt, :], start=True, stop=True)
                            last.then_inc(s["z_ps"], 1)
                    pe.wait_ge(s["t_r"], (2 * LEVELS - 1) * (h + 1))
                    for tt in range(TT):
                        c = slice(tt * P, (tt + 1) * P)
                        pe.matmul(b[3][:, c], t_t[:, tt, :], vb_tok[:, tt, :], start=True, stop=True)
                        last = pe.matmul(b[4][:, c], kbe_tok[:, tt, :], t_t[:, tt, :], start=True, stop=True)
                    last.then_inc(s["u_ps2"], 1)
                    pe.wait_ge(s["u_sb"], 2 * h + 2)
                    pe.wait_ge(s["qd_r"], h + 1)
                    for c in range(NCH):
                        r = slice(CHUNK * (c % 2), CHUNK * (c % 2) + CHUNK)
                        cc = slice(CHUNK * c, CHUNK * (c + 1))
                        if c:
                            pe.wait_ge(s["st2"], (NCH - 1) * h + c)
                            pe.matmul(b[5][r, 0:P], w_t[:, cc], st[:, c % 2], start=True, stop=True).then_inc(s["ws_ps"], 1)
                            pe.matmul(b[1 + c % 2][:, (c // 2) * P:(c // 2) * P + CHUNK], st[:, c % 2], q_dec[:, cc],
                                      start=True, stop=True, skip_group_check=True)
                        if c < NCH - 1:
                            pe.wait_ge(s["vn_r"], NCH * h + c + 1)
                            pe.matmul(b[0][:, 0:P], kdec_tok[r, c // 2, :], v_new[r, c // 2, :],
                                      start=True, stop=True).then_inc(s["kv_ps"], 1)
                    pe.wait_ge(s["vn_r"], NCH * (h + 1))
                    pe.wait_ge(s["qk_r"], h + 1)
                    for tt in range(TT):
                        last = pe.matmul(b[3][:, tt * P:(tt + 1) * P], v_new[:, tt, :], dec[:, tt, :],
                                         start=True, stop=True)
                    last.then_inc(s["oo_ps"], 1)
                    pe.wait_ge(s["oo_sq"], h + 1)
                    pe.matmul(b[4][:], ones[:], o_sq, start=True, stop=True).then_inc(s["oo_ss"], 1)

        def act_gdn(act):
            with act.Fori(0, GDN_H // 2) as hp2:
                for e in range(2):
                    h = 2 * hp2 + e
                    for u in range(5):
                        q = Panel(N_GDN, 10, hp2, 5 * e + u)
                        act_split(act, q.next())
                        wait_panel(act, q)
                        if u == 0:
                            act.wait_ge(s["gdn_done"], h + 1)
                        if u < 3:
                            act.wait_ge(s["ub0"], 3 * h + u + 1)
                            act.copy(ub[:, CONV - 1:CONV - 1 + SEQ], g_bank[q.par][:]).then_inc(s["c_in"], 1)
                            act.wait_ge(s["c_in"], 3 * h + u + 1)
                            act.sem_inc(bank_free[q.par], 1)
                            act.wait_ge(s["c_y"], 3 * h + u + 1)
                            if u == 2:
                                act.wait_ge(s["c_s"], 3 * h + 1)
                            act.activation(tz[:, u % 2], qkv[:, u], ACT.Tanh, scale=0.5).then_inc(s["c_t"], 1)
                        elif u == 3:
                            act.activation(zs, g_bank[q.par][:], ACT.Tanh, scale=0.5).then_inc(s["z_in"], 1)
                        else:
                            act.activation(ga, g_bank[q.par][:], ACT.Tanh, scale=0.5).then_inc(s["ga_in"], 1)
                            act.wait_ge(s["ga_in"], h + 1)
                            act.sem_inc(bank_free[q.par], 1)
                    act.wait_ge(s["bc_ps"], 2 * h + 2)
                    act.copy(gc_b, b[0][:]).then_inc(s["bc_sb"], 1)
                    act.copy(be_b, b[1][:]).then_inc(s["bc_sb"], 1)
                    act.activation(eg_b, b[0][:], ACT.Exp).then_inc(s["eg_r"], 1)
                    for i in range(2):
                        act.wait_ge(s["c_s"], 3 * h + i + 1)
                        act.activation(sq2[:, i], qkv[:, i], ACT.Square).then_inc(s["l_sq"], 1)
                    for i in range(2):
                        act.wait_ge(s["l_ss"], 2 * h + i + 1)
                        act.activation(rr[:, i], b[2 + i][:], ACT.Ln, scale=0.25, bias=eps[:]).then_inc(s["l_ln"], 1)
                    for i in range(2):
                        act.wait_ge(s["l_ln"], 2 * h + i + 1)
                        act.activation(rr[:, i], rr[:, i], ACT.Exp, scale=-0.5).then_inc(s["l_r"], 1)
                    act.wait_ge(s["dm_b"], h + 1)
                    act.activation(dec, dec, ACT.Exp).then_inc(s["dm_c"], 1)
                    act.wait_ge(s["ek_a"], h + 1)
                    act.activation(ek, ek, ACT.Exp, scale=-1.0).then_inc(s["ek_b"], 1)
                    for i, dst in enumerate((vb_tok, kbe_tok, kdec_tok)):
                        act.wait_ge(s["tok_ps"], 3 * h + i + 1)
                        act.copy(dst, tiles(b[(2, 3, 0)[i]][:])).then_inc(s["tok_sb"], 1)
                    for lv in range(1, LEVELS):
                        act.wait_ge(s["yy_ps"], LEVELS * h + lv + 1)
                        act.copy(y_m, tiles(b[0][:])).then_inc(s["y_sb2"], 1)
                    act.wait_ge(s["u_ps2"], h + 1)
                    act.copy(u_m, tiles(b[3][:])).then_inc(s["u_sb"], 1)
                    act.copy(w_t, b[4][:]).then_inc(s["u_sb"], 1)
                    act.wait_ge(s["oo_y1"], h + 1)
                    act.activation(o_sq, y_m.rearrange("p t c -> p (t c)"), ACT.Square).then_inc(s["oo_sq"], 1)
                    act.wait_ge(s["oo_ss"], h + 1)
                    act.activation(r_o, b[4][:], ACT.Ln, scale=1.0 / P, bias=eps[:]).then_inc(s["oo_ln"], 1)
                    act.wait_ge(s["oo_ln"], h + 1)
                    act.activation(r_o, r_o, ACT.Exp, scale=-0.5).then_inc(s["oo_r"], 1)
                    act.wait_ge(s["oo_y4"], h + 1)
                    act.mul(m_hi[:, bass.ds(h, 1)].rearrange("p a t -> p (a t)"), y_o, 0.5).then_inc(s["oo_hi"], 1)

        def dve_gdn(dve):
            dve.memset(ub[:, 0:CONV - 1], 0.0).then_inc(s["memsets"], 1)
            dve.sem_inc(s["ub0"], 1)
            dve.sem_inc(s["gdn_done"], 1)
            dve.wait_ge(s["memsets"], 4)
            with dve.Fori(0, GDN_H // 2) as hp2:
                for e in range(2):
                    h = 2 * hp2 + e

                    def col(ap, c):
                        return ap[:, bass.ds(c, 1)]

                    for u in range(5):
                        q = Panel(N_GDN, 10, hp2, 5 * e + u)
                        dve_split(dve, q.next())
                        if u == 0:
                            for i in range(2):
                                dve.tensor_copy(pick[0:40, i], ident[0:40, bass.ds(32 * i + h, 1)].broadcast_to([40, P])
                                                ).then_inc(s["pick_r"], 1)
                        if u < 3:
                            dve.wait_ge(s["c_in"], 3 * h + u + 1)
                            y = qkv[:, u]
                            dve.tensor_scalar(y, ub[:, 0:SEQ], col(conv_w, u * 8 + h), None, ALU.mult).then_inc(s["c_chain"], 1)
                            for jj in range(1, CONV):
                                dve.wait_ge(s["c_chain"], 9 * h + 3 * u + jj)
                                ins = dve.scalar_tensor_tensor(y, ub[:, jj:jj + SEQ], col(conv_w, jj * 24 + u * 8 + h), y,
                                                               ALU.mult, ALU.add)
                                ins.then_inc(s["c_chain"] if jj < CONV - 1 else s["c_y"], 1)
                            dve.wait_ge(s["c_y"], 3 * h + u + 1)
                            dve.sem_inc(s["ub0"], 1)
                            dve.wait_ge(s["c_t"], 3 * h + u + 1)
                            dve.scalar_tensor_tensor(y, tz[:, u % 2], 1.0, y, ALU.add, ALU.mult).then_inc(s["c_s"], 1)
                        elif u == 3:
                            dve.wait_ge(s["z_in"], h + 1)
                            dve.scalar_tensor_tensor(zs, zs, 1.0, g_bank[q.par][:], ALU.add, ALU.mult).then_inc(bank_free[q.par], 1)
                    dve.wait_ge(s["bc_sb"], 2 * h + 2)
                    g_tok = gb_tok[:, :, bass.ds(h, 1)].broadcast_to([P, TT, P])
                    dve.tensor_tensor(dec, tiles(gc_b), g_tok, ALU.subtract).then_inc(s["dm_a"], 1)
                    ends = gc_b.rearrange("p (c t) -> p c t", t=CHUNK)
                    dve.tensor_tensor(ek.rearrange("p (c t) -> p c t", t=CHUNK), ends,
                                      ends[:, :, CHUNK - 1:CHUNK].broadcast_to([P, NCH, CHUNK]), ALU.subtract).then_inc(s["ek_a"], 1)
                    dve.wait_ge(s["dm_a"], h + 1)
                    dve.tensor_scalar(dec, dec, 0.0, None, ALU.min).then_inc(s["dm_b"], 1)
                    dve.wait_ge(s["c_s"], 3 * h + 3)
                    dve.scalar_tensor_tensor(vn, vn, 0.5, be_b, ALU.mult, ALU.mult).then_inc(s["vb_r"], 1)
                    for i, f in ((1, 0.5), (0, 0.5 * P ** -0.5)):
                        dve.wait_ge(s["l_r"], 2 * h + 2)
                        dve.scalar_tensor_tensor(qkv[:, i], qkv[:, i], f, rr[:, i], ALU.mult, ALU.mult).then_inc(s["l_y"], 1)
                    dve.wait_ge(s["l_y"], 2 * h + 1)
                    dve.tensor_tensor(kb, kn, be_b, ALU.mult).then_inc(s["kb_r"], 1)
                    dve.wait_ge(s["kk_ps"], h + 1)
                    dve.wait_ge(s["dec_r"], h + 1)
                    dve.tensor_tensor(a_tr, tiles(b[4][:]), dec, ALU.mult).then_inc(s["kk_r"], 1)
                    dve.wait_ge(s["kk_r"], h + 1)
                    dve.wait_ge(s["qk_ps"], h + 1)
                    dve.tensor_tensor(dec, tiles(b[5][:]), dec, ALU.mult).then_inc(s["qk_r"], 1)
                    eye = ident[:].unsqueeze(1).broadcast_to([P, TT, P])
                    nt = 2 * LEVELS - 1
                    dve.wait_ge(s["al_r"], LEVELS * h + 1)
                    dve.tensor_tensor(t_t, eye, tiles(a_lv[:, 0]), ALU.subtract).then_inc(s["t_r"], 1)
                    dve.wait_ge(s["yy_ps"], LEVELS * h + 1)
                    dve.tensor_tensor(t_m, eye, tiles(b[0][:]), ALU.subtract).then_inc(s["t_r"], 1)
                    for lv in range(1, LEVELS):
                        nz = 2 * (LEVELS - 1) - 1
                        if lv < LEVELS - 1:
                            dve.wait_ge(s["z_ps"], nz * h + 2 * lv)
                            dve.wait_ge(s["t_r"], nt * h + 2 * lv)
                            dve.tensor_tensor(t_m, t_m, tiles(b[1][:]), ALU.subtract).then_inc(s["t_r"], 1)
                            dve.tensor_tensor(t_t, t_t, tiles(b[2][:]), ALU.subtract).then_inc(s["t_r"], 1)
                        else:
                            dve.wait_ge(s["z_ps"], nz * (h + 1))
                            dve.wait_ge(s["t_r"], nt * h + 2 * lv)
                            dve.tensor_tensor(t_t, t_t, tiles(b[2][:]), ALU.subtract).then_inc(s["t_r"], 1)
                    dve.wait_ge(s["u_sb"], 2 * h + 2)
                    for c in range(NCH):
                        r = slice(CHUNK * (c % 2), CHUNK * (c % 2) + CHUNK)
                        if c == 0:
                            dve.tensor_copy(v_new[r, 0], u_m[r, 0]).then_inc(s["vn_r"], 1)
                        else:
                            dve.wait_ge(s["ws_ps"], (NCH - 1) * h + c)
                            dve.tensor_tensor(v_new[r, c // 2], u_m[r, c // 2], b[5][r, 0:P], ALU.subtract).then_inc(s["vn_r"], 1)
                        if c < NCH - 1:
                            dve.wait_ge(s["kv_ps"], (NCH - 1) * h + c + 1)
                            e1 = CHUNK * (c + 1) - 1
                            if c == 0:
                                dve.tensor_copy(st[:, 1], b[0][:, 0:P]).then_inc(s["st2"], 1)
                            else:
                                dve.wait_ge(s["st2"], (NCH - 1) * h + c)
                                dve.scalar_tensor_tensor(st[:, (c + 1) % 2], st[:, c % 2], eg_b[:, e1:e1 + 1], b[0][:, 0:P],
                                                         ALU.mult, ALU.add).then_inc(s["st2"], 1)
                    dve.wait_ge(s["oo_ps"], h + 1)
                    dve.tensor_copy(y_m, tiles(b[3][:])).then_inc(s["oo_c"], 1)
                    dve.wait_ge(s["oo_c"], 3 * h + 1)
                    yv = y_m.rearrange("p t (e c) -> p t e c", e=2)
                    dve.tensor_tensor(yv[:, 1:, 0], yv[:, 1:, 0], tiles(b[1][:])[:, 1:, 0:CHUNK], ALU.add).then_inc(s["oo_c"], 1)
                    dve.tensor_tensor(yv[:, :, 1], yv[:, :, 1], tiles(b[2][:])[:, :, 0:CHUNK], ALU.add).then_inc(s["oo_c"], 1)
                    dve.wait_ge(s["oo_c"], 3 * h + 3)
                    dve.sem_inc(s["oo_y1"], 1)
                    dve.scalar_tensor_tensor(y_o, y_m.rearrange("p t c -> p (t c)"), gains[:, G_GDN:G_GDN + 1], zs,
                                             ALU.mult, ALU.mult).then_inc(s["oo_y2"], 1)
                    dve.wait_ge(s["oo_y2"], h + 1)
                    dve.wait_ge(s["oo_r"], h + 1)
                    dve.tensor_tensor(y_o, y_o, r_o, ALU.mult).then_inc(s["oo_y3"], 1)
                    dve.wait_ge(s["oo_y3"], 2 * h + 1)
                    dve.wait_ge(s["ga_in"], h + 1)
                    dve.scalar_tensor_tensor(y_o, ga, 1.0, y_o, ALU.add, ALU.mult).then_inc(s["oo_y3"], 1)
                    dve.wait_ge(s["oo_y3"], 2 * h + 2)
                    dve.tensor_tensor(y_o, y_o, o_att[:, bass.ds(h, 1)].rearrange("p a t -> p (a t)"), ALU.add).then_inc(s["oo_y4"], 1)
                    dve.wait_ge(s["oo_y4"], h + 1)
                    dve.wait_ge(s["oo_hi"], h + 1)
                    dve.scalar_tensor_tensor(m_lo[:, bass.ds(h, 1)].rearrange("p a t -> p (a t)"), y_o, 0.5,
                                             m_hi[:, bass.ds(h, 1)].rearrange("p a t -> p (a t)").bitcast(F32),
                                             ALU.mult, ALU.subtract).then_inc(s["gdn_done"], 1)

        def pool_gdn(pool):
            with pool.Fori(0, GDN_H) as h:
                pool.wait_ge(s["dm_c"], h + 1)
                pool.tensor_tensor(dec, dec, mask(LEVELS + 1), ALU.mult).then_inc(s["dec_r"], 1)
                pool.wait_ge(s["kb_r"], h + 1)
                pool.wait_ge(s["eg_r"], h + 1)
                pool.tensor_tensor(kbe, kb, eg_b, ALU.mult).then_inc(s["kbe_r"], 1)
                pool.wait_ge(s["ek_b"], h + 1)
                pool.wait_ge(s["l_y"], 2 * h + 2)
                pool.tensor_tensor(ek, ek, kn, ALU.mult).then_inc(s["ek_c"], 1)
                for lv in range(LEVELS):
                    pool.wait_ge(s["kk_r"], h + 1)
                    if lv >= 2:
                        pool.wait_ge(s["yy_ps"], LEVELS * h + lv - 1)
                        if lv == 2:
                            pool.wait_ge(s["t_r"], (2 * LEVELS - 1) * h + 1)
                    pool.tensor_tensor(tiles(a_lv[:, lv % 2]), a_tr, mask(lv + 1), ALU.mult).then_inc(s["al_r"], 1)
                pool.tensor_tensor(q_dec, qn, eg_b, ALU.mult).then_inc(s["qd_r"], 1)

        at[0] = 0
        nb1 = norm_bufs()
        mlp_bufs = take(2, SEQ), take(2, SEQ)
        nm1 = Norm(G_FFN0, True)
        nmf = Norm(G_FINAL, False)
        nm2 = Norm(G_MIX1, True)
        nm3 = Norm(G_MLP1, True)
        y_tok = take(TT, D)

        block = ctx.enter_context(nc.Block())

        @block.sync
        def _(sp):
            sp_start(sp)
            sp_gla(sp)
            sp_panels(sp, N_WO0, rows(t["l0_w_out"]))
            sp_mlp(sp, N_FF0, t["l0_w_ff1"], t["l0_w_ff2"])
            sp_in1(sp)
            sp_att(sp)
            sp_gdn(sp)
            sp_panels(sp, N_WO1, rows(t["w_out_2"][0]))
            sp_mlp(sp, N_FF1, t["w_mlp_up_2"][0], t["w_mlp_down_2"][0])
            sp_out(sp, y_tok)

        @block.tensor
        def _(pe):
            pe_start(pe)
            pe.wait_ge(s["memsets"], 3)
            fence(pe, 1)
            pe_norm(pe, nm0, nb0)
            pe_gates(pe)
            pe_gla(pe)
            pe.wait_ge(s["gla_done"], GLA_H + 1)
            pe_wout(pe, N_WO0)
            fence(pe, 2)
            pe_norm(pe, nm1, nb1)
            pe_mlp(pe, N_FF0, 0, KT)
            fence(pe, 3)
            pe_norm(pe, nmf, nb1)
            fence(pe, 4)
            pe_norm(pe, nm2, nb2)
            pe_in1(pe)
            pe_att(pe)
            fence(pe, 5)
            pe_gdn(pe)
            pe.wait_ge(s["gdn_done"], GDN_H + 1)
            pe_wout(pe, N_WO1)
            fence(pe, 6)
            pe_norm(pe, nm3, nb1)
            pe_mlp(pe, N_FF1, 1, 3 * KT)
            fence(pe, 7)
            pe_out(pe, y_tok)

        @block.scalar
        def _(act):
            act_start(act)
            act_split(act, Panel(N_GK, 0, 0, 0))
            fence(act, 1)
            act_norm(act, nm0, nb0)
            act_gates(act)
            act_gla(act)
            act_wout(act, N_WO0)
            fence(act, 2)
            act_norm(act, nm1, nb1)
            act_mlp(act, N_FF0, 0, mlp_bufs, 0)
            fence(act, 3)
            act_norm(act, nmf, nb1)
            fence(act, 4)
            act_norm(act, nm2, nb2)
            act_in1(act)
            act_att(act)
            fence(act, 5)
            act_gdn(act)
            act_wout(act, N_WO1)
            fence(act, 6)
            act_norm(act, nm3, nb1)
            act_mlp(act, N_FF1, 1, mlp_bufs, 1)
            fence(act, 7)
            act_out(act, y_tok)

        @block.vector
        def _(dve):
            dve_start(dve)
            dve_split(dve, Panel(N_GK, 0, 0, 0))
            fence(dve, 1)
            dve_norm(dve, nm0, nb0)
            dve_gates(dve)
            dve_gla(dve)
            dve_wout(dve, N_WO0)
            fence(dve, 2)
            for done in gla_sems + gate_sems:
                dve.sem_clear(done)
            dve_norm(dve, nm1, nb1)
            dve.sem_inc(s["hid_ready"], 2)
            dve.sem_inc(s["down_done"], 1)
            dve_mlp(dve, N_FF0, 0, mlp_bufs, 0)
            fence(dve, 3)
            dve_norm(dve, nmf, nb1)
            fence(dve, 4)
            dve.sem_inc(s["att_done"], 1)
            dve_norm(dve, nm2, nb2)
            dve_in1(dve)
            dve_att(dve)
            fence(dve, 5)
            dve_gdn(dve)
            dve_wout(dve, N_WO1)
            fence(dve, 6)
            dve_norm(dve, nm3, nb1)
            dve_mlp(dve, N_FF1, 1, mlp_bufs, 1)
            fence(dve, 7)

        @block.gpsimd
        def _(pool):
            fence(pool, 1)
            pool_gla(pool)
            fence(pool, 2)
            fence(pool, 3)
            fence(pool, 4)
            pool_in1(pool)
            pool_att(pool)
            fence(pool, 5)
            pool_gdn(pool)
            fence(pool, 6)
            fence(pool, 7)


NAMES = ["x", "l0_norm_mix", "l0_w_in", "l0_w_gk_up", "l0_b_gk", "l0_g_onorm", "l0_w_out", "l0_norm_ffn",
         "l0_w_ff1", "l0_w_ff2", "final_norm", "norm_mix_g_2", "w_in_2", "conv_w_2", "a_log_2", "dt_bias_2",
         "gdn_norm_g_2", "q_norm_g_2", "k_norm_g_2", "w_out_2", "norm_mlp_g_2", "w_mlp_up_2", "w_mlp_down_2"]


def kernel(**inputs):
    import concourse.bacc as bacc
    from concourse.bass_utils import run_bass_kernel_spmd

    nc = bacc.Bacc("TRN2", target_bir_lowering=False, num_devices=1)
    arrays = {f"in_{n}": np.ascontiguousarray(inputs[n]) for n in NAMES}
    square, wide = host_constants()
    arrays["const_square"], arrays["const_wide"] = square, wide
    aps = {k: nc.dram_tensor(k, a.shape, mybir.dt.from_np(a.dtype), kind="ExternalInput").ap()
           for k, a in arrays.items()}
    out = nc.dram_tensor("out", (1, SEQ, D), F32, kind="ExternalOutput").ap()
    build(nc, {n: aps[f"in_{n}"] for n in NAMES}, out, aps["const_square"], aps["const_wide"])
    r = run_bass_kernel_spmd(nc, [arrays], core_ids=[0])
    return r.results[0]["out"]
```

```python
from contextlib import ExitStack

import numpy as np

import concourse.bass as bass
from concourse import mybir

F32 = mybir.dt.float32
F32R = mybir.dt.float32r
U32 = mybir.dt.uint32
ALU = mybir.AluOpType
ACT = mybir.ActivationFunctionType
AX = mybir.AxisListType

P = 128
SEQ, D, DFF = 512, 1024, 4096
KT = D // P
TT = SEQ // P
EPS = 1e-6
CHUNK = 64
NCH = SEQ // CHUNK
LEVELS = 6

GLA_H, GLA_K, GLA_V = 4, 128, 256
GLA_RANK = 16
GLA_GATE_NORM = 16.0
GLA_Q0, GLA_K0, GLA_V0, GLA_R0, GLA_G0 = 0, 512, 1024, 2048, 3072

GDN_H = 8
QKV0, Z0 = 0, 3072
GA0 = 4096
GB0 = GA0 + GDN_H
AQ0 = GB0 + GDN_H
AK0 = AQ0 + D
AV0 = AK0 + 256
IQ0 = AV0 + 256
IK0 = IQ0 + 512
IW0 = IK0 + 64
GTA0 = IW0 + 8
GTB0 = GTA0 + D
CONV = 4
ATT_H, ATT_KV = 8, 2
IDX_H, IDX_D = 8, 64
TOPK = min(256, SEQ // 4)
NOT_CAUSAL = -3.0e38
TAKEN = -3.4e38
BIG = 1.0e30

G_MIX0, G_FFN0, G_FINAL, G_MIX1, G_MLP1 = 0, 8, 16, 24, 32
G_BGK, G_ON, G_GDN, G_QN, G_KN = 40, 44, 46, 47, 48
N_GAIN = 49


def host_constants():
    j, i = np.meshgrid(np.arange(P), np.arange(P), indexing="ij")
    same = (j // CHUNK) == (i // CHUNK)
    masks = [(j == i)]
    for lv in range(LEVELS):
        s = 1 << lv
        masks.append((j // (2 * s) == i // (2 * s)) & (j % (2 * s) < s) & (i % (2 * s) >= s))
    masks.append(same & (j <= i))
    masks = np.stack(masks, 1).astype(np.float32)
    ident = np.eye(P, dtype=np.float32)

    def rope(seq, rot, width):
        inv = (np.float32(500000.0) ** (-np.arange(0, rot, 2, dtype=np.float32) / np.float32(rot))).astype(np.float32)
        ang = (np.arange(seq, dtype=np.float32)[:, None] * inv[None, :]).astype(np.float32)
        half = rot // 2
        c = np.ones((P, seq), np.float32)
        s = np.zeros((P, seq), np.float32)
        swap = np.zeros((P, P), np.float32)
        for b in range(0, P, width):
            for f in range(half):
                c[b + f] = c[b + half + f] = np.cos(ang[:, f])
                s[b + f] = s[b + half + f] = np.sin(ang[:, f])
                swap[b + half + f, b + f] = -1.0
                swap[b + f, b + half + f] = 1.0
        return c, s, swap

    ca, sa, pa = rope(SEQ, 32, P)
    ci, si, pi = rope(SEQ, 16, IDX_D)
    keep = np.ones((P, SEQ), np.float32)
    keep[:, ::CHUNK] = 0.0
    square = np.concatenate([ident, masks.reshape(P, -1), pa, pi], axis=1)
    wide = np.stack([ca, sa, ci, si, keep], 0)
    return square, wide


def build(nc, t, out, const_square, const_wide, upto=99):
    with ExitStack() as ctx:
        def sb(name, shape, dt=F32):
            return ctx.enter_context(nc.sbuf_tensor(name, shape, dt))

        def sem(name):
            return ctx.enter_context(nc.semaphore(name))

        s = {}

        cleared = []

        def sems(names, reuse=False):
            got = []
            for name in names.split():
                s[name] = cleared.pop() if reuse and cleared else sem(name)
                got.append(s[name])
            return got

        raw = [sb(f"raw{b}", [P, KT, P]) for b in range(2)]
        w_hi = [sb(f"w_hi{b}", [P, KT, P], F32R) for b in range(2)]
        w_lo = [sb(f"w_lo{b}", [P, KT, P], F32R) for b in range(2)]
        h_hi, h_lo = sb("h_hi", [P, KT, SEQ], F32R), sb("h_lo", [P, KT, SEQ], F32R)
        with nc.sbuf_tensor("m_hi", [P, KT, SEQ], F32R) as m_hi, nc.sbuf_tensor("m_lo", [P, KT, SEQ], F32R) as m_lo:
            pass
        q_all, q_sq = sb("q_all", [P, KT, SEQ]), sb("q_sq", [P, KT, SEQ])
        x = sb("x", [P, KT, SEQ])
        ident = sb("ident", [P, P])
        masks = sb("masks", [P, LEVELS + 2, P])
        swap_a, swap_i = sb("swap_a", [P, P]), sb("swap_i", [P, P])
        ones = sb("ones", [P, P])
        gains = sb("gains", [P, N_GAIN])
        conv_w = sb("conv_w", [P, CONV * 3 * GDN_H])
        eps = sb("eps", [P, 1])
        arena = sb("arena", [P, 22400])
        at = [0]

        def take(*shape):
            n = int(np.prod(shape))
            v = arena[:, at[0]:at[0] + n]
            at[0] += n
            assert at[0] <= 22400, at[0]
            if len(shape) == 2:
                v = v.rearrange("p (a b) -> p a b", a=shape[0])
            if len(shape) == 3:
                v = v.rearrange("p (a b c) -> p a b c", a=shape[0], b=shape[1])
            return v

        bank = [ctx.enter_context(nc.psum_tensor(f"bank{i}", [P, SEQ], F32)) for i in range(8)]
        g_bank, b = bank[0:2], bank[2:8]

        def tiles(ap, n=TT):
            return ap.rearrange("p (t c) -> p t c", t=n)

        def mask(lv):
            return masks[:, lv, :].unsqueeze(1).broadcast_to([P, TT, P])

        sems("piece_in w_hi_ready w_ready phase_done x_in params_in consts_in out_done")
        raw_in = [sem(f"raw_in{i}") for i in range(2)]
        mm_done = [sem(f"mm_done{i}") for i in range(2)]
        bank_free = [sem(f"bank_free{i}") for i in range(2)]
        pieces_sent = [0]

        class Panel:

            def __init__(self, base, per, h, u):
                self.par = (base + u) % 2
                self.n = base + u + per * h
                self.k = (base + u - self.par) // 2 + (per // 2) * h
                self.key = (base, per, h, u)

            def next(self):
                base, per, h, u = self.key
                return Panel(base, per, h, u + 1)

        def load(sp, q, pieces):
            sp.wait_ge(s["w_ready"], q.n + 1)
            for i, (src, c) in enumerate(pieces):
                if i == len(pieces) - 1:
                    if i:
                        sp.wait_ge(s["piece_in"], 16 * pieces_sent[0])
                    sp.dma_start(raw[q.par][:, :, c:c + src.shape[2]], src).then_inc(raw_in[q.par], 16)
                else:
                    sp.dma_start(raw[q.par][:, :, c:c + src.shape[2]], src).then_inc(s["piece_in"], 16)
                    pieces_sent[0] += 1

        def act_split(act, q):
            act.wait_ge(raw_in[q.par], 16 * (q.k + 1))
            act.wait_ge(mm_done[q.par], q.k + 1)
            act.copy(w_hi[q.par][:], raw[q.par][:]).then_inc(s["w_hi_ready"], 1)

        def dve_split(dve, q):
            dve.wait_ge(s["w_hi_ready"], q.n + 1)
            dve.tensor_tensor(w_lo[q.par][:], raw[q.par][:], w_hi[q.par][:].bitcast(F32),
                              ALU.subtract).then_inc(s["w_ready"], 1)

        def pool_split(pool, q):
            pool.wait_ge(s["w_ready"], q.n + 2)
            pool.wait_ge(s["w_hi_ready"], q.n + 1)
            pool.tensor_tensor(w_lo[q.par][:], raw[q.par][:], w_hi[q.par][:].bitcast(F32),
                               ALU.subtract).then_inc(s["w_ready"], 1)

        def pe_panel(pe, q, hi, lo, ready=None, count=0):
            pe.wait_ge(s["w_ready"], q.n + 3)
            pe.wait_ge(bank_free[q.par], q.k + 1)
            for k in range(KT):
                if ready is not None:
                    pe.wait_ge(ready, count + k + 1)
                pe.matmul(g_bank[q.par][:], w_hi[q.par][:, k], hi[:, k], start=(k == 0), stop=False)
                pe.matmul(g_bank[q.par][:], w_hi[q.par][:, k], lo[:, k], start=False, stop=False)
                last = pe.matmul(g_bank[q.par][:], w_lo[q.par][:, k], hi[:, k], start=False, stop=(k == KT - 1))
            last.then_inc(mm_done[q.par], 1)

        def wait_panel(eng, q):
            eng.wait_ge(mm_done[q.par], q.k + 2)

        N_GK = 0
        N_GLA = 1
        N_WO0 = N_GLA + 6 * GLA_H
        N_FF0 = N_WO0 + KT
        GROUPS = DFF // D
        N_IN1 = N_FF0 + 16 * GROUPS
        N_GDN = N_IN1 + 10 + 2 * ATT_H
        N_WO1 = N_GDN + 5 * GDN_H
        N_FF1 = N_WO1 + KT
        N_END = N_FF1 + 16 * GROUPS

        def rows(w):
            return w.rearrange("(k p) c -> p k c", p=P)

        def fence(eng, p):
            eng.drain().then_inc(s["phase_done"], 1)
            eng.wait_ge(s["phase_done"], 4 * p)

        at[0] = 0
        x_tok = take(TT, D)
        par_rows = take(2, P)
        sems("x_t x_s memsets par_t par_s")

        def sp_start(sp):
            gain_rows = [("l0_norm_mix", G_MIX0, 8), ("l0_norm_ffn", G_FFN0, 8), ("final_norm", G_FINAL, 8),
                         ("norm_mix_g_2", G_MIX1, 8), ("norm_mlp_g_2", G_MLP1, 8), ("l0_b_gk", G_BGK, 4),
                         ("l0_g_onorm", G_ON, 2), ("gdn_norm_g_2", G_GDN, 1), ("q_norm_g_2", G_QN, 1),
                         ("k_norm_g_2", G_KN, 1)]
            xv = t["x"].rearrange("b (t p) d -> p (b t) d", p=P)
            sp.dma_start(x_tok, xv).then_inc(s["x_in"], 16)
            sp.dma_start(ident[:], const_square[:, 0:P]).then_inc(s["x_in"], 16)
            load(sp, Panel(N_GK, 0, 0, 0), [(rows(t["l0_w_in"])[:, :, GLA_G0:GLA_G0 + 16], 0),
                                            (rows(t["l0_w_in"])[:, :, 0:P - 16], 16)])
            for name, r, n in gain_rows:
                a = t[name]
                if len(a.shape) == 2:
                    a = a.rearrange("a d -> (a d)")
                sp.dma_start(par_rows[r:r + n, 0, :], a.rearrange("(k p) -> k p", p=P)).then_inc(s["params_in"], 16)
            sp.dma_start(par_rows[0:CONV * 24, 1, :],
                         t["conv_w_2"].rearrange("a j (c p) -> (a j c) p", p=P)).then_inc(s["params_in"], 16)
            c0 = P
            sp.dma_start(masks[:], const_square[:, c0:c0 + 8 * P].rearrange("p (l c) -> p l c", c=P)).then_inc(s["consts_in"], 16)
            sp.dma_start(swap_a[:], const_square[:, c0 + 8 * P:c0 + 9 * P]).then_inc(s["consts_in"], 16)
            sp.dma_start(swap_i[:], const_square[:, c0 + 9 * P:c0 + 10 * P]).then_inc(s["consts_in"], 16)

        PARAM_DMAS = 11

        def pe_start(pe):
            pe.sem_inc(mm_done[0], 1)
            pe.sem_inc(mm_done[1], 1)
            pe.wait_ge(s["x_in"], 32)
            for k in range(KT):
                if k >= 2:
                    pe.wait_ge(s["x_s"], k - 1)
                for tt in range(TT):
                    last = pe.transpose(b[k % 2][:, tt * P:(tt + 1) * P], x_tok[:, tt, k * P:(k + 1) * P], ident[:])
                last.then_inc(s["x_t"], 1)
            pe.wait_ge(s["params_in"], 16 * PARAM_DMAS)
            pe.transpose(b[2][:, 0:N_GAIN], par_rows[0:N_GAIN, 0, :], ident[0:N_GAIN, 0:N_GAIN]).then_inc(s["par_t"], 1)
            n = CONV * 24
            pe.transpose(b[3][:, 0:n], par_rows[0:n, 1, :], ident[0:n, 0:n]).then_inc(s["par_t"], 1)

        def act_start(act):
            for k in range(KT):
                act.wait_ge(s["x_t"], k + 1)
                act.copy(x[:, k], b[k % 2][:]).then_inc(s["x_s"], 1)
            act.wait_ge(s["par_t"], 1)
            act.copy(gains[:], b[2][:, 0:N_GAIN]).then_inc(s["par_s"], 1)
            act.wait_ge(s["par_t"], 2)
            act.copy(conv_w[:], b[3][:, 0:CONV * 24]).then_inc(s["par_s"], 1)

        def dve_start(dve):
            dve.sem_inc(s["w_ready"], 2)
            dve.sem_inc(bank_free[0], 1)
            dve.sem_inc(bank_free[1], 1)
            dve.memset(ones[:], 1.0).then_inc(s["memsets"], 1)
            dve.memset(eps[:], EPS).then_inc(s["memsets"], 1)
            dve.wait_ge(s["par_s"], 2)
            dve.tensor_scalar(gains[:, G_ON:G_ON + 3], gains[:, G_ON:G_ON + 3], 0.5, None, ALU.mult).then_inc(s["memsets"], 1)

        sems("n_sq n_acc n_ss n_ln n_r n_h n_hi h_ready")
        norm_uses = [0]

        class Norm:
            def __init__(self, gain, split):
                self.i, self.gain, self.split = norm_uses[0], gain, split
                self.j = sum(1 for q in norm_list if q.split)
                norm_uses[0] += 1
                norm_list.append(self)

        norm_list = []

        def norm_bufs():
            return take(2, SEQ), take(SEQ), take(SEQ), take(2, SEQ)

        def act_norm(act, nm, bufs):
            sq, acc, r, hb = bufs
            i = nm.i
            for k in range(KT):
                if k >= 2:
                    act.wait_ge(s["n_acc"], KT * i + k - 1)
                act.activation(sq[:, k % 2], x[:, k], ACT.Square).then_inc(s["n_sq"], 1)
            act.wait_ge(s["n_ss"], i + 1)
            act.activation(r, b[0][:], ACT.Ln, scale=1.0 / D, bias=eps[:]).then_inc(s["n_ln"], 1)
            act.wait_ge(s["n_ln"], i + 1)
            act.activation(r, r, ACT.Exp, scale=-0.5).then_inc(s["n_r"], 1)
            if nm.split:
                for k in range(KT):
                    act.wait_ge(s["n_h"], KT * i + k + 1)
                    act.copy(h_hi[:, k], hb[:, k % 2]).then_inc(s["n_hi"], 1)

        def dve_norm(dve, nm, bufs):
            sq, acc, r, hb = bufs
            i = nm.i
            for k in range(KT):
                dve.wait_ge(s["n_sq"], KT * i + k + 1)
                if k == 0:
                    dve.tensor_copy(acc, sq[:, 0]).then_inc(s["n_acc"], 1)
                else:
                    dve.wait_ge(s["n_acc"], KT * i + k)
                    dve.tensor_tensor(acc, acc, sq[:, k % 2], ALU.add).then_inc(s["n_acc"], 1)
            dve.wait_ge(s["n_r"], i + 1)
            for k in range(KT):
                g = gains[:, nm.gain + k:nm.gain + k + 1]
                if nm.split:
                    if k >= 2:
                        dve.wait_ge(s["h_ready"], KT * nm.j + k - 1)
                    dve.scalar_tensor_tensor(hb[:, k % 2], x[:, k], g, r, ALU.mult, ALU.mult).then_inc(s["n_h"], 1)
                    if k >= 1:
                        dve_norm_lo(dve, nm, hb, k - 1)
                else:
                    dve.scalar_tensor_tensor(x[:, k], x[:, k], g, r, ALU.mult, ALU.mult).then_inc(s["n_h"], 1)
            if nm.split:
                dve_norm_lo(dve, nm, hb, KT - 1)
            else:
                dve.wait_ge(s["n_h"], KT * (i + 1))

        def dve_norm_lo(dve, nm, hb, k):
            dve.wait_ge(s["n_hi"], KT * nm.j + k + 1)
            dve.tensor_tensor(h_lo[:, k], hb[:, k % 2], h_hi[:, k].bitcast(F32), ALU.subtract).then_inc(s["h_ready"], 1)

        def pe_norm(pe, nm, bufs):
            sq, acc, r, hb = bufs
            pe.wait_ge(s["n_acc"], KT * (nm.i + 1))
            pe.matmul(b[0][:], ones[:], acc, start=True, stop=True).then_inc(s["n_ss"], 1)

        at[0] = 0
        nb0 = norm_bufs()
        nm0 = Norm(G_MIX0, True)
        keep_at = at[0]
        keep = take(SEQ)
        gk_up = take(512)
        gk_low = take(SEQ)
        b_all = take(GLA_H, SEQ)
        gt = take(2, SEQ)
        head_in = take(6, SEQ)
        own, at[0] = at[0], 0
        head_in = [head_in, take(6, SEQ)]
        assert at[0] <= keep_at
        at[0] = own
        v_tok = take(TT, GLA_V)
        arg = take(2, SEQ)
        ex = take(2, SEQ)
        mlev = take(2, SEQ)
        sm = take(2, SEQ)
        a_t = take(TT, P)
        eb, qe, kd = take(SEQ), take(SEQ), take(SEQ)
        kd_tok = take(TT, P)
        state = take(NCH, GLA_V)
        osq = ex
        rb = take(SEQ)
        sems("gk_in")
        gate_sems = sems("gkl gk_ps ga ge gl gm gd gscan gbs")
        gla_sems = sems("q_in k_in v_in vt_ps vt_sb tg gate_r arg_r ab_r ex_r mlev_r slev at_r eb_r qe_r kd_r kdt_ps kdt_sb "
             "u_ps sm_r st_r o_ps osq_r osum on_ps oln or_r y1 y2 y_hi gla_done")

        def u_at(c):
            o = (c // 2 % 2) * GLA_V
            return b[2 + 2 * (c % 2) + c // 4][:, o:o + GLA_V]

        def sp_gla(sp):
            sp.wait_ge(s["phase_done"], 4)
            sp.dma_start(keep, const_wide[4]).then_inc(s["gk_in"], 16)
            sp.dma_start(gk_up[0:GLA_RANK, :], t["l0_w_gk_up"]).then_inc(s["gk_in"], 16)
            w = rows(t["l0_w_in"])
            with sp.Fori(0, GLA_H) as h:
                starts = [GLA_Q0 + P * h, GLA_K0 + P * h, GLA_V0 + 2 * P * h, GLA_V0 + P + 2 * P * h,
                          GLA_R0 + 2 * P * h, GLA_R0 + P + 2 * P * h]
                for u, c in enumerate(starts):
                    load(sp, Panel(N_GLA, 6, h, u), [(w[:, :, bass.ds(c, P)], 0)])

        def pe_gates(pe):
            pe_panel(pe, Panel(N_GK, 0, 0, 0), h_hi, h_lo, s["h_ready"], 0)
            pe.wait_ge(s["gk_in"], 32)
            pe.wait_ge(s["gkl"], 1)
            for h in range(GLA_H):
                if h >= 2:
                    pe.wait_ge(s["gm"], h - 1)
                    pe.wait_ge(s["ga"], h - 1)
                pe.matmul(b[h % 2][:], gk_up[0:GLA_RANK, h * P:(h + 1) * P], gk_low[0:GLA_RANK, :],
                          start=True, stop=True).then_inc(s["gk_ps"], 1)

        def act_gates(act):
            q = Panel(N_GK, 0, 0, 0)
            act_split(act, q.next())
            wait_panel(act, q)
            act.copy(gk_low[0:GLA_RANK, :], g_bank[q.par][0:GLA_RANK, :]).then_inc(s["gkl"], 1)
            for h in range(GLA_H):
                act.wait_ge(s["gk_ps"], h + 1)
                if h >= 2:
                    act.wait_ge(s["gd"], h - 1)
                act.activation(gt[:, h % 2], b[h % 2][:], ACT.Abs,
                               bias=gains[:, G_BGK + h:G_BGK + h + 1]).then_inc(s["ga"], 1)
                act.wait_ge(s["ga"], h + 1)
                act.activation(gt[:, h % 2], gt[:, h % 2], ACT.Exp, scale=-1.0).then_inc(s["ge"], 1)
                act.wait_ge(s["ge"], h + 1)
                act.activation(gt[:, h % 2], gt[:, h % 2], ACT.Ln, bias=1.0).then_inc(s["gl"], 1)

        def dve_gates(dve):
            q = Panel(N_GK, 0, 0, 0)
            dve_split(dve, q.next())
            dve.wait_ge(s["gkl"], 1)
            dve.sem_inc(bank_free[q.par], 1)
            dve.wait_ge(s["gk_in"], 32)
            for h in range(GLA_H):
                dve.wait_ge(s["ga"], h + 1)
                dve.tensor_scalar(arg[:, h % 2], b[h % 2][:], gains[:, G_BGK + h:G_BGK + h + 1], 0.0,
                                  ALU.add, ALU.min).then_inc(s["gm"], 1)
                dve.wait_ge(s["gm"], h + 1)
                dve.wait_ge(s["gl"], h + 1)
                dve.tensor_tensor(arg[:, h % 2], arg[:, h % 2], gt[:, h % 2], ALU.subtract).then_inc(s["gd"], 1)
                dve.wait_ge(s["gd"], h + 1)
                dve.tensor_tensor_scan(b_all[:, h], keep, arg[:, h % 2], 0.0, ALU.mult, ALU.add).then_inc(s["gscan"], 1)
                dve.wait_ge(s["gscan"], h + 1)
                dve.tensor_scalar(b_all[:, h], b_all[:, h], 1.0 / GLA_GATE_NORM, None, ALU.mult).then_inc(s["gbs"], 1)
            dve.sem_inc(s["gla_done"], 1)

        NL = LEVELS + 1

        def gla_heads(eng, body):
            with eng.Fori(0, GLA_H // 2 - 1) as hp2:
                body(hp2, 0, True)
                body(hp2, 1, True)
            body(GLA_H // 2 - 1, 0, True)
            body(GLA_H // 2 - 1, 1, False)

        def pe_part(pe, q, i):
            if i == 0:
                pe.wait_ge(s["w_ready"], q.n + 3)
                pe.wait_ge(bank_free[q.par], q.k + 1)
            for k in (2 * i, 2 * i + 1):
                pe.matmul(g_bank[q.par][:], w_hi[q.par][:, k], h_hi[:, k], start=(k == 0), stop=False)
                pe.matmul(g_bank[q.par][:], w_hi[q.par][:, k], h_lo[:, k], start=False, stop=False)
                last = pe.matmul(g_bank[q.par][:], w_lo[q.par][:, k], h_hi[:, k], start=False, stop=(k == KT - 1))
            if i == 3:
                last.then_inc(mm_done[q.par], 1)

        def pe_gla(pe):
            for u in range(6):
                pe_panel(pe, Panel(N_GLA, 12, 0, u), h_hi, h_lo)

            def body(hp2, e, front):
                h = 2 * hp2 + e
                qf, kf, vf = head_in[e][:, 0], head_in[e][:, 1], head_in[e][:, 2:4]

                def part(*js):
                    if front:
                        for j in js:
                            pe_part(pe, Panel(N_GLA, 12, hp2, 6 * (e + 1) + j // 4), j % 4)

                pe.wait_ge(s["q_in"], h + 1)
                pe.wait_ge(s["k_in"], h + 1)
                for tt in range(TT):
                    c = slice(tt * P, (tt + 1) * P)
                    last = pe.matmul(b[0][:, c], kf[:, c], qf[:, c], start=True, stop=True)
                last.then_inc(s["slev"], 1)
                pe.wait_ge(s["oln"], h + 1)
                for xh in range(2):
                    pe.wait_ge(s["v_in"], 2 * h + xh + 1)
                    for tt in range(TT):
                        last = pe.transpose(b[4 + xh][:, tt * P:(tt + 1) * P], vf[:, xh, tt * P:(tt + 1) * P], ident[:])
                    last.then_inc(s["vt_ps"], 1)
                part(0, 1)
                for lv in range(LEVELS):
                    pe.wait_ge(s["mlev_r"], LEVELS * h + lv + 1)
                    if lv >= 1:
                        pe.wait_ge(s["at_r"] if lv == 1 else s["sm_r"], NL * h + 1 if lv == 1 else LEVELS * h + lv - 1)
                    for tt in range(TT):
                        c = slice(tt * P, (tt + 1) * P)
                        last = pe.matmul(b[(lv + 1) % 2][:, c], mlev[:, lv % 2, c], mlev[:, lv % 2, c],
                                         start=True, stop=True)
                    last.then_inc(s["slev"], 1)
                    part(2 * lv + 2, 2 * lv + 3)
                pe.wait_ge(s["kd_r"], h + 1)
                pe.wait_ge(s["y1"], 2 * h + 2)
                for tt in range(TT):
                    c = slice(tt * P, (tt + 1) * P)
                    last = pe.transpose(b[2][:, c], kd[:, c], ident[:])
                last.then_inc(s["kdt_ps"], 1)
                part(14, 15)
                pe.wait_ge(s["kdt_sb"], h + 1)
                pe.wait_ge(s["vt_sb"], 2 * h + 2)
                for c in range(NCH - 1):
                    r = slice(CHUNK * (c % 2), CHUNK * (c % 2) + CHUNK)
                    o = u_at(c)
                    last = pe.matmul(o, kd_tok[r, c // 2, :], v_tok[r, c // 2, :], start=True, stop=True)
                last.then_inc(s["u_ps"], 1)
                part(16, 17, 18, 19)
                pe.wait_ge(s["at_r"], NL * (h + 1))
                pe.wait_ge(s["st_r"], (NCH - 1) * (h + 1))
                pe.wait_ge(s["qe_r"], h + 1)
                for xh in range(2):
                    vc = slice(xh * P, (xh + 1) * P)
                    for tt in range(TT):
                        pe.matmul(b[2 + xh][:, tt * P:(tt + 1) * P], v_tok[:, tt, vc], a_t[:, tt, :],
                                  start=True, stop=False, skip_group_check=True)
                        for c in (2 * tt, 2 * tt + 1):
                            if c:
                                cc = slice(CHUNK * c, CHUNK * (c + 1))
                                last = pe.matmul(b[2 + xh][:, cc], state[:, c, vc], qe[:, cc],
                                                 start=False, stop=True, skip_group_check=True)
                    last.then_inc(s["o_ps"], 1)
                part(20, 21)
                pe.wait_ge(s["osum"], h + 1)
                pe.matmul(b[4][:], ones[:], osq[:, 0], start=True, stop=True).then_inc(s["on_ps"], 1)
                part(22, 23)

            gla_heads(pe, body)

        def act_gla(act):
            def q_evac(g, e, u, q):
                wait_panel(act, q)
                dst = head_in[e % 2]
                if u == 0:
                    act.mul(dst[:, 0], g_bank[q.par][:], GLA_K ** -0.5).then_inc(s["q_in"], 1)
                    act.wait_ge(s["q_in"], g + 1)
                    act.sem_inc(bank_free[q.par], 1)
                elif u == 1:
                    act.copy(dst[:, 1], g_bank[q.par][:]).then_inc(s["k_in"], 1)
                    act.wait_ge(s["k_in"], g + 1)
                    act.sem_inc(bank_free[q.par], 1)
                else:
                    act.activation(dst[:, u], g_bank[q.par][:], ACT.Tanh, scale=0.5).then_inc(s["tg"], 1)

            def decay(g, i):
                act.wait_ge(s["arg_r"], NL * g + i + 1)
                act.activation(arg[:, i % 2], arg[:, i % 2], ACT.Abs).then_inc(s["ab_r"], 1)
                act.wait_ge(s["ab_r"], NL * g + i + 1)
                if i == 2:
                    act.wait_ge(s["kd_r"], g + 1)
                if i >= 3:
                    act.wait_ge(s["mlev_r"], LEVELS * g + i - 2)
                act.activation(ex[:, i % 2], arg[:, i % 2], ACT.Exp, scale=-1.0).then_inc(s["ex_r"], 1)

            def to_start(g):
                act.activation(eb, b_all[:, bass.ds(g, 1)].rearrange("p a t -> p (a t)"), ACT.Exp).then_inc(s["eb_r"], 1)

            for u in range(6):
                q = Panel(N_GLA, 12, 0, u)
                act_split(act, q.next())
                if u < 2 or u >= 4:
                    q_evac(0, 0, u, q)
            to_start(0)
            decay(0, 0)
            decay(0, 1)
            act.sem_inc(s["oln"], 1)

            def body(hp2, e, front):
                h = 2 * hp2 + e
                yb = head_in[e][:, 2:4]

                def q(u):
                    return Panel(N_GLA, 12, hp2, 6 * (e + 1) + u)

                if front:
                    act_split(act, q(1))
                decay(h, 2)
                for xh in range(2):
                    act.wait_ge(s["vt_ps"], 2 * h + xh + 1)
                    act.copy(v_tok[:, :, xh * P:(xh + 1) * P], tiles(b[4 + xh][:])).then_inc(s["vt_sb"], 1)
                decay(h, 3)
                if front:
                    q_evac(h + 1, e + 1, 0, q(0))
                    act_split(act, q(2))
                decay(h, 4)
                decay(h, 5)
                if front:
                    q_evac(h + 1, e + 1, 1, q(1))
                    act_split(act, q(3))
                decay(h, 6)
                if front:
                    act_split(act, q(4))
                act.wait_ge(s["kdt_ps"], h + 1)
                act.copy(kd_tok, tiles(b[2][:])).then_inc(s["kdt_sb"], 1)
                if front:
                    act_split(act, q(5))
                    q_evac(h + 1, e + 1, 4, q(4))
                    act_split(act, q(6))
                for xh in range(2):
                    act.wait_ge(s["o_ps"], 2 * h + xh + 1)
                    act.activation(osq[:, xh], b[2 + xh][:], ACT.Square).then_inc(s["osq_r"], 1)
                act.wait_ge(s["on_ps"], h + 1)
                act.activation(rb, b[4][:], ACT.Ln, scale=1.0 / GLA_V, bias=eps[:]).then_inc(s["oln"], 1)
                act.wait_ge(s["oln"], h + 2)
                act.activation(rb, rb, ACT.Exp, scale=-0.5).then_inc(s["or_r"], 1)
                if front:
                    decay(h + 1, 0)
                    decay(h + 1, 1)
                    to_start(h + 1)
                    q_evac(h + 1, e + 1, 5, q(5))
                for xh in range(2):
                    act.wait_ge(s["y2"], 2 * h + xh + 1)
                    act.copy(m_hi[:, bass.ds(2 * h + xh, 1)].rearrange("p a t -> p (a t)"), yb[:, xh]).then_inc(s["y_hi"], 1)

            gla_heads(act, body)

        def dve_gla(dve):
            def evac(g, e, u, q):
                dst = head_in[e % 2][:, u]
                if u < 4:
                    wait_panel(dve, q)
                    dve.tensor_copy(dst, g_bank[q.par][:]).then_inc(s["v_in"], 1)
                    dve.wait_ge(s["v_in"], 2 * g + u - 1)
                    dve.sem_inc(bank_free[q.par], 1)
                else:
                    dve.wait_ge(s["tg"], 2 * g + u - 3)
                    dve.scalar_tensor_tensor(dst, dst, 1.0, g_bank[q.par][:], ALU.add, ALU.mult).then_inc(bank_free[q.par], 1)

            def exponent(g, i):
                bh = b_all[:, bass.ds(g, 1)].rearrange("p a t -> p (a t)")
                w, c = (CHUNK, CHUNK - 1) if i == 0 else (1 << i, (1 << i) // 2 - 1)
                v = bh.rearrange("p (c t) -> p c t", t=w)
                if i >= 2:
                    dve.wait_ge(s["ex_r"], NL * g + i - 1)
                dve.tensor_tensor(arg[:, i % 2].rearrange("p (c t) -> p c t", t=w), v,
                                  v[:, :, c:c + 1].broadcast_to([P, SEQ // w, w]), ALU.subtract).then_inc(s["arg_r"], 1)

            for u in range(6):
                q = Panel(N_GLA, 12, 0, u)
                dve_split(dve, q.next())
                if u == 0:
                    exponent(0, 0)
                    exponent(0, 1)
                if u >= 2:
                    evac(0, 0, u, q)

            def body(hp2, e, front):
                h = 2 * hp2 + e
                gate, yb = head_in[e][:, 4:6], head_in[e][:, 2:4]

                def q(u):
                    return Panel(N_GLA, 12, hp2, 6 * (e + 1) + u)

                exponent(h, 2)
                dve.wait_ge(s["slev"], NL * h + 1)
                dve.tensor_tensor(a_t, tiles(b[0][:]), mask(0), ALU.mult).then_inc(s["at_r"], 1)
                if front:
                    dve_split(dve, q(1))
                for lv in range(LEVELS):
                    if lv + 3 <= LEVELS:
                        exponent(h, lv + 3)
                    dve.wait_ge(s["slev"], NL * h + lv + 2)
                    if lv >= 2:
                        dve.wait_ge(s["at_r"], NL * h + lv)
                    dve.tensor_tensor(tiles(sm[:, lv % 2]), tiles(b[(lv + 1) % 2][:]), mask(lv + 1),
                                      ALU.mult).then_inc(s["sm_r"], 1)
                    if front and lv % 2 == 0:
                        dve_split(dve, q(2 + lv // 2))
                if front:
                    evac(h + 1, e + 1, 2, q(2))
                    dve_split(dve, q(5))
                    evac(h + 1, e + 1, 3, q(3))
                for c in range(NCH - 1):
                    dve.wait_ge(s["u_ps"], h + 1)
                    u = u_at(c)
                    if c == 0:
                        dve.wait_ge(s["eb_r"], h + 1)
                        dve.tensor_copy(state[:, 1], u).then_inc(s["st_r"], 1)
                    else:
                        dve.wait_ge(s["st_r"], (NCH - 1) * h + c)
                        e1 = CHUNK * (c + 1) - 1
                        dve.scalar_tensor_tensor(state[:, c + 1], state[:, c], eb[:, e1:e1 + 1], u,
                                                 ALU.mult, ALU.add).then_inc(s["st_r"], 1)
                if front:
                    evac(h + 1, e + 1, 4, q(4))
                    dve_split(dve, q(6))
                dve.wait_ge(s["osq_r"], 2 * h + 2)
                dve.tensor_tensor(osq[:, 0], osq[:, 0], osq[:, 1], ALU.add).then_inc(s["osum"], 1)
                for xh in range(2):
                    dve.scalar_tensor_tensor(yb[:, xh], b[2 + xh][:], gains[:, G_ON + xh:G_ON + xh + 1],
                                             gate[:, xh], ALU.mult, ALU.mult).then_inc(s["y1"], 1)
                if front:
                    exponent(h + 1, 0)
                    exponent(h + 1, 1)
                dve.wait_ge(s["or_r"], h + 1)
                dve.wait_ge(s["y1"], 2 * h + 4)
                for xh in range(2):
                    dve.tensor_tensor(yb[:, xh], yb[:, xh], rb, ALU.mult).then_inc(s["y2"], 1)
                if front:
                    evac(h + 1, e + 1, 5, q(5))
                for xh in range(2):
                    dve.wait_ge(s["y_hi"], 2 * h + xh + 1)
                    i = bass.ds(2 * h + xh, 1)
                    last = dve.tensor_tensor(m_lo[:, i].rearrange("p a t -> p (a t)"), yb[:, xh],
                                             m_hi[:, i].rearrange("p a t -> p (a t)").bitcast(F32), ALU.subtract)
                last.then_inc(s["gla_done"], 1)

            dve.sem_inc(s["y1"], 2)
            gla_heads(dve, body)

        def pool_gla(pool):
            with pool.Fori(0, GLA_H // 2) as hp2:
                for e in range(2):
                    h = 2 * hp2 + e
                    qf, kf = head_in[e][:, 0], head_in[e][:, 1]

                    def add(lv):
                        pool.wait_ge(s["sm_r"], LEVELS * h + lv + 1)
                        pool.wait_ge(s["at_r"], NL * h + lv + 1)
                        pool.tensor_tensor(a_t, a_t, tiles(sm[:, lv % 2]), ALU.add).then_inc(s["at_r"], 1)

                    pool.wait_ge(s["q_in"], h + 1)
                    pool.wait_ge(s["k_in"], h + 1)
                    pool.wait_ge(s["ex_r"], NL * h + 1)
                    pool.tensor_tensor(kd, kf, ex[:, 0], ALU.mult).then_inc(s["kd_r"], 1)
                    for lv in range(LEVELS):
                        w = 1 << lv
                        pool.wait_ge(s["ex_r"], NL * h + lv + 2)
                        if lv >= 2:
                            pool.wait_ge(s["slev"], NL * h + lv)

                        def half(ap, i):
                            return ap.rearrange("p (c i t) -> p c i t", i=2, t=w)[:, :, i, :]

                        ev = ex[:, (lv + 1) % 2]
                        pool.tensor_tensor(half(mlev[:, lv % 2], 0), half(kf, 0), half(ev, 0), ALU.mult)
                        pool.tensor_tensor(half(mlev[:, lv % 2], 1), half(qf, 1), half(ev, 1), ALU.mult).then_inc(s["mlev_r"], 1)
                        if lv >= 2:
                            add(lv - 2)
                    add(LEVELS - 2)
                    add(LEVELS - 1)
                    pool.wait_ge(s["eb_r"], h + 1)
                    pool.tensor_tensor(qe, qf, eb, ALU.mult).then_inc(s["qe_r"], 1)

        sems("x_add")
        adds = [0]

        def sp_panels(sp, base, w):
            with sp.Fori(0, KT // 2) as m:
                for u in range(2):
                    load(sp, Panel(base, 2, m, u), [(w[:, :, bass.ds(2 * P * m + P * u, P)], 0)])

        def pe_wout(pe, base):
            with pe.Fori(0, KT // 2) as m:
                for u in range(2):
                    pe_panel(pe, Panel(base, 2, m, u), m_hi, m_lo)

        def act_wout(act, base):
            with act.Fori(0, KT // 2) as m:
                for u in range(2):
                    act_split(act, Panel(base, 2, m, u).next())

        def dve_wout(dve, base):
            with dve.Fori(0, KT // 2) as m:
                for u in range(2):
                    q = Panel(base, 2, m, u)
                    dve_split(dve, q.next())
                    wait_panel(dve, q)
                    xm = x[:, bass.ds(2 * m + u, 1)].rearrange("p a t -> p (a t)")
                    dve.tensor_tensor(xm, xm, g_bank[q.par][:], ALU.add).then_inc(bank_free[q.par], 1)

        sems("rl sqr hid_hi hid_ready down_done")

        def sp_mlp(sp, base, w1, w2):
            with sp.Fori(0, GROUPS) as g:
                for u in range(8):
                    load(sp, Panel(base, 16, g, u), [(rows(w1)[:, :, bass.ds(D * g + P * u, P)], 0)])
                w2g = w2.rearrange("(g k p) c -> p (g k) c", p=P, k=KT)
                for u in range(8):
                    load(sp, Panel(base, 16, g, 8 + u), [(w2g[:, bass.ds(KT * g, KT), P * u:P * (u + 1)], 0)])

        def pe_mlp(pe, base, i, first):
            with pe.Fori(0, GROUPS) as g:
                for u in range(8):
                    pe_panel(pe, Panel(base, 16, g, u), h_hi, h_lo, s["h_ready"] if u == 0 else None, first)
                for u in range(8):
                    pe_panel(pe, Panel(base, 16, g, 8 + u), m_hi, m_lo, s["hid_ready"] if u == 0 else None,
                             KT * GROUPS * i + KT * g + 2)

        def act_mlp(act, base, i, bufs, ends):
            rl, sq = bufs
            n = KT * GROUPS * i

            def group(g, no_next):
                for u in range(16):
                    q = Panel(base, 16, g, u)
                    if not (no_next and u == 15):
                        act_split(act, q.next())
                    if u < 8:
                        wait_panel(act, q)
                        act.wait_ge(s["hid_ready"], n + KT * g + u + 1)
                        act.activation(rl[:, u % 2], g_bank[q.par][:], ACT.Relu).then_inc(s["rl"], 1)
                        if u == 0:
                            act.wait_ge(s["down_done"], GROUPS * i + g + 1)
                        act.wait_ge(s["sqr"], n + KT * g + u + 1)
                        act.copy(m_hi[:, u], sq[:, u % 2]).then_inc(s["hid_hi"], 1)

            with act.Fori(0, GROUPS - ends) as g:
                group(g, False)
            if ends:
                group(GROUPS - 1, True)

        def dve_mlp(dve, base, i, bufs, ends):
            rl, sq = bufs
            n = KT * GROUPS * i

            def group(g, no_next):
                for u in range(16):
                    q = Panel(base, 16, g, u)
                    if not (no_next and u == 15):
                        dve_split(dve, q.next())
                    if u < 8:
                        dve.wait_ge(s["rl"], n + KT * g + u + 1)
                        dve.tensor_tensor(sq[:, u % 2], rl[:, u % 2], rl[:, u % 2], ALU.mult).then_inc(s["sqr"], 1)
                        dve.sem_inc(bank_free[q.par], 1)
                        dve.wait_ge(s["sqr"], n + KT * g + u + 1)
                        dve.wait_ge(s["hid_hi"], n + KT * g + u + 1)
                        dve.tensor_tensor(m_lo[:, u], sq[:, u % 2], m_hi[:, u].bitcast(F32),
                                          ALU.subtract).then_inc(s["hid_ready"], 1)
                    else:
                        wait_panel(dve, q)
                        dve.tensor_tensor(x[:, u - 8], x[:, u - 8], g_bank[q.par][:], ALU.add).then_inc(bank_free[q.par], 1)
                dve.sem_inc(s["down_done"], 1)

            with dve.Fori(0, GROUPS - ends) as g:
                group(g, False)
            if ends:
                group(GROUPS - 1, True)

        sems("y_ps y_sb")
        at_out = [0]

        def pe_out(pe, y_tok):
            for tt in range(TT):
                for hf in range(2):
                    i = 2 * tt + hf
                    if i >= 2:
                        pe.wait_ge(s["y_sb"], i - 1)
                    for k in range(4):
                        last = pe.transpose(b[i % 2][:, k * P:(k + 1) * P], x[:, 4 * hf + k, tt * P:(tt + 1) * P], ident[:])
                    last.then_inc(s["y_ps"], 1)

        def act_out(act, y_tok):
            for i in range(2 * TT):
                act.wait_ge(s["y_ps"], i + 1)
                act.copy(y_tok[:, i // 2, (i % 2) * 512:(i % 2 + 1) * 512], b[i % 2][:]).then_inc(s["y_sb"], 1)

        def sp_out(sp, y_tok):
            ov = out.rearrange("b (t p) d -> p (b t) d", p=P)
            for tt in range(TT):
                sp.wait_ge(s["y_sb"], 2 * tt + 2)
                sp.dma_start(ov[:, tt], y_tok[:, tt]).then_inc(s["out_done"], 16)
            sp.wait_ge(s["out_done"], 16 * TT)

        at[0] = 22400 - (SEQ + TT * 40 + ATT_H * SEQ)
        kept0 = at[0]
        gb = take(SEQ)
        gb_tok = take(TT, 40)
        o_att = take(ATT_H, SEQ)

        at[0] = 0
        ca, sa = take(SEQ), take(SEQ)
        ci_si_keep = take(3 * SEQ)
        ci, si, keep2 = (ci_si_keep[:, i * SEQ:(i + 1) * SEQ] for i in range(3))
        ak = take(2, SEQ)
        ms = [None, ci_si_keep[:, 0:1280]]
        v_key = [take(TT, P) for _ in range(ATT_KV)]
        sel = take(1280)
        r0 = at[0]
        ms[0] = take(1280)
        p_t = take(1280)
        aq = take(2, SEQ)
        r1, at[0] = at[0], r0
        iqs = take(4, SEQ)
        at[0] = r0
        nb2 = norm_bufs()
        assert at[0] <= r1
        at[0] = r1
        rp_c, rp_s = take(SEQ), take(SEQ)
        r128, sq128 = take(SEQ), take(SEQ)
        w_tok = take(TT, IDX_H)
        n_max, r_sum = take(2 * TT), take(TT)
        hp = take(4)
        small = take(SEQ)
        ik = take(SEQ)
        sc = take(1152)
        av = take(2, SEQ)
        gtmp = take(3, SEQ)
        lg = gtmp[:, 0:2]
        top8 = take(3, 8)
        assert at[0] <= kept0, (at[0], kept0)
        off = [0, 128, 384, 768]
        koff = [0, 512, 896, 1152]

        sems("t_in in1 z_ga z_ge z_gl z_gt z_mx z_sp z_g z_gb z_ea z_b wt_ps wt_sb gbt_ps gbt_sb "
             "r_sq r_ss r_ln r_r r_y rp_ps rp_cc rp_ss rp_out av_ps av_sb lg_ps lg_r lg_a sc_m mx8 rp8 sel_r zsel "
             "aq_in gtb_in s_ps ms_r nm_r nms ex_a rs_r pn_r pt_ps pt_sb pv_ps att_done")

        def sp_in1(sp):
            w = rows(t["w_in_2"][0])
            first = Panel(N_IN1, 0, 0, 0)
            load(sp, first, [(w[:, :, c:c + 32], d) for c, d in ((GA0, 0), (GB0, 32), (IW0, 64), (GTA0, 96))])
            load(sp, Panel(N_IN1, 0, 0, 1), [(w[:, :, IK0:IK0 + IDX_D], 0), (w[:, :, IK0:IK0 + IDX_D], IDX_D)])
            cols = [IQ0 + P * i for i in range(4)] + [AK0, AK0 + P, AV0, AV0 + P] + [c + P * i for c in (GTB0, AQ0) for i in range(ATT_H)]
            for i, c in enumerate(cols):
                load(sp, Panel(N_IN1, 0, 0, 2 + i), [(w[:, :, c:c + P], 0)])
                if i == 0:
                    sp.wait_ge(s["phase_done"], 16)
                    for j, dst in enumerate((ca, sa, ci, si, keep2)):
                        sp.dma_start(dst, const_wide[j]).then_inc(s["t_in"], 16)
                    for j, n in enumerate(("dt_bias_2", "a_log_2")):
                        sp.dma_start(hp[0:GDN_H, j:j + 1], t[n].rearrange("a d -> d a")).then_inc(s["t_in"], 16)

        def pe_rms(pe, c, bk):
            pe.wait_ge(s["r_sq"], c + 1)
            pe.matmul(bk[:], ones[:], sq128, start=True, stop=True).then_inc(s["r_ss"], 1)

        def act_rms(act, c, src, bk):
            if isinstance(c, int) and c == 0:
                pass
            else:
                act.wait_ge(s["r_ss"], c)
                act.wait_ge(s["r_y"], c)
            act.activation(sq128, src, ACT.Square).then_inc(s["r_sq"], 1)
            act.wait_ge(s["r_ss"], c + 1)
            act.activation(r128, bk[:], ACT.Ln, scale=1.0 / P, bias=eps[:]).then_inc(s["r_ln"], 1)
            act.wait_ge(s["r_ln"], c + 1)
            act.activation(r128, r128, ACT.Exp, scale=-0.5).then_inc(s["r_r"], 1)

        def dve_rms(dve, c, src, gain):
            dve.wait_ge(s["r_r"], c + 1)
            dve.scalar_tensor_tensor(src, src, gains[:, gain:gain + 1], r128, ALU.mult, ALU.mult).then_inc(s["r_y"], 1)

        def pe_rope(pe, c, src, swap):
            if not (isinstance(c, int) and c == 0):
                pe.wait_ge(s["rp_ss"], c)
            pe.matmul(b[5][:], swap[:], src, start=True, stop=True).then_inc(s["rp_ps"], 1)

        def pool_rope(pool, c, src, cos):
            if not (isinstance(c, int) and c == 0):
                pool.wait_ge(s["rp_out"], c)
            pool.tensor_tensor(rp_c, src, cos, ALU.mult).then_inc(s["rp_cc"], 1)

        def dve_rope(dve, c, src, sin):
            if not (isinstance(c, int) and c == 0):
                dve.wait_ge(s["rp_out"], c)
            dve.wait_ge(s["rp_ps"], c + 1)
            dve.tensor_tensor(rp_s, b[5][:], sin, ALU.mult).then_inc(s["rp_ss"], 1)
            dve.wait_ge(s["rp_cc"], c + 1)
            dve.wait_ge(s["rp_ss"], c + 1)
            dve.tensor_tensor(src, rp_c, rp_s, ALU.add).then_inc(s["rp_out"], 1)

        idx_ropes = [(0, ik)] + [(1 + j, iqs[:, j]) for j in range(4)]

        def pe_in1(pe):
            for u in range(10):
                pe_panel(pe, Panel(N_IN1, 0, 0, u), h_hi, h_lo, s["h_ready"] if u == 0 else None, 2 * KT)
                if u == 1:
                    pe.wait_ge(s["in1"], 1)
                    for tt in range(TT):
                        last = pe.transpose(b[0][:, tt * P:(tt + 1) * P], small[:, tt * P:(tt + 1) * P], ident[:])
                    last.then_inc(s["wt_ps"], 1)
            pe.wait_ge(s["z_gb"], 2)
            pe.wait_ge(s["z_b"], 2)
            for tt in range(TT):
                last = pe.transpose(b[1][:, tt * 40:(tt + 1) * 40], gb[0:40, tt * P:(tt + 1) * P], ident[0:40, 0:40])
            last.then_inc(s["gbt_ps"], 1)
            pe.wait_ge(s["t_in"], 16 * 7)
            pe.wait_ge(s["consts_in"], 48)
            pe.wait_ge(s["in1"], 6)
            for c, src in idx_ropes:
                pe_rope(pe, c, src, swap_i)
            for i in range(2):
                pe_rms(pe, i, b[4])
            for i in range(2):
                pe.wait_ge(s["r_y"], i + 1)
                pe_rope(pe, 5 + i, ak[:, i], swap_a)
            for i in range(2):
                pe.wait_ge(s["in1"], 9 + i)
                for tt in range(TT):
                    last = pe.transpose(b[2 + i][:, tt * P:(tt + 1) * P], av[:, i, tt * P:(tt + 1) * P], ident[:])
                last.then_inc(s["av_ps"], 1)
            pe.wait_ge(s["wt_sb"], 1)
            pe.wait_ge(s["rp_out"], 5)
            i = 0
            for q in range(1, TT):
                for hh in range(IDX_H):
                    if i >= 2:
                        pe.wait_ge(s["lg_r"], i - 1)
                    else:
                        pe.wait_ge(s["gbt_sb"], 1)
                    r = slice(IDX_D * (hh % 2), IDX_D * (hh % 2) + IDX_D)
                    pe.matmul(b[i % 2][:, 0:P * (q + 1)], iqs[r, hh // 2, q * P:(q + 1) * P], ik[r, 0:P * (q + 1)],
                              start=True, stop=True).then_inc(s["lg_ps"], 1)
                    pe_part(pe, Panel(N_IN1, 0, 0, 10 + i // 4), i % 4)
                    i += 1
            for u in range(10 + i // 4, 10 + ATT_H):
                pe_panel(pe, Panel(N_IN1, 0, 0, u), h_hi, h_lo)
            for h in range(ATT_H + 1):
                if h < ATT_H:
                    pe_panel(pe, Panel(N_IN1, 0, 0, 10 + ATT_H + h), h_hi, h_lo)
                if h >= 1:
                    pe.wait_ge(s["r_sq"], h + 2)
                    if h >= 3:
                        pe.wait_ge(s["r_ln"], h)
                    pe.matmul(b[4 + h % 2][:], ones[:], q_sq[:, h - 1], start=True, stop=True).then_inc(s["r_ss"], 1)

        def act_in1(act):
            dst = [small, ik] + [iqs[:, j] for j in range(4)] + [ak[:, 0], ak[:, 1], av[:, 0], av[:, 1]]
            for u in range(10):
                q = Panel(N_IN1, 0, 0, u)
                act_split(act, q.next())
                wait_panel(act, q)
                act.copy(dst[u], g_bank[q.par][:]).then_inc(s["in1"], 1)
                act.wait_ge(s["in1"], u + 1)
                act.sem_inc(bank_free[q.par], 1)
                if u == 1:
                    act.wait_ge(s["wt_ps"], 1)
                    act.mul(w_tok, tiles(b[0][:])[:, :, 64:64 + IDX_H], (IDX_H * IDX_D) ** -0.5).then_inc(s["wt_sb"], 1)
                    act.wait_ge(s["t_in"], 16 * 7)
                    g = gtmp[0:GDN_H, 0]
                    act.activation(g, small[0:GDN_H, :], ACT.Abs, bias=hp[0:GDN_H, 0:1]).then_inc(s["z_ga"], 1)
                    act.activation(hp[0:GDN_H, 2:3], hp[0:GDN_H, 1:2], ACT.Exp).then_inc(s["z_ea"], 1)
                    act.wait_ge(s["z_ga"], 1)
                    act.activation(g, g, ACT.Exp, scale=-1.0).then_inc(s["z_ge"], 1)
                    act.wait_ge(s["z_ge"], 1)
                    act.activation(g, g, ACT.Ln, bias=1.0).then_inc(s["z_gl"], 1)
                    act.wait_ge(s["z_b"], 1)
                    act.activation(gb[32:32 + GDN_H, :], small[32:32 + GDN_H, :], ACT.Tanh, scale=0.5).then_inc(s["z_gt"], 1)
            act.wait_ge(s["gbt_ps"], 1)
            act.copy(gb_tok, b[1][:, 0:TT * 40].rearrange("p (t c) -> p t c", t=TT)).then_inc(s["gbt_sb"], 1)
            for i in range(2):
                act_rms(act, i, ak[:, i], b[4])
            for i in range(2):
                act.wait_ge(s["av_ps"], i + 1)
                act.copy(v_key[i], tiles(b[2 + i][:])).then_inc(s["av_sb"], 1)
            for h in range(ATT_H):
                q = Panel(N_IN1, 0, 0, 10 + h)
                act_split(act, q.next())
                wait_panel(act, q)
                act.activation(o_att[:, h], g_bank[q.par][:], ACT.Tanh, scale=0.5).then_inc(s["gtb_in"], 1)
                act.wait_ge(s["gtb_in"], h + 1)
                act.sem_inc(bank_free[q.par], 1)
            for h in range(ATT_H + 1):
                if h < ATT_H:
                    q = Panel(N_IN1, 0, 0, 10 + ATT_H + h)
                    act_split(act, q.next())
                    wait_panel(act, q)
                    act.copy(q_all[:, h], g_bank[q.par][:]).then_inc(s["aq_in"], 1)
                    act.wait_ge(s["aq_in"], h + 1)
                    act.sem_inc(bank_free[q.par], 1)
                    act.activation(q_sq[:, h], q_all[:, h], ACT.Square).then_inc(s["r_sq"], 1)
                if h >= 1:
                    act.wait_ge(s["r_ss"], h + 2)
                    act.activation(q_sq[:, h - 1], b[4 + h % 2][:], ACT.Ln, scale=1.0 / P, bias=eps[:]).then_inc(s["r_ln"], 1)
            for h in range(ATT_H):
                act.wait_ge(s["r_ln"], h + 3)
                act.activation(q_sq[:, h], q_sq[:, h], ACT.Exp, scale=-0.5).then_inc(s["r_r"], 1)

        def dve_in1(dve):
            dve.memset(gb[0:64, :], 0.0).then_inc(s["z_b"], 1)
            for u in range(10):
                dve_split(dve, Panel(N_IN1, 0, 0, u).next())
                if u == 1:
                    g, m = gtmp[0:GDN_H, 0], gtmp[0:GDN_H, 1]
                    dve.wait_ge(s["in1"], 1)
                    dve.wait_ge(s["t_in"], 16 * 7)
                    dve.tensor_scalar(m, small[0:GDN_H, :], hp[0:GDN_H, 0:1], 0.0, ALU.add, ALU.max).then_inc(s["z_mx"], 1)
                    dve.wait_ge(s["z_mx"], 1)
                    dve.wait_ge(s["z_gl"], 1)
                    dve.tensor_tensor(m, m, g, ALU.add).then_inc(s["z_sp"], 1)
                    dve.wait_ge(s["z_sp"], 1)
                    dve.wait_ge(s["z_ea"], 1)
                    dve.tensor_scalar(m, m, hp[0:GDN_H, 2:3], -1.0, ALU.mult, ALU.mult).then_inc(s["z_g"], 1)
                    dve.wait_ge(s["z_g"], 1)
                    dve.wait_ge(s["z_b"], 1)
                    dve.tensor_tensor_scan(gb[0:GDN_H, :], keep2[0:GDN_H, :], m, 0.0, ALU.mult, ALU.add).then_inc(s["z_gb"], 1)
                    dve.wait_ge(s["z_gt"], 1)
                    bt = gb[32:32 + GDN_H, :]
                    dve.tensor_scalar(bt, bt, 1.0, 0.5, ALU.add, ALU.mult).then_inc(s["z_gb"], 1)
                    dve.sem_inc(s["z_b"], 1)
            for c, src in idx_ropes:
                dve_rope(dve, c, src, si)
            for i in range(2):
                dve_rms(dve, i, ak[:, i], G_KN)
            for i in range(2):
                dve_rope(dve, 5 + i, ak[:, i], sa)
            sco = [None, 0, 256, 640]
            dve.wait_ge(s["wt_sb"], 1)
            i = 0
            for q in range(1, TT):
                n = P * (q + 1)
                acc = sc[:, sco[q]:sco[q] + n]
                for hh in range(IDX_H):
                    dve.wait_ge(s["lg_ps"], i + 1)
                    w = w_tok[:, q, hh:hh + 1]
                    if hh == 0:
                        dve.tensor_scalar(acc, b[i % 2][:, 0:n], 0.0, w, ALU.max, ALU.mult).then_inc(s["lg_r"], 1)
                        dve.wait_ge(s["lg_r"], i + 1)
                        if i:
                            dve.wait_ge(s["lg_a"], i)
                        dve.sem_inc(s["lg_a"], 1)
                    else:
                        lgt = lg[:, i % 2, 0:n]
                        dve.tensor_scalar(lgt, b[i % 2][:, 0:n], 0.0, w, ALU.max, ALU.mult).then_inc(s["lg_r"], 1)
                        dve.wait_ge(s["lg_r"], i + 1)
                        dve.wait_ge(s["lg_a"], i)
                        dve.tensor_tensor(acc, acc, lgt, ALU.add).then_inc(s["lg_a"], 1)
                    i += 1
            dve.wait_ge(s["sc_m"], 3)
            with dve.Fori(0, TOPK // 8):
                for q in range(1, TT):
                    dve.max(out=top8[:, q - 1], in_=sc[:, sco[q]:sco[q] + P * (q + 1)])
                dve.drain()
                for q in range(1, TT):
                    acc = sc[:, sco[q]:sco[q] + P * (q + 1)]
                    dve.match_replace(out=acc, in_to_replace=top8[:, q - 1], in_values=acc, imm_value=TAKEN)
                dve.drain()
            for q in range(1, TT):
                n = P * (q + 1)
                dve.tensor_scalar(sel[:, off[q]:off[q] + n], sc[:, sco[q]:sco[q] + n], TAKEN, 1.0,
                                  ALU.is_equal, ALU.subtract).then_inc(s["sel_r"], 1)
            dve.wait_ge(s["sel_r"], 3)
            dve.wait_ge(s["zsel"], 2)

        def pool_in1(pool):
            pool.wait_ge(s["t_in"], 16 * 7)
            pool.wait_ge(s["in1"], 6)
            for c, src in idx_ropes:
                pool_rope(pool, c, src, ci)
            for i in range(2):
                pool.wait_ge(s["r_y"], i + 1)
                pool_rope(pool, 5 + i, ak[:, i], ca)
            pool.memset(sel[:, 0:P], 0.0).then_inc(s["zsel"], 1)
            pool.wait_ge(s["zsel"], 1)
            pool.affine_select(out=sel[:, 0:P], in_=sel[:, 0:P], compare_op=ALU.is_ge, fill=-1.0, base=0,
                               pattern=[[-1, P]], channel_multiplier=1).then_inc(s["zsel"], 1)
            sco = [None, 0, 256, 640]
            for q in range(1, TT):
                for u in range(3 * q + 8, min(3 * q + 11, 18)):
                    pool_split(pool, Panel(N_IN1, 0, 0, u))
                pool.wait_ge(s["lg_a"], IDX_H * q)
                d = sc[:, sco[q] + P * q:sco[q] + P * (q + 1)]
                pool.affine_select(out=d, in_=d, compare_op=ALU.is_ge, fill=NOT_CAUSAL, base=0,
                                   pattern=[[-1, P]], channel_multiplier=1).then_inc(s["sc_m"], 1)
            for u in range(18, 10 + 2 * ATT_H + 1):
                pool_split(pool, Panel(N_IN1, 0, 0, u))

        HPK = ATT_H // ATT_KV
        S_ORDER = (3, 1, 0, 2)
        s_at = {3: (b[0], 0), 1: (b[2], 0), 0: (b[1], 0), 2: (b[1], P)}
        K_ORDER = (0, 2, 3, 1)
        t_at = {0: (b[3], 0), 2: (g_bank[1], 0), 3: (g_bank[0], 0), 1: (g_bank[0], P)}

        def att_steps(eng, body):
            with eng.Fori(0, HPK - 1) as j:
                body(j, 0, True)
                body(j, 1, True)
            body(HPK - 1, 0, True)
            body(HPK - 1, 1, False)

        def pe_att(pe):
            def front(i, e):
                pe.wait_ge(s["r_y"], i + 3)
                pe_rope(pe, i + 7, aq[:, e], swap_a)
                pe.wait_ge(s["rp_out"], i + 8)
                for q in S_ORDER:
                    bk, o = s_at[q]
                    last = pe.matmul(bk[:, o:o + P * (q + 1)], aq[:, e, q * P:(q + 1) * P], ak[:, e, 0:P * (q + 1)],
                                     start=True, stop=True)
                    if q != 0:
                        last.then_inc(s["s_ps"], 1)

            def body(j, e, more):
                i = 2 * j + e
                if more:
                    pe.wait_ge(s["ms_r"], TT * i + TT)
                    front(i + 1, 1 - e)
                pe.wait_ge(s["pn_r"], TT * i + TT)
                for k in K_ORDER:
                    bk, o = t_at[k]
                    for q in range(k, TT):
                        last = pe.transpose(bk[:, o + (q - k) * P:o + (q - k + 1) * P],
                                            ms[e][:, off[q] + k * P:off[q] + (k + 1) * P], ident[:])
                    if k != 3:
                        last.then_inc(s["pt_ps"], 1)
                pe.wait_ge(s["att_done"], i + 1)
                for n, k in enumerate(K_ORDER):
                    pe.wait_ge(s["pt_sb"], TT * i + n + 1)
                    last = pe.matmul(b[4][:, k * P:SEQ], v_key[e][:, k, :], p_t[:, koff[k]:koff[k] + SEQ - k * P],
                                     start=(n == 0), stop=(n == TT - 1), skip_group_check=True)
                last.then_inc(s["pv_ps"], 1)

            front(0, 0)
            att_steps(pe, body)

        def act_att(act):
            def body(j, e, more):
                i = 2 * j + e
                act.wait_ge(s["nms"], i + 1)
                for q in S_ORDER:
                    m = ms[e][:, off[q]:off[q] + P * (q + 1)]
                    act.activation(m, m, ACT.Exp, scale=P ** -0.5, bias=n_max[:, 4 * e + q:4 * e + q + 1],
                                   accum_out=r_sum[:, q:q + 1]).then_inc(s["ex_a"], 1)
                for n, k in enumerate(K_ORDER):
                    act.wait_ge(s["pt_ps"], (TT - 1) * i + (1, 2, 3, 3)[n])
                    bk, o = t_at[k]
                    act.copy(p_t[:, koff[k]:koff[k] + SEQ - k * P], bk[:, o:o + SEQ - k * P]).then_inc(s["pt_sb"], 1)

            att_steps(act, body)

        def dve_att(dve):
            def queries(j, e):
                i, h = 2 * j + e, j + HPK * e
                dve.wait_ge(s["r_r"], i + 3)
                dve.wait_ge(s["r_r"], ATT_H + 2)
                dve.scalar_tensor_tensor(aq[:, e], q_all[:, bass.ds(h, 1)].rearrange("p a t -> p (a t)"),
                                         gains[:, G_QN:G_QN + 1], q_sq[:, bass.ds(h, 1)].rearrange("p a t -> p (a t)"),
                                         ALU.mult, ALU.mult).then_inc(s["r_y"], 1)

            def output(j, e):
                i, h = 2 * j + e, j + HPK * e
                dve.wait_ge(s["pv_ps"], i + 1)
                o = o_att[:, bass.ds(h, 1)].rearrange("p a t -> p (a t)")
                dve.scalar_tensor_tensor(o, o, 1.0, b[4][:], ALU.add, ALU.mult).then_inc(s["att_done"], 1)

            def scores(i, e):
                for n, q in enumerate(S_ORDER):
                    dve.wait_ge(s["s_ps"], (TT - 1) * i + (1, 2, 3, 3)[n])
                    w = P * (q + 1)
                    bk, o = s_at[q]
                    dve.scalar_tensor_tensor(ms[e][:, off[q]:off[q] + w], sel[:, off[q]:off[q] + w], BIG, bk[:, o:o + w],
                                             ALU.mult, ALU.add).then_inc(s["ms_r"], 1)
                for n, q in enumerate(S_ORDER):
                    dve.wait_ge(s["ms_r"], TT * i + n + 1)
                    dve.tensor_reduce(n_max[:, 4 * e + q:4 * e + q + 1], ms[e][:, off[q]:off[q] + P * (q + 1)], AX.X, ALU.max,
                                      negate=True).then_inc(s["nm_r"], 1)
                dve.wait_ge(s["nm_r"], TT * i + TT)
                nm = n_max[:, 4 * e:4 * e + 4]
                dve.tensor_scalar(nm, nm, P ** -0.5, None, ALU.mult).then_inc(s["nms"], 1)

            def body(j, e, more):
                i = 2 * j + e
                if more:
                    queries(j + e, 1 - e)
                    dve_rope(dve, i + 8, aq[:, 1 - e], sa)
                dve.wait_ge(s["ex_a"], TT * i + TT)
                dve.reciprocal(r_sum, r_sum).then_inc(s["rs_r"], 1)
                dve.wait_ge(s["rs_r"], i + 1)
                for q in S_ORDER:
                    m = ms[e][:, off[q]:off[q] + P * (q + 1)]
                    dve.tensor_scalar(m, m, r_sum[:, q:q + 1], None, ALU.mult).then_inc(s["pn_r"], 1)
                if more:
                    scores(i + 1, 1 - e)
                output(j, e)

            queries(0, 0)
            dve_rope(dve, 7, aq[:, 0], sa)
            scores(0, 0)
            att_steps(dve, body)

        def pool_att(pool):
            with pool.Fori(0, HPK) as j:
                for e in range(2):
                    i = 2 * j + e
                    pool.wait_ge(s["r_y"], i + 3)
                    pool_rope(pool, i + 7, aq[:, e], ca)

        at[0] = 0
        ub = take(SEQ + CONV)
        qkv = take(2 * 3, SEQ)
        tz = take(2, SEQ)
        zg = take(2, SEQ)
        kbe, q_dec = take(SEQ), take(SEQ)
        pick = take(2, P)
        gc_b, be_b, eg_b = take(SEQ), take(SEQ), take(SEQ)
        sq2 = take(2, SEQ)
        kb = take(SEQ)
        dec = take(TT, P)
        ek = take(SEQ)
        a_tr = take(TT, P)
        a_lv = take(2, SEQ)
        t_all = take(2 * TT, P)
        y_m = take(TT, P)
        rr = take(2, SEQ)
        vb_tok, kbe_tok = tiles(rr[:, 0]), tiles(rr[:, 1])
        kdec_tok = take(TT, P)
        u_m, w_t, v_new = take(TT, P), take(SEQ), take(TT, P)
        st = take(2, P)
        assert at[0] <= kept0, (at[0], kept0)
        o_sq, r_o, y_o = sq2[:, 0], rr[:, 0], sq2[:, 1]
        NT = 4 + 2 * (LEVELS - 1)

        def t_m(tt):
            return t_all[:, 4 * (tt // 2) + tt % 2, :]

        def t_t(tt):
            return t_all[:, 4 * (tt // 2) + 2 + tt % 2, :]

        cleared += gla_sems + gate_sems
        sems("c_chain oo_c ub0 c_in c_y c_s tz_t tz_d pick_r bc_ps bc_sb eg_r l_sq l_ss l_ln l_r l_y kb_r vb_r "
             "dm_a dm_b dm_c dec_r ek_a ek_b ek_c kk_ps kk_r qk_ps qk_r kbe_r qd_r tok_ps tok_sb al_r yy_ps y_sb2 "
             "z_ps t_r u_ps2 u_sb ws_ps vn_r kv_ps st2 oo_ps oo_sq oo_ss oo_ln oo_r oo_y1 oo_y2 oo_y3 oo_y4 oo_hi "
             "gdn_done", reuse=True)

        def sp_gdn(sp):
            w = rows(t["w_in_2"][0])
            with sp.Fori(0, GDN_H // 2) as hp2:
                for e in range(2):
                    for u, c in enumerate((QKV0, QKV0 + 1024, QKV0 + 2048, Z0, GTA0)):
                        load(sp, Panel(N_GDN, 10, hp2, 5 * e + u), [(w[:, :, bass.ds(c + P * e + 2 * P * hp2, P)], 0)])

        def gdn_heads(eng, body):
            with eng.Fori(0, GDN_H // 2 - 1) as hp2:
                body(hp2, 0, True)
                body(hp2, 1, True)
            body(GDN_H // 2 - 1, 0, True)
            body(GDN_H // 2 - 1, 1, False)

        def pe_bcast(pe, g, i, bk):
            pe.wait_ge(s["pick_r"], 2 * g + 2)
            pe.matmul(bk[:], pick[0:40, i], gb[0:40, :], start=True, stop=True).then_inc(s["bc_ps"], 1)

        def pe_l2(pe, g, i, bk):
            pe.wait_ge(s["l_sq"], 2 * g + i + 1)
            pe.matmul(bk[:], ones[:], sq2[:, i], start=True, stop=True).then_inc(s["l_ss"], 1)

        def pe_gdn(pe):
            for u in range(5):
                pe_panel(pe, Panel(N_GDN, 10, 0, u), h_hi, h_lo)
            pe_bcast(pe, 0, 0, b[5])
            pe_bcast(pe, 0, 1, b[4])
            pe_l2(pe, 0, 0, b[3])
            pe.wait_ge(s["bc_sb"], 2)
            pe_l2(pe, 0, 1, b[4])

            def body(hp2, e, front):
                h = 2 * hp2 + e

                def part(j):
                    if front:
                        pe_part(pe, Panel(N_GDN, 10, hp2, 5 * (e + 1) + j // 4), j % 4)

                def token_major(i, src, ready, bk):
                    pe.wait_ge(ready, h + 1)
                    for tt in range(TT):
                        c = slice(tt * P, (tt + 1) * P)
                        last = pe.transpose(bk[:, c], src[:, c], ident[:])
                    last.then_inc(s["tok_ps"], 1)

                kn, qn, vn = qkv[:, 3 * e + 1], qkv[:, 3 * e], qkv[:, 3 * e + 2]
                pe.wait_ge(s["kb_r"], h + 1)
                for bk, rhs, done in ((b[4], kb, s["kk_ps"]), (b[5], qn, s["qk_ps"])):
                    if rhs is qn:
                        pe.wait_ge(s["l_y"], 2 * h + 2)
                    for tt in range(TT):
                        c = slice(tt * P, (tt + 1) * P)
                        last = pe.matmul(bk[:, c], kn[:, c], rhs[:, c], start=True, stop=True)
                    last.then_inc(done, 1)
                part(0)
                part(1)
                part(2)
                part(3)
                pe.wait_ge(s["oo_ln"], h + 1)
                for lv in range(LEVELS):
                    pe.wait_ge(s["al_r"], LEVELS * h + lv + 1)
                    al = a_lv[:, lv % 2]
                    for f in range(2):
                        bk = b[2 * f]
                        if lv >= 1:
                            pe.wait_ge(s["t_r"], NT * h + (3 if lv == 1 else 4 + 2 * (lv - 2) + 1) + f)
                        for i in range(2):
                            c = slice((2 * f + i) * P, (2 * f + i + 1) * P)
                            o = bk[:, i * P:(i + 1) * P]
                            if lv == 0:
                                last = pe.transpose(o, al[:, c], ident[:])
                            else:
                                last = pe.matmul(o, al[:, c], t_m(2 * f + i), start=True, stop=True)
                        last.then_inc(s["yy_ps"], 1)
                    if lv == 0:
                        pe.wait_ge(s["kk_r"], h + 1)
                        token_major(0, vn, s["vb_r"], b[4])
                        continue
                    if lv < LEVELS - 1:
                        part(3 + lv)
                    for f in range(2):
                        pe.wait_ge(s["y_sb2"], 2 * (LEVELS - 1) * h + 2 * (lv - 1) + f + 1)
                        for side in ((0, 1) if lv < LEVELS - 1 else (1,)):
                            for i in range(2):
                                tt = 2 * f + i
                                o = b[2 * f + 1][:, (2 * side + i) * P:(2 * side + i + 1) * P]
                                if side == 0:
                                    last = pe.matmul(o, t_t(tt), y_m[:, tt, :], start=True, stop=True)
                                else:
                                    last = pe.matmul(o, y_m[:, tt, :], t_t(tt), start=True, stop=True)
                        last.then_inc(s["z_ps"], 1)
                    if lv == 1:
                        pe.wait_ge(s["qk_r"], h + 1)
                        token_major(1, kbe, s["kbe_r"], b[5])
                    if lv == 2:
                        pe.wait_ge(s["tok_sb"], 3 * h + 1)
                        token_major(2, ek, s["ek_c"], b[4])
                    if lv == 3 and front:
                        pe.wait_ge(s["tok_sb"], 3 * h + 2)
                        pe_bcast(pe, h + 1, 0, b[5])
                    if lv == 4 and front:
                        pe.wait_ge(s["tok_sb"], 3 * h + 3)
                        pe_bcast(pe, h + 1, 1, b[4])
                pe.wait_ge(s["tok_sb"], 3 * h + 3)
                if front:
                    pe.wait_ge(s["bc_sb"], 2 * h + 4)
                for f in range(2):
                    pe.wait_ge(s["t_r"], NT * (h + 1) - 1 + f)
                    for tt in (2 * f, 2 * f + 1):
                        c = slice(tt * P, (tt + 1) * P)
                        pe.matmul(b[2 * f + 1][:, c], t_t(tt), vb_tok[:, tt, :], start=True, stop=True)
                        last = pe.matmul(b[4][:, c], kbe_tok[:, tt, :], t_t(tt), start=True, stop=True)
                last.then_inc(s["u_ps2"], 1)
                for c in range(NCH):
                    r = slice(CHUNK * (c % 2), CHUNK * (c % 2) + CHUNK)
                    cc = slice(CHUNK * c, CHUNK * (c + 1))
                    if c:
                        pe.wait_ge(s["st2"], (NCH - 1) * h + c)
                        pe.matmul(b[5][r, 0:P], w_t[:, cc], st[:, c % 2], start=True, stop=True).then_inc(s["ws_ps"], 1)
                        if c == 1:
                            pe.wait_ge(s["qd_r"], h + 1)
                        pe.matmul(b[1 + c % 2][:, (c // 2) * P:(c // 2) * P + CHUNK], st[:, c % 2], q_dec[:, cc],
                                  start=True, stop=True, skip_group_check=True)
                    if c == 5 and front:
                        pe_l2(pe, h + 1, 0, b[3])
                    if c == 6 and front:
                        pe_l2(pe, h + 1, 1, b[4])
                    if c < NCH - 1:
                        pe.wait_ge(s["vn_r"], NCH * h + c + 1)
                        pe.matmul(b[0][:, 0:P], kdec_tok[r, c // 2, :], v_new[r, c // 2, :],
                                  start=True, stop=True).then_inc(s["kv_ps"], 1)
                    part(8 + c)
                pe.wait_ge(s["vn_r"], NCH * (h + 1))
                pe.wait_ge(s["qk_r"], h + 1)
                if front:
                    pe.wait_ge(s["l_ln"], 2 * h + 3)
                for tt in range(TT):
                    last = pe.matmul(b[3][:, tt * P:(tt + 1) * P], v_new[:, tt, :], dec[:, tt, :],
                                     start=True, stop=True)
                last.then_inc(s["oo_ps"], 1)
                for j in range(16, 20):
                    part(j)
                pe.wait_ge(s["oo_sq"], h + 1)
                pe.matmul(b[0][:], ones[:], o_sq, start=True, stop=True).then_inc(s["oo_ss"], 1)

            gdn_heads(pe, body)

        def act_conv_in(act, g, q, u):
            wait_panel(act, q)
            act.wait_ge(s["ub0"], 3 * g + u + 1)
            act.copy(ub[:, CONV - 1:CONV - 1 + SEQ], g_bank[q.par][:]).then_inc(s["c_in"], 1)
            act.wait_ge(s["c_in"], 3 * g + u + 1)
            act.sem_inc(bank_free[q.par], 1)

        def act_tanh(act, i, par, src):
            if not (isinstance(i, int) and i < 2):
                act.wait_ge(s["tz_d"], i - 1)
            act.activation(tz[:, par], src, ACT.Tanh, scale=0.5).then_inc(s["tz_t"], 1)

        def act_l2(act, g, banks):
            for i in range(2):
                act.wait_ge(s["l_ss"], 2 * g + i + 1)
                act.activation(rr[:, i], banks[i][:], ACT.Ln, scale=0.25, bias=eps[:]).then_inc(s["l_ln"], 1)
            for i in range(2):
                act.wait_ge(s["l_ln"], 2 * g + i + 1)
                act.activation(rr[:, i], rr[:, i], ACT.Exp, scale=-0.5).then_inc(s["l_r"], 1)

        def act_bcast(act, g, i, bk):
            act.wait_ge(s["bc_ps"], 2 * g + i + 1)
            act.copy(gc_b if i == 0 else be_b, bk[:]).then_inc(s["bc_sb"], 1)

        def act_gdn(act):
            for u in range(5):
                q = Panel(N_GDN, 10, 0, u)
                act_split(act, q.next())
                if u < 3:
                    act_conv_in(act, 0, q, u)
                    act.wait_ge(s["c_y"], u + 1)
                    act_tanh(act, u, u % 2, qkv[:, u])
                else:
                    wait_panel(act, q)
                    act_tanh(act, u, u % 2, g_bank[q.par][:])
            act_bcast(act, 0, 0, b[5])
            act_bcast(act, 0, 1, b[4])
            for i in range(2):
                act.wait_ge(s["c_s"], i + 1)
                act.activation(sq2[:, i], qkv[:, i], ACT.Square).then_inc(s["l_sq"], 1)
            act_l2(act, 0, (b[3], b[4]))
            act_decays(act, 0)
            act.wait_ge(s["ek_a"], 1)
            act.activation(ek, ek, ACT.Exp, scale=-1.0).then_inc(s["ek_b"], 1)
            act.sem_inc(s["oo_ln"], 1)

            def body(hp2, e, front):
                h = 2 * hp2 + e
                g = h + 1
                o = 3 * (1 - e)

                def q(u):
                    return Panel(N_GDN, 10, hp2, 5 * (e + 1) + u)

                def tanh(u, src):
                    act_tanh(act, 10 * hp2 + 5 * (e + 1) + u, (e + 1 + u) % 2, src)

                def tok(i):
                    act.wait_ge(s["tok_ps"], 3 * h + i + 1)
                    act.copy((vb_tok, kbe_tok, kdec_tok)[i], tiles(b[(4, 5, 4)[i]][:])).then_inc(s["tok_sb"], 1)

                def level(lv):
                    for f in range(2):
                        act.wait_ge(s["yy_ps"], 2 * LEVELS * h + 2 * lv + f + 1)
                        act.copy(y_m[:, 2 * f:2 * f + 2], b[2 * f][:, 0:2 * P].rearrange("p (t c) -> p t c", t=2)
                                 ).then_inc(s["y_sb2"], 1)

                if front:
                    act_split(act, q(1))
                    act_conv_in(act, g, q(0), 0)
                level(1)
                tok(0)
                level(2)
                tok(1)
                if front:
                    act_split(act, q(2))
                level(3)
                tok(2)
                if front:
                    act.wait_ge(s["c_y"], 3 * g + 1)
                    tanh(0, qkv[:, o])
                level(4)
                if front:
                    act_bcast(act, g, 0, b[5])
                level(5)
                if front:
                    act_bcast(act, g, 1, b[4])
                    act_conv_in(act, g, q(1), 1)
                act.wait_ge(s["u_ps2"], h + 1)
                for f in range(2):
                    act.copy(u_m[:, 2 * f:2 * f + 2], tiles(b[2 * f + 1][:])[:, 2 * f:2 * f + 2]).then_inc(s["u_sb"], 1)
                act.copy(w_t, b[4][:]).then_inc(s["u_sb"], 1)
                if front:
                    act_split(act, q(3))
                    act.wait_ge(s["c_s"], 3 * g + 1)
                    act.activation(sq2[:, 0], qkv[:, o], ACT.Square).then_inc(s["l_sq"], 1)
                    act.wait_ge(s["c_y"], 3 * g + 2)
                    tanh(1, qkv[:, o + 1])
                    act.wait_ge(s["c_s"], 3 * g + 2)
                    act.activation(sq2[:, 1], qkv[:, o + 1], ACT.Square).then_inc(s["l_sq"], 1)
                    act_conv_in(act, g, q(2), 2)
                    act_split(act, q(4))
                    act_l2(act, g, (b[3], b[4]))
                    act.wait_ge(s["c_y"], 3 * g + 3)
                    tanh(2, qkv[:, o + 2])
                    act.wait_ge(s["st2"], (NCH - 1) * (h + 1))
                    act_decays(act, g)
                    act_split(act, q(5))
                    wait_panel(act, q(3))
                    tanh(3, g_bank[q(3).par][:])
                act.wait_ge(s["oo_y1"], h + 1)
                act.activation(o_sq, y_m.rearrange("p t c -> p (t c)"), ACT.Square).then_inc(s["oo_sq"], 1)
                if front:
                    act.wait_ge(s["ek_a"], g + 1)
                    act.activation(ek, ek, ACT.Exp, scale=-1.0).then_inc(s["ek_b"], 1)
                act.wait_ge(s["oo_ss"], h + 1)
                act.activation(r_o, b[0][:], ACT.Ln, scale=1.0 / P, bias=eps[:]).then_inc(s["oo_ln"], 1)
                act.wait_ge(s["oo_ln"], h + 2)
                act.activation(r_o, r_o, ACT.Exp, scale=-0.5).then_inc(s["oo_r"], 1)
                if front:
                    wait_panel(act, q(4))
                    tanh(4, g_bank[q(4).par][:])
                act.wait_ge(s["oo_y4"], h + 1)
                act.mul(m_hi[:, bass.ds(h, 1)].rearrange("p a t -> p (a t)"), y_o, 0.5).then_inc(s["oo_hi"], 1)

            gdn_heads(act, body)

        def act_decays(act, g):
            act.wait_ge(s["dm_b"], g + 1)
            act.activation(dec, dec, ACT.Exp).then_inc(s["dm_c"], 1)
            act.activation(eg_b, gc_b, ACT.Exp).then_inc(s["eg_r"], 1)

        def dve_gdn(dve):
            dve.memset(ub[:, 0:CONV - 1], 0.0).then_inc(s["memsets"], 1)
            dve.sem_inc(s["ub0"], 1)
            dve.sem_inc(s["gdn_done"], 1)
            dve.wait_ge(s["memsets"], 4)

            def head(hp2, e):
                g = 2 * hp2 + e
                o = 3 * (e % 2)

                def picks():
                    for i in range(2):
                        dve.tensor_copy(pick[0:40, i], ident[0:40, bass.ds(32 * i + g, 1)].broadcast_to([40, P])
                                        ).then_inc(s["pick_r"], 1)

                def conv(u, steps):
                    y = qkv[:, o + u]
                    for jj in steps:
                        w = conv_w[:, bass.ds(jj * 24 + u * 8 + g, 1)]
                        if jj == 0:
                            dve.wait_ge(s["c_in"], 3 * g + u + 1)
                            dve.tensor_scalar(y, ub[:, 0:SEQ], w, None, ALU.mult).then_inc(s["c_chain"], 1)
                        else:
                            dve.wait_ge(s["c_chain"], 9 * g + 3 * u + jj)
                            dve.scalar_tensor_tensor(y, ub[:, jj:jj + SEQ], w, y, ALU.mult, ALU.add
                                                     ).then_inc(s["c_chain"] if jj < CONV - 1 else s["c_y"], 1)
                        if jj == CONV - 1:
                            dve.wait_ge(s["c_y"], 3 * g + u + 1)
                            dve.sem_inc(s["ub0"], 1)

                def tanh_in(u):
                    i = 10 * hp2 + 5 * e + u
                    dve.wait_ge(s["tz_t"], i + 1)
                    return tz[:, (5 * e + u) % 2], i

                def silu(u):
                    y = qkv[:, o + u]
                    th, i = tanh_in(u)
                    dve.scalar_tensor_tensor(y, th, 1.0, y, ALU.add, ALU.mult).then_inc(s["c_s"], 1)
                    dve.wait_ge(s["c_s"], 3 * g + u + 1)
                    dve.sem_inc(s["tz_d"], 1)

                def gate_z(q):
                    th, i = tanh_in(3)
                    dve.scalar_tensor_tensor(zg[:, e % 2], th, 1.0, g_bank[q.par][:], ALU.add, ALU.mult).then_inc(s["tz_d"], 1)
                    dve.wait_ge(s["tz_d"], i + 1)
                    dve.sem_inc(bank_free[q.par], 1)

                def gate_a(q):
                    th, i = tanh_in(4)
                    dve.sem_inc(bank_free[q.par], 1)
                    dve.wait_ge(s["tz_d"], i)
                    dve.scalar_tensor_tensor(zg[:, e % 2], th, 1.0, zg[:, e % 2], ALU.add, ALU.mult).then_inc(s["tz_d"], 1)

                def decays():
                    dve.wait_ge(s["bc_sb"], 2 * g + 2)
                    g_tok = gb_tok[:, :, bass.ds(g, 1)].broadcast_to([P, TT, P])
                    dve.tensor_tensor(dec, tiles(gc_b), g_tok, ALU.subtract).then_inc(s["dm_a"], 1)
                    dve.wait_ge(s["dm_a"], g + 1)
                    dve.tensor_scalar(dec, dec, 0.0, None, ALU.min).then_inc(s["dm_b"], 1)

                def to_end():
                    ends = gc_b.rearrange("p (c t) -> p c t", t=CHUNK)
                    dve.tensor_tensor(ek.rearrange("p (c t) -> p c t", t=CHUNK), ends,
                                      ends[:, :, CHUNK - 1:CHUNK].broadcast_to([P, NCH, CHUNK]), ALU.subtract).then_inc(s["ek_a"], 1)

                def l2(i):
                    f = (0.5 * P ** -0.5, 0.5)[i]
                    dve.wait_ge(s["l_r"], 2 * g + 2)
                    dve.scalar_tensor_tensor(qkv[:, o + i], qkv[:, o + i], f, rr[:, i], ALU.mult, ALU.mult).then_inc(s["l_y"], 1)

                def beta_k():
                    dve.wait_ge(s["l_y"], 2 * g + 1)
                    dve.tensor_tensor(kb, qkv[:, o + 1], be_b, ALU.mult).then_inc(s["kb_r"], 1)

                def beta_v():
                    dve.scalar_tensor_tensor(qkv[:, o + 2], qkv[:, o + 2], 0.5, be_b, ALU.mult, ALU.mult).then_inc(s["vb_r"], 1)

                return picks, conv, silu, gate_z, gate_a, decays, to_end, l2, beta_k, beta_v

            picks, conv, silu, gate_z, gate_a, decays, to_end, l2, beta_k, beta_v = head(0, 0)
            picks()
            dve.wait_ge(s["w_ready"], N_GDN + 3)
            for u in range(5):
                q0 = Panel(N_GDN, 10, 0, u)
                dve_split(dve, q0.next())
                if u < 3:
                    conv(u, range(CONV))
                    silu(u)
                elif u == 3:
                    gate_z(q0)
                else:
                    gate_a(q0)
            decays()
            to_end()
            l2(1)
            beta_k()
            l2(0)
            beta_v()

            def body(hp2, e, front):
                h = 2 * hp2 + e
                picks, conv, silu, gate_z, gate_a, decays, to_end, l2, beta_k, beta_v = head(hp2, e + 1)

                def q(u):
                    return Panel(N_GDN, 10, hp2, 5 * (e + 1) + u)

                if front:
                    dve_split(dve, q(1))
                dve.wait_ge(s["kk_ps"], h + 1)
                dve.wait_ge(s["dec_r"], h + 1)
                dve.tensor_tensor(a_tr, tiles(b[4][:]), dec, ALU.mult).then_inc(s["kk_r"], 1)
                dve.wait_ge(s["kk_r"], h + 1)
                dve.wait_ge(s["qk_ps"], h + 1)
                dve.tensor_tensor(dec, tiles(b[5][:]), dec, ALU.mult).then_inc(s["qk_r"], 1)
                eye = ident[:].unsqueeze(1).broadcast_to([P, 2, P])
                dve.wait_ge(s["al_r"], LEVELS * h + 1)
                for f in range(2):
                    dve.tensor_tensor(t_all[:, 4 * f + 2:4 * f + 4], eye, tiles(a_lv[:, 0])[:, 2 * f:2 * f + 2],
                                      ALU.subtract).then_inc(s["t_r"], 1)
                for f in range(2):
                    dve.wait_ge(s["yy_ps"], 2 * LEVELS * h + f + 1)
                    dve.tensor_tensor(t_all[:, 4 * f:4 * f + 2], eye, b[2 * f][:, 0:2 * P].rearrange("p (t c) -> p t c", t=2),
                                      ALU.subtract).then_inc(s["t_r"], 1)
                if front:
                    dve.wait_ge(s["bc_ps"], 2 * h + 2)
                    picks()
                    conv(0, (0,))
                for lv in range(1, LEVELS):
                    for f in range(2):
                        dve.wait_ge(s["z_ps"], 2 * (LEVELS - 1) * h + 2 * (lv - 1) + f + 1)
                        dve.wait_ge(s["t_r"], NT * h + 4 + 2 * (lv - 1) + (f if lv > 1 else 0))
                        o = 0 if lv < LEVELS - 1 else 2
                        dve.tensor_tensor(t_all[:, 4 * f + o:4 * f + 4], t_all[:, 4 * f + o:4 * f + 4],
                                          tiles(b[2 * f + 1][:])[:, o:], ALU.subtract).then_inc(s["t_r"], 1)
                    if front:
                        if lv < 4:
                            conv(0, (lv,))
                        if lv == 2:
                            dve_split(dve, q(2))
                        if lv == 4:
                            silu(0)
                dve.wait_ge(s["u_sb"], 3 * h + 3)
                for c in range(NCH):
                    r = slice(CHUNK * (c % 2), CHUNK * (c % 2) + CHUNK)
                    if c == 0:
                        dve.tensor_copy(v_new[r, 0], u_m[r, 0]).then_inc(s["vn_r"], 1)
                    else:
                        dve.wait_ge(s["ws_ps"], (NCH - 1) * h + c)
                        dve.tensor_tensor(v_new[r, c // 2], u_m[r, c // 2], b[5][r, 0:P], ALU.subtract).then_inc(s["vn_r"], 1)
                    if c < NCH - 1:
                        dve.wait_ge(s["kv_ps"], (NCH - 1) * h + c + 1)
                        e1 = CHUNK * (c + 1) - 1
                        if c == 0:
                            dve.tensor_copy(st[:, 1], b[0][:, 0:P]).then_inc(s["st2"], 1)
                        else:
                            dve.wait_ge(s["st2"], (NCH - 1) * h + c)
                            dve.scalar_tensor_tensor(st[:, (c + 1) % 2], st[:, c % 2], eg_b[:, e1:e1 + 1], b[0][:, 0:P],
                                                     ALU.mult, ALU.add).then_inc(s["st2"], 1)
                    if front:
                        if c < 2:
                            conv(1, (2 * c, 2 * c + 1))
                        elif c == 2:
                            dve_split(dve, q(3))
                        elif c == 3:
                            silu(1)
                        elif c == 4:
                            conv(2, (0, 1))
                        elif c == 5:
                            conv(2, (2, 3))
                        elif c == 6:
                            dve_split(dve, q(4))
                dve.wait_ge(s["oo_ps"], h + 1)
                if front:
                    decays()
                    l2(1)
                    beta_k()
                    l2(0)
                dve.tensor_copy(y_m, tiles(b[3][:])).then_inc(s["oo_c"], 1)
                dve.wait_ge(s["oo_c"], 3 * h + 1)
                yv = y_m.rearrange("p t (e c) -> p t e c", e=2)
                dve.tensor_tensor(yv[:, 1:, 0], yv[:, 1:, 0], tiles(b[1][:])[:, 1:, 0:CHUNK], ALU.add).then_inc(s["oo_c"], 1)
                dve.tensor_tensor(yv[:, :, 1], yv[:, :, 1], tiles(b[2][:])[:, :, 0:CHUNK], ALU.add).then_inc(s["oo_c"], 1)
                dve.wait_ge(s["oo_c"], 3 * h + 3)
                dve.sem_inc(s["oo_y1"], 1)
                if front:
                    to_end()
                    silu(2)
                    beta_v()
                dve.wait_ge(s["tz_d"], 10 * hp2 + 5 * e + 5)
                dve.scalar_tensor_tensor(y_o, y_m.rearrange("p t c -> p (t c)"), gains[:, G_GDN:G_GDN + 1], zg[:, e],
                                         ALU.mult, ALU.mult).then_inc(s["oo_y2"], 1)
                if front:
                    dve_split(dve, q(5))
                    gate_z(q(3))
                dve.wait_ge(s["oo_y2"], h + 1)
                dve.wait_ge(s["oo_r"], h + 1)
                dve.tensor_tensor(y_o, y_o, r_o, ALU.mult).then_inc(s["oo_y3"], 1)
                dve.wait_ge(s["oo_y3"], h + 1)
                dve.tensor_tensor(y_o, y_o, o_att[:, bass.ds(h, 1)].rearrange("p a t -> p (a t)"), ALU.add).then_inc(s["oo_y4"], 1)
                dve.wait_ge(s["oo_y4"], h + 1)
                if front:
                    gate_a(q(4))
                dve.wait_ge(s["oo_hi"], h + 1)
                dve.scalar_tensor_tensor(m_lo[:, bass.ds(h, 1)].rearrange("p a t -> p (a t)"), y_o, 0.5,
                                         m_hi[:, bass.ds(h, 1)].rearrange("p a t -> p (a t)").bitcast(F32),
                                         ALU.mult, ALU.subtract).then_inc(s["gdn_done"], 1)

            gdn_heads(dve, body)

        def pool_gdn(pool):
            with pool.Fori(0, GDN_H // 2) as hp2:
                for e in range(2):
                    h = 2 * hp2 + e
                    qn, kn = qkv[:, 3 * e], qkv[:, 3 * e + 1]
                    pool.wait_ge(s["dm_c"], h + 1)
                    pool.tensor_tensor(dec, dec, mask(LEVELS + 1), ALU.mult).then_inc(s["dec_r"], 1)
                    for lv in range(LEVELS):
                        pool.wait_ge(s["kk_r"], h + 1)
                        if lv >= 2:
                            pool.wait_ge(s["yy_ps"], 2 * LEVELS * h + 2 * lv - 2)
                            if lv == 2:
                                pool.wait_ge(s["t_r"], NT * h + 2)
                        pool.tensor_tensor(tiles(a_lv[:, lv % 2]), a_tr, mask(lv + 1), ALU.mult).then_inc(s["al_r"], 1)
                        if lv == 1:
                            pool.wait_ge(s["kb_r"], h + 1)
                            pool.wait_ge(s["eg_r"], h + 1)
                            pool.tensor_tensor(kbe, kb, eg_b, ALU.mult).then_inc(s["kbe_r"], 1)
                        if lv == 2:
                            pool.wait_ge(s["ek_b"], h + 1)
                            pool.wait_ge(s["l_y"], 2 * h + 2)
                            pool.tensor_tensor(ek, ek, kn, ALU.mult).then_inc(s["ek_c"], 1)
                    pool.tensor_tensor(q_dec, qn, eg_b, ALU.mult).then_inc(s["qd_r"], 1)

        at[0] = 0
        nb1 = norm_bufs()
        mlp_bufs = take(2, SEQ), take(2, SEQ)
        nm1 = Norm(G_FFN0, True)
        nmf = Norm(G_FINAL, False)
        nm2 = Norm(G_MIX1, True)
        nm3 = Norm(G_MLP1, True)
        y_tok = take(TT, D)

        block = ctx.enter_context(nc.Block())

        @block.sync
        def _(sp):
            sp_start(sp)
            sp_gla(sp)
            sp_panels(sp, N_WO0, rows(t["l0_w_out"]))
            sp_mlp(sp, N_FF0, t["l0_w_ff1"], t["l0_w_ff2"])
            sp_in1(sp)
            sp_gdn(sp)
            sp_panels(sp, N_WO1, rows(t["w_out_2"][0]))
            sp_mlp(sp, N_FF1, t["w_mlp_up_2"][0], t["w_mlp_down_2"][0])
            sp_out(sp, y_tok)

        @block.tensor
        def _(pe):
            pe_start(pe)
            pe.wait_ge(s["memsets"], 3)
            fence(pe, 1)
            pe_norm(pe, nm0, nb0)
            pe_gates(pe)
            pe_gla(pe)
            pe.wait_ge(s["gla_done"], GLA_H + 1)
            pe_wout(pe, N_WO0)
            fence(pe, 2)
            pe_norm(pe, nm1, nb1)
            pe_mlp(pe, N_FF0, 0, KT)
            fence(pe, 3)
            pe_norm(pe, nmf, nb1)
            fence(pe, 4)
            pe_norm(pe, nm2, nb2)
            pe_in1(pe)
            pe_att(pe)
            fence(pe, 5)
            pe_gdn(pe)
            pe.wait_ge(s["gdn_done"], GDN_H + 1)
            pe_wout(pe, N_WO1)
            fence(pe, 6)
            pe_norm(pe, nm3, nb1)
            pe_mlp(pe, N_FF1, 1, 3 * KT)
            fence(pe, 7)
            pe_out(pe, y_tok)

        @block.scalar
        def _(act):
            act_start(act)
            act_split(act, Panel(N_GK, 0, 0, 0))
            fence(act, 1)
            act_norm(act, nm0, nb0)
            act_gates(act)
            act_gla(act)
            act_wout(act, N_WO0)
            fence(act, 2)
            act_norm(act, nm1, nb1)
            act_mlp(act, N_FF0, 0, mlp_bufs, 0)
            fence(act, 3)
            act_norm(act, nmf, nb1)
            fence(act, 4)
            act_norm(act, nm2, nb2)
            act_in1(act)
            act_att(act)
            fence(act, 5)
            act_gdn(act)
            act_wout(act, N_WO1)
            fence(act, 6)
            act_norm(act, nm3, nb1)
            act_mlp(act, N_FF1, 1, mlp_bufs, 1)
            fence(act, 7)
            act_out(act, y_tok)

        @block.vector
        def _(dve):
            dve_start(dve)
            dve_split(dve, Panel(N_GK, 0, 0, 0))
            fence(dve, 1)
            dve_norm(dve, nm0, nb0)
            dve_gates(dve)
            dve_gla(dve)
            dve_wout(dve, N_WO0)
            fence(dve, 2)
            for done in gla_sems + gate_sems:
                dve.sem_clear(done)
            dve_norm(dve, nm1, nb1)
            dve.sem_inc(s["hid_ready"], 2)
            dve.sem_inc(s["down_done"], 1)
            dve_mlp(dve, N_FF0, 0, mlp_bufs, 0)
            fence(dve, 3)
            dve_norm(dve, nmf, nb1)
            fence(dve, 4)
            dve.sem_inc(s["att_done"], 1)
            dve_norm(dve, nm2, nb2)
            dve_in1(dve)
            dve_att(dve)
            fence(dve, 5)
            dve_gdn(dve)
            dve_wout(dve, N_WO1)
            fence(dve, 6)
            dve_norm(dve, nm3, nb1)
            dve_mlp(dve, N_FF1, 1, mlp_bufs, 1)
            fence(dve, 7)

        @block.gpsimd
        def _(pool):
            fence(pool, 1)
            pool_gla(pool)
            fence(pool, 2)
            fence(pool, 3)
            fence(pool, 4)
            pool_in1(pool)
            pool_att(pool)
            fence(pool, 5)
            pool_gdn(pool)
            fence(pool, 6)
            fence(pool, 7)


NAMES = ["x", "l0_norm_mix", "l0_w_in", "l0_w_gk_up", "l0_b_gk", "l0_g_onorm", "l0_w_out", "l0_norm_ffn",
         "l0_w_ff1", "l0_w_ff2", "final_norm", "norm_mix_g_2", "w_in_2", "conv_w_2", "a_log_2", "dt_bias_2",
         "gdn_norm_g_2", "q_norm_g_2", "k_norm_g_2", "w_out_2", "norm_mlp_g_2", "w_mlp_up_2", "w_mlp_down_2"]


def kernel(**inputs):
    import concourse.bacc as bacc
    from concourse.bass_utils import run_bass_kernel_spmd

    nc = bacc.Bacc("TRN2", target_bir_lowering=False, num_devices=1)
    arrays = {f"in_{n}": np.ascontiguousarray(inputs[n]) for n in NAMES}
    square, wide = host_constants()
    arrays["const_square"], arrays["const_wide"] = square, wide
    aps = {k: nc.dram_tensor(k, a.shape, mybir.dt.from_np(a.dtype), kind="ExternalInput").ap()
           for k, a in arrays.items()}
    out = nc.dram_tensor("out", (1, SEQ, D), F32, kind="ExternalOutput").ap()
    build(nc, {n: aps[f"in_{n}"] for n in NAMES}, out, aps["const_square"], aps["const_wide"])
    r = run_bass_kernel_spmd(nc, [arrays], core_ids=[0])
    return r.results[0]["out"]
```

```python
from contextlib import ExitStack

import numpy as np

import concourse.bass as bass
from concourse import mybir

F32 = mybir.dt.float32
F32R = mybir.dt.float32r
U32 = mybir.dt.uint32
ALU = mybir.AluOpType
ACT = mybir.ActivationFunctionType
AX = mybir.AxisListType

P = 128
SEQ, D, DFF = 512, 1024, 4096
KT = D // P
TT = SEQ // P
EPS = 1e-6
CHUNK = 64
NCH = SEQ // CHUNK
LEVELS = 6

GLA_H, GLA_K, GLA_V = 4, 128, 256
GLA_RANK = 16
GLA_GATE_NORM = 16.0
GLA_Q0, GLA_K0, GLA_V0, GLA_R0, GLA_G0 = 0, 512, 1024, 2048, 3072

GDN_H = 8
QKV0, Z0 = 0, 3072
GA0 = 4096
GB0 = GA0 + GDN_H
AQ0 = GB0 + GDN_H
AK0 = AQ0 + D
AV0 = AK0 + 256
IQ0 = AV0 + 256
IK0 = IQ0 + 512
IW0 = IK0 + 64
GTA0 = IW0 + 8
GTB0 = GTA0 + D
CONV = 4
ATT_H, ATT_KV = 8, 2
IDX_H, IDX_D = 8, 64
TOPK = min(256, SEQ // 4)
NOT_CAUSAL = -3.0e38
TAKEN = -3.4e38
BIG = 1.0e30

G_MIX0, G_FFN0, G_FINAL, G_MIX1, G_MLP1 = 0, 8, 16, 24, 32
G_BGK, G_ON, G_GDN, G_QN, G_KN = 40, 44, 46, 47, 48
N_GAIN = 49


def host_constants():
    j, i = np.meshgrid(np.arange(P), np.arange(P), indexing="ij")
    same = (j // CHUNK) == (i // CHUNK)
    masks = [(j == i)]
    for lv in range(LEVELS):
        s = 1 << lv
        masks.append((j // (2 * s) == i // (2 * s)) & (j % (2 * s) < s) & (i % (2 * s) >= s))
    masks.append(same & (j <= i))
    masks = np.stack(masks, 1).astype(np.float32)
    ident = np.eye(P, dtype=np.float32)

    def rope(seq, rot, width):
        inv = (np.float32(500000.0) ** (-np.arange(0, rot, 2, dtype=np.float32) / np.float32(rot))).astype(np.float32)
        ang = (np.arange(seq, dtype=np.float32)[:, None] * inv[None, :]).astype(np.float32)
        half = rot // 2
        c = np.ones((P, seq), np.float32)
        s = np.zeros((P, seq), np.float32)
        swap = np.zeros((P, P), np.float32)
        for b in range(0, P, width):
            for f in range(half):
                c[b + f] = c[b + half + f] = np.cos(ang[:, f])
                s[b + f] = s[b + half + f] = np.sin(ang[:, f])
                swap[b + half + f, b + f] = -1.0
                swap[b + f, b + half + f] = 1.0
        return c, s, swap

    ca, sa, pa = rope(SEQ, 32, P)
    ci, si, pi = rope(SEQ, 16, IDX_D)
    keep = np.ones((P, SEQ), np.float32)
    keep[:, ::CHUNK] = 0.0
    square = np.concatenate([ident, masks.reshape(P, -1), pa, pi], axis=1)
    wide = np.stack([ca, sa, ci, si, keep], 0)
    return square, wide


def build(nc, t, out, const_square, const_wide):
    with ExitStack() as ctx:
        def sb(name, shape, dt=F32):
            return ctx.enter_context(nc.sbuf_tensor(name, shape, dt))

        def sem(name):
            return ctx.enter_context(nc.semaphore(name))

        s = {}

        cleared = []

        def sems(names, reuse=False):
            got = []
            for name in names.split():
                s[name] = cleared.pop() if reuse and cleared else sem(name)
                got.append(s[name])
            return got

        raw = [sb(f"raw{b}", [P, KT, P]) for b in range(2)]
        w_hi = [sb(f"w_hi{b}", [P, KT, P], F32R) for b in range(2)]
        w_lo = [sb(f"w_lo{b}", [P, KT, P], F32R) for b in range(2)]
        h_hi, h_lo = sb("h_hi", [P, KT, SEQ], F32R), sb("h_lo", [P, KT, SEQ], F32R)
        with nc.sbuf_tensor("m_hi", [P, KT, SEQ], F32R) as m_hi, nc.sbuf_tensor("m_lo", [P, KT, SEQ], F32R) as m_lo:
            pass
        q_all, q_sq = sb("q_all", [P, KT, SEQ]), sb("q_sq", [P, KT, SEQ])
        x = sb("x", [P, KT, SEQ])
        ident = sb("ident", [P, P])
        masks = sb("masks", [P, LEVELS + 2, P])
        swap_a, swap_i = sb("swap_a", [P, P]), sb("swap_i", [P, P])
        ones = sb("ones", [P, P])
        gains = sb("gains", [P, N_GAIN])
        conv_w = sb("conv_w", [P, CONV * 3 * GDN_H])
        eps = sb("eps", [P, 1])
        arena = sb("arena", [P, 22400])
        at = [0]

        def take(*shape):
            n = int(np.prod(shape))
            v = arena[:, at[0]:at[0] + n]
            at[0] += n
            assert at[0] <= 22400, at[0]
            if len(shape) == 2:
                v = v.rearrange("p (a b) -> p a b", a=shape[0])
            if len(shape) == 3:
                v = v.rearrange("p (a b c) -> p a b c", a=shape[0], b=shape[1])
            return v

        bank = [ctx.enter_context(nc.psum_tensor(f"bank{i}", [P, SEQ], F32)) for i in range(8)]
        g_bank, b = bank[0:2], bank[2:8]

        def tiles(ap, n=TT):
            return ap.rearrange("p (t c) -> p t c", t=n)

        def mask(lv):
            return masks[:, lv, :].unsqueeze(1).broadcast_to([P, TT, P])

        sems("piece_in w_hi_ready w_ready phase_done x_in x_in1 x_in2 x_in3 params_in consts_in out_done")
        raw_in = [sem(f"raw_in{i}") for i in range(2)]
        mm_done = [sem(f"mm_done{i}") for i in range(2)]
        bank_free = [sem(f"bank_free{i}") for i in range(2)]
        pieces_sent = [0]

        class Panel:

            def __init__(self, base, per, h, u):
                self.par = (base + u) % 2
                self.n = base + u + per * h
                self.k = (base + u - self.par) // 2 + (per // 2) * h
                self.key = (base, per, h, u)

            def next(self):
                base, per, h, u = self.key
                return Panel(base, per, h, u + 1)

        def load(sp, q, pieces):
            sp.wait_ge(s["w_ready"], q.n + 1)
            for i, (src, c) in enumerate(pieces):
                if i == len(pieces) - 1:
                    if i:
                        sp.wait_ge(s["piece_in"], 16 * pieces_sent[0])
                    sp.dma_start(raw[q.par][:, :, c:c + src.shape[2]], src).then_inc(raw_in[q.par], 16)
                else:
                    sp.dma_start(raw[q.par][:, :, c:c + src.shape[2]], src).then_inc(s["piece_in"], 16)
                    pieces_sent[0] += 1

        def act_split(act, q):
            act.wait_ge(raw_in[q.par], 16 * (q.k + 1))
            act.wait_ge(mm_done[q.par], q.k + 1)
            act.copy(w_hi[q.par][:], raw[q.par][:]).then_inc(s["w_hi_ready"], 1)

        def dve_split(dve, q):
            dve.wait_ge(s["w_hi_ready"], q.n + 1)
            dve.tensor_tensor(w_lo[q.par][:], raw[q.par][:], w_hi[q.par][:].bitcast(F32),
                              ALU.subtract).then_inc(s["w_ready"], 1)

        def pool_split(pool, q):
            pool.wait_ge(s["w_ready"], q.n + 2)
            pool.wait_ge(s["w_hi_ready"], q.n + 1)
            pool.tensor_tensor(w_lo[q.par][:], raw[q.par][:], w_hi[q.par][:].bitcast(F32),
                               ALU.subtract).then_inc(s["w_ready"], 1)

        def pe_panel(pe, q, hi, lo, ready=None, count=0):
            pe.wait_ge(s["w_ready"], q.n + 3)
            pe.wait_ge(bank_free[q.par], q.k + 1)
            for k in range(KT):
                if ready is not None:
                    pe.wait_ge(ready, count + k + 1)
                pe.matmul(g_bank[q.par][:], w_hi[q.par][:, k], hi[:, k], start=(k == 0), stop=False)
                pe.matmul(g_bank[q.par][:], w_hi[q.par][:, k], lo[:, k], start=False, stop=False)
                last = pe.matmul(g_bank[q.par][:], w_lo[q.par][:, k], hi[:, k], start=False, stop=(k == KT - 1))
            last.then_inc(mm_done[q.par], 1)

        def wait_panel(eng, q):
            eng.wait_ge(mm_done[q.par], q.k + 2)

        N_GK = 0
        N_GLA = 1
        N_WO0 = N_GLA + 6 * GLA_H
        N_FF0 = N_WO0 + KT
        GROUPS = DFF // D
        N_IN1 = N_FF0 + 16 * GROUPS
        N_GDN = N_IN1 + 10 + 2 * ATT_H
        N_WO1 = N_GDN + 5 * GDN_H
        N_FF1 = N_WO1 + KT
        N_END = N_FF1 + 16 * GROUPS

        def rows(w):
            return w.rearrange("(k p) c -> p k c", p=P)

        def fence(eng, p):
            eng.drain().then_inc(s["phase_done"], 1)
            eng.wait_ge(s["phase_done"], 4 * p)

        at[0] = 0
        x_tok = take(TT, D)
        par_rows = take(2, P)
        x_sq, x_acc = take(2, SEQ), take(SEQ)
        sems("x_t x_s memsets par_t par_s n_sq n_acc n_ss n_ln n_r n_h n_hi h_ready")

        def sp_start(sp):
            gain_rows = [("l0_norm_mix", G_MIX0, 8), ("l0_norm_ffn", G_FFN0, 8), ("final_norm", G_FINAL, 8),
                         ("norm_mix_g_2", G_MIX1, 8), ("norm_mlp_g_2", G_MLP1, 8), ("l0_b_gk", G_BGK, 4),
                         ("l0_g_onorm", G_ON, 2), ("gdn_norm_g_2", G_GDN, 1), ("q_norm_g_2", G_QN, 1),
                         ("k_norm_g_2", G_KN, 1)]
            xv = t["x"].rearrange("b (t p) d -> p (b t) d", p=P)
            sp.dma_start(ident[:], const_square[:, 0:P]).then_inc(s["x_in"], 16)
            for i in range(4):
                sp.dma_start(x_tok[:, :, 2 * P * i:2 * P * (i + 1)], xv[:, :, 2 * P * i:2 * P * (i + 1)]
                             ).then_inc(s["x_in" if i == 0 else f"x_in{i}"], 16)
            for name, r, n in gain_rows:
                a = t[name]
                if len(a.shape) == 2:
                    a = a.rearrange("a d -> (a d)")
                sp.dma_start(par_rows[r:r + n, 0, :], a.rearrange("(k p) -> k p", p=P)).then_inc(s["params_in"], 16)
            sp.dma_start(par_rows[0:CONV * 24, 1, :],
                         t["conv_w_2"].rearrange("a j (c p) -> (a j c) p", p=P)).then_inc(s["params_in"], 16)
            load(sp, Panel(N_GK, 0, 0, 0), [(rows(t["l0_w_in"])[:, :, GLA_G0:GLA_G0 + 16], 0),
                                            (rows(t["l0_w_in"])[:, :, 0:P - 16], 16)])
            c0 = P
            sp.dma_start(masks[:], const_square[:, c0:c0 + 8 * P].rearrange("p (l c) -> p l c", c=P)).then_inc(s["consts_in"], 16)
            sp.dma_start(swap_a[:], const_square[:, c0 + 8 * P:c0 + 9 * P]).then_inc(s["consts_in"], 16)
            sp.dma_start(swap_i[:], const_square[:, c0 + 9 * P:c0 + 10 * P]).then_inc(s["consts_in"], 16)

        PARAM_DMAS = 11

        def pe_start(pe):
            pe.sem_inc(mm_done[0], 1)
            pe.sem_inc(mm_done[1], 1)
            pe.wait_ge(s["x_in"], 32)
            for k in range(KT):
                if k in (2, 4, 6):
                    pe.wait_ge(s[f"x_in{k // 2}"], 16)
                if k >= 2:
                    pe.wait_ge(s["x_s"], k - 1)
                for tt in range(TT):
                    last = pe.transpose(b[k % 2][:, tt * P:(tt + 1) * P], x_tok[:, tt, k * P:(k + 1) * P], ident[:])
                last.then_inc(s["x_t"], 1)
            pe.wait_ge(s["params_in"], 16 * PARAM_DMAS)
            pe.transpose(b[2][:, 0:N_GAIN], par_rows[0:N_GAIN, 0, :], ident[0:N_GAIN, 0:N_GAIN]).then_inc(s["par_t"], 1)
            n = CONV * 24
            pe.transpose(b[3][:, 0:n], par_rows[0:n, 1, :], ident[0:n, 0:n]).then_inc(s["par_t"], 1)

        def act_start(act):
            for k in range(KT):
                act.wait_ge(s["x_t"], k + 1)
                act.copy(x[:, k], b[k % 2][:]).then_inc(s["x_s"], 1)
                act.wait_ge(s["x_s"], k + 1)
                if k >= 2:
                    act.wait_ge(s["n_acc"], k - 1)
                act.activation(x_sq[:, k % 2], x[:, k], ACT.Square).then_inc(s["n_sq"], 1)
            act.wait_ge(s["par_t"], 1)
            act.copy(gains[:], b[2][:, 0:N_GAIN]).then_inc(s["par_s"], 1)
            act.wait_ge(s["par_t"], 2)
            act.copy(conv_w[:], b[3][:, 0:CONV * 24]).then_inc(s["par_s"], 1)

        def dve_start(dve):
            dve.sem_inc(s["w_ready"], 2)
            dve.sem_inc(bank_free[0], 1)
            dve.sem_inc(bank_free[1], 1)
            dve.memset(ones[:], 1.0).then_inc(s["memsets"], 1)
            dve.memset(eps[:], EPS).then_inc(s["memsets"], 1)
            for k in range(KT):
                dve.wait_ge(s["n_sq"], k + 1)
                if k == 0:
                    dve.tensor_copy(x_acc, x_sq[:, 0]).then_inc(s["n_acc"], 1)
                else:
                    dve.wait_ge(s["n_acc"], k)
                    dve.tensor_tensor(x_acc, x_acc, x_sq[:, k % 2], ALU.add).then_inc(s["n_acc"], 1)
            dve.wait_ge(s["par_s"], 2)
            dve.tensor_scalar(gains[:, G_ON:G_ON + 3], gains[:, G_ON:G_ON + 3], 0.5, None, ALU.mult).then_inc(s["memsets"], 1)

        def act_norm(act):
            act.wait_ge(s["n_ss"], 1)
            act.activation(r_0, b[0][:], ACT.Ln, scale=1.0 / D, bias=eps[:]).then_inc(s["n_ln"], 1)
            act.wait_ge(s["n_ln"], 1)
            act.activation(r_0, r_0, ACT.Exp, scale=-0.5).then_inc(s["n_r"], 1)
            for k in range(KT):
                act.wait_ge(s["n_h"], k + 1)
                act.copy(h_hi[:, k], hb[:, k % 2]).then_inc(s["n_hi"], 1)

        def dve_norm(dve):
            def low(k):
                dve.wait_ge(s["n_hi"], k + 1)
                dve.tensor_tensor(h_lo[:, k], hb[:, k % 2], h_hi[:, k].bitcast(F32), ALU.subtract).then_inc(s["h_ready"], 1)

            dve.wait_ge(s["n_r"], 1)
            for k in range(KT):
                if k >= 2:
                    dve.wait_ge(s["h_ready"], k - 1)
                dve.scalar_tensor_tensor(hb[:, k % 2], x[:, k], gains[:, G_MIX0 + k:G_MIX0 + k + 1], r_0,
                                         ALU.mult, ALU.mult).then_inc(s["n_h"], 1)
                if k >= 1:
                    low(k - 1)
            low(KT - 1)

        def pe_norm(pe):
            pe.wait_ge(s["memsets"], 2)
            pe.wait_ge(s["x_s"], KT)
            pe.wait_ge(s["n_acc"], KT)
            pe.matmul(b[0][:], ones[:], x_acc, start=True, stop=True).then_inc(s["n_ss"], 1)

        at[0] = 0
        r_0, hb = take(SEQ), take(2, SEQ)
        at[0] = keep_at = 6 * SEQ
        keep = take(SEQ)
        gk_up = take(512)
        gk_low = take(SEQ)
        b_all = take(GLA_H, SEQ)
        head_in = take(6, SEQ)
        own, at[0] = at[0], 0
        head_in = [head_in, take(6, SEQ)]
        assert at[0] <= keep_at
        at[0] = own
        v_tok = take(TT, GLA_V)
        arg = take(2, SEQ)
        ex = take(2, SEQ)
        mlev = take(2, SEQ)
        sm = take(2, SEQ)
        a_t = take(TT, P)
        gt, gm = [mlev[:, 0], mlev[:, 1], sm[:, 0], sm[:, 1]], [arg[:, 0], arg[:, 1], ex[:, 0], ex[:, 1]]
        eb, qe, kd = take(SEQ), take(SEQ), take(SEQ)
        kd_tok = take(TT, P)
        state = take(NCH, GLA_V)
        osq = ex
        rb = take(SEQ)
        sems("gk_in")
        gate_sems = sems("gkl gk_ps ga ge gl gm gd gscan gbs")
        gla_sems = sems("q_in k_in v_in vt_ps vt_sb tg arg_r ab_r ex_r mlev_r slev at_r eb_r qe_r kd_r kdt_ps kdt_sb "
             "u_ps sm_r st_r o_ps osq_r osum on_ps oln or_r y1 y2 y_hi gla_done")

        def u_at(c):
            o = (c // 2 % 2) * GLA_V
            return b[2 + 2 * (c % 2) + c // 4][:, o:o + GLA_V]

        def sp_gla(sp):
            sp.wait_ge(s["phase_done"], 4)
            sp.dma_start(keep, const_wide[4]).then_inc(s["gk_in"], 16)
            sp.dma_start(gk_up[0:GLA_RANK, :], t["l0_w_gk_up"]).then_inc(s["gk_in"], 16)
            w = rows(t["l0_w_in"])
            with sp.Fori(0, GLA_H) as h:
                starts = [GLA_Q0 + P * h, GLA_K0 + P * h, GLA_V0 + 2 * P * h, GLA_V0 + P + 2 * P * h,
                          GLA_R0 + 2 * P * h, GLA_R0 + P + 2 * P * h]
                for u, c in enumerate(starts):
                    load(sp, Panel(N_GLA, 6, h, u), [(w[:, :, bass.ds(c, P)], 0)])

        def pe_gates(pe):
            pe_panel(pe, Panel(N_GK, 0, 0, 0), h_hi, h_lo, s["h_ready"], 0)
            pe.wait_ge(s["gk_in"], 32)
            pe.wait_ge(s["gkl"], 1)
            for h in range(GLA_H):
                pe.matmul(b[h][:], gk_up[0:GLA_RANK, h * P:(h + 1) * P], gk_low[0:GLA_RANK, :],
                          start=True, stop=True).then_inc(s["gk_ps"], 1)

        def act_gates(act):
            q = Panel(N_GK, 0, 0, 0)
            act_split(act, q.next())
            wait_panel(act, q)
            act.copy(gk_low[0:GLA_RANK, :], g_bank[q.par][0:GLA_RANK, :]).then_inc(s["gkl"], 1)
            for h in range(GLA_H):
                act.wait_ge(s["gk_ps"], h + 1)
                act.activation(gt[h], b[h][:], ACT.Abs, bias=gains[:, G_BGK + h:G_BGK + h + 1]).then_inc(s["ga"], 1)
            act_split(act, Panel(N_GLA, 12, 0, 1))
            for h in range(GLA_H):
                act.wait_ge(s["ga"], h + 1)
                act.activation(gt[h], gt[h], ACT.Exp, scale=-1.0).then_inc(s["ge"], 1)
            for h in range(GLA_H):
                act.wait_ge(s["ge"], h + 1)
                act.activation(gt[h], gt[h], ACT.Ln, bias=1.0).then_inc(s["gl"], 1)

        def dve_gates(dve):
            q = Panel(N_GK, 0, 0, 0)
            dve_split(dve, q.next())
            dve.wait_ge(s["gkl"], 1)
            dve.sem_inc(bank_free[q.par], 1)
            dve.wait_ge(s["gk_in"], 32)
            for h in range(GLA_H):
                dve.wait_ge(s["ga"], h + 1)
                dve.tensor_scalar(gm[h], b[h][:], gains[:, G_BGK + h:G_BGK + h + 1], 0.0,
                                  ALU.add, ALU.min).then_inc(s["gm"], 1)
            dve_split(dve, Panel(N_GLA, 12, 0, 1))
            for h in range(GLA_H):
                dve.wait_ge(s["gm"], h + 1)
                dve.wait_ge(s["gl"], h + 1)
                dve.tensor_tensor(gm[h], gm[h], gt[h], ALU.subtract).then_inc(s["gd"], 1)
                dve.wait_ge(s["gd"], h + 1)
                dve.tensor_tensor_scan(b_all[:, h], keep, gm[h], 0.0, ALU.mult, ALU.add).then_inc(s["gscan"], 1)
                dve.wait_ge(s["gscan"], h + 1)
                dve.tensor_scalar(b_all[:, h], b_all[:, h], 1.0 / GLA_GATE_NORM, None, ALU.mult).then_inc(s["gbs"], 1)
            dve.sem_inc(s["gla_done"], 1)

        NL = LEVELS + 1

        def gla_heads(eng, body):
            with eng.Fori(0, GLA_H // 2 - 1) as hp2:
                body(hp2, 0, True)
                body(hp2, 1, True)
            body(GLA_H // 2 - 1, 0, True)
            body(GLA_H // 2 - 1, 1, False)

        def pe_eighth(pe, q, k, hi=h_hi, lo=h_lo):
            if k == 0:
                pe.wait_ge(s["w_ready"], q.n + 3)
                pe.wait_ge(bank_free[q.par], q.k + 1)
            pe.matmul(g_bank[q.par][:], w_hi[q.par][:, k], hi[:, k], start=(k == 0), stop=False)
            pe.matmul(g_bank[q.par][:], w_hi[q.par][:, k], lo[:, k], start=False, stop=False)
            last = pe.matmul(g_bank[q.par][:], w_lo[q.par][:, k], hi[:, k], start=False, stop=(k == KT - 1))
            if k == KT - 1:
                last.then_inc(mm_done[q.par], 1)

        def pe_part(pe, q, i):
            pe_eighth(pe, q, 2 * i)
            pe_eighth(pe, q, 2 * i + 1)

        def pe_gla(pe):
            for u in range(6):
                pe_panel(pe, Panel(N_GLA, 12, 0, u), h_hi, h_lo)

            def body(hp2, e, front):
                h = 2 * hp2 + e
                qf, kf, vf = head_in[e][:, 0], head_in[e][:, 1], head_in[e][:, 2:4]

                def part(*js):
                    if front:
                        for j in js:
                            pe_part(pe, Panel(N_GLA, 12, hp2, 6 * (e + 1) + j // 4), j % 4)
                    else:
                        pe.wait_ge(s["gla_done"], GLA_H)
                        for j in js:
                            k = (j - 4) // 2
                            if 0 <= k < 2 * (GLA_H - 1):
                                pe_eighth(pe, Panel(N_WO0, 0, 0, j % 2), k, m_hi, m_lo)

                pe.wait_ge(s["q_in"], h + 1)
                pe.wait_ge(s["k_in"], h + 1)
                for tt in range(TT):
                    c = slice(tt * P, (tt + 1) * P)
                    last = pe.matmul(b[0][:, c], kf[:, c], qf[:, c], start=True, stop=True)
                last.then_inc(s["slev"], 1)
                pe.wait_ge(s["oln"], h + 1)
                for xh in range(2):
                    pe.wait_ge(s["v_in"], 2 * h + xh + 1)
                    for tt in range(TT):
                        last = pe.transpose(b[4 + xh][:, tt * P:(tt + 1) * P], vf[:, xh, tt * P:(tt + 1) * P], ident[:])
                    last.then_inc(s["vt_ps"], 1)
                part(0, 1, 2)
                for lv in range(LEVELS):
                    pe.wait_ge(s["mlev_r"], LEVELS * h + lv + 1)
                    if lv >= 1:
                        pe.wait_ge(s["at_r"] if lv == 1 else s["sm_r"], NL * h + 1 if lv == 1 else LEVELS * h + lv - 1)
                    for tt in range(TT):
                        c = slice(tt * P, (tt + 1) * P)
                        last = pe.matmul(b[(lv + 1) % 2][:, c], mlev[:, lv % 2, c], mlev[:, lv % 2, c],
                                         start=True, stop=True)
                    last.then_inc(s["slev"], 1)
                    part(*range(2 * lv + 3, 2 * lv + 5 - (lv == LEVELS - 1)))
                pe.wait_ge(s["kd_r"], h + 1)
                pe.wait_ge(s["y1"], 2 * h + 2)
                for tt in range(TT):
                    c = slice(tt * P, (tt + 1) * P)
                    last = pe.transpose(b[2][:, c], kd[:, c], ident[:])
                last.then_inc(s["kdt_ps"], 1)
                part(14, 15)
                pe.wait_ge(s["kdt_sb"], h + 1)
                pe.wait_ge(s["vt_sb"], 2 * h + 2)
                for c in range(NCH - 1):
                    r = slice(CHUNK * (c % 2), CHUNK * (c % 2) + CHUNK)
                    o = u_at(c)
                    last = pe.matmul(o, kd_tok[r, c // 2, :], v_tok[r, c // 2, :], start=True, stop=True)
                last.then_inc(s["u_ps"], 1)
                part(16, 17, 18, 19)
                pe.wait_ge(s["at_r"], NL * (h + 1))
                pe.wait_ge(s["st_r"], (NCH - 1) * (h + 1))
                pe.wait_ge(s["qe_r"], h + 1)
                for xh in range(2):
                    vc = slice(xh * P, (xh + 1) * P)
                    for tt in range(TT):
                        pe.matmul(b[2 + xh][:, tt * P:(tt + 1) * P], v_tok[:, tt, vc], a_t[:, tt, :],
                                  start=True, stop=False, skip_group_check=True)
                        for c in (2 * tt, 2 * tt + 1):
                            if c:
                                cc = slice(CHUNK * c, CHUNK * (c + 1))
                                last = pe.matmul(b[2 + xh][:, cc], state[:, c, vc], qe[:, cc],
                                                 start=False, stop=True, skip_group_check=True)
                    last.then_inc(s["o_ps"], 1)
                part(20, 21)
                pe.wait_ge(s["osum"], h + 1)
                pe.matmul(b[4][:], ones[:], osq[:, 0], start=True, stop=True).then_inc(s["on_ps"], 1)
                part(22, 23)

            gla_heads(pe, body)

        def act_gla(act):
            def q_evac(g, e, u, q):
                wait_panel(act, q)
                dst = head_in[e % 2]
                if u == 0:
                    act.mul(dst[:, 0], g_bank[q.par][:], GLA_K ** -0.5).then_inc(s["q_in"], 1)
                    act.wait_ge(s["q_in"], g + 1)
                    act.sem_inc(bank_free[q.par], 1)
                elif u == 1:
                    act.copy(dst[:, 1], g_bank[q.par][:]).then_inc(s["k_in"], 1)
                    act.wait_ge(s["k_in"], g + 1)
                    act.sem_inc(bank_free[q.par], 1)
                else:
                    act.activation(dst[:, u], g_bank[q.par][:], ACT.Tanh, scale=0.5).then_inc(s["tg"], 1)

            def decay(g, i):
                act.wait_ge(s["arg_r"], NL * g + i + 1)
                act.activation(arg[:, i % 2], arg[:, i % 2], ACT.Abs).then_inc(s["ab_r"], 1)
                act.wait_ge(s["ab_r"], NL * g + i + 1)
                if i == 2:
                    act.wait_ge(s["kd_r"], g + 1)
                if i >= 3:
                    act.wait_ge(s["mlev_r"], LEVELS * g + i - 2)
                act.activation(ex[:, i % 2], arg[:, i % 2], ACT.Exp, scale=-1.0).then_inc(s["ex_r"], 1)

            def to_start(g):
                act.activation(eb, b_all[:, bass.ds(g, 1)].rearrange("p a t -> p (a t)"), ACT.Exp).then_inc(s["eb_r"], 1)

            for u in range(6):
                q = Panel(N_GLA, 12, 0, u)
                if u:
                    act_split(act, q.next())
                if u < 2 or u >= 4:
                    q_evac(0, 0, u, q)
            to_start(0)
            decay(0, 0)
            decay(0, 1)
            act.sem_inc(s["oln"], 1)

            def body(hp2, e, front):
                h = 2 * hp2 + e
                yb = head_in[e][:, 2:4]

                def q(u):
                    return Panel(N_GLA, 12, hp2, 6 * (e + 1) + u)

                act_split(act, q(1))
                decay(h, 2)
                for xh in range(2):
                    act.wait_ge(s["vt_ps"], 2 * h + xh + 1)
                    act.copy(v_tok[:, :, xh * P:(xh + 1) * P], tiles(b[4 + xh][:])).then_inc(s["vt_sb"], 1)
                decay(h, 3)
                if front:
                    q_evac(h + 1, e + 1, 0, q(0))
                    act_split(act, q(2))
                decay(h, 4)
                decay(h, 5)
                if front:
                    q_evac(h + 1, e + 1, 1, q(1))
                    act_split(act, q(3))
                decay(h, 6)
                if front:
                    act_split(act, q(4))
                act.wait_ge(s["kdt_ps"], h + 1)
                act.copy(kd_tok, tiles(b[2][:])).then_inc(s["kdt_sb"], 1)
                if front:
                    act_split(act, q(5))
                    q_evac(h + 1, e + 1, 4, q(4))
                    act_split(act, q(6))
                for xh in range(2):
                    act.wait_ge(s["o_ps"], 2 * h + xh + 1)
                    act.activation(osq[:, xh], b[2 + xh][:], ACT.Square).then_inc(s["osq_r"], 1)
                act.wait_ge(s["on_ps"], h + 1)
                act.activation(rb, b[4][:], ACT.Ln, scale=1.0 / GLA_V, bias=eps[:]).then_inc(s["oln"], 1)
                act.wait_ge(s["oln"], h + 2)
                act.activation(rb, rb, ACT.Exp, scale=-0.5).then_inc(s["or_r"], 1)
                if front:
                    decay(h + 1, 0)
                    decay(h + 1, 1)
                    to_start(h + 1)
                    q_evac(h + 1, e + 1, 5, q(5))
                for xh in range(2):
                    act.wait_ge(s["y2"], 2 * h + xh + 1)
                    act.copy(m_hi[:, bass.ds(2 * h + xh, 1)].rearrange("p a t -> p (a t)"), yb[:, xh]).then_inc(s["y_hi"], 1)

            gla_heads(act, body)

        def dve_gla(dve):
            def evac(g, e, u, q):
                dst = head_in[e % 2][:, u]
                if u < 4:
                    wait_panel(dve, q)
                    dve.tensor_copy(dst, g_bank[q.par][:]).then_inc(s["v_in"], 1)
                    dve.wait_ge(s["v_in"], 2 * g + u - 1)
                    dve.sem_inc(bank_free[q.par], 1)
                else:
                    dve.wait_ge(s["tg"], 2 * g + u - 3)
                    dve.scalar_tensor_tensor(dst, dst, 1.0, g_bank[q.par][:], ALU.add, ALU.mult).then_inc(bank_free[q.par], 1)

            def exponent(g, i):
                bh = b_all[:, bass.ds(g, 1)].rearrange("p a t -> p (a t)")
                w, c = (CHUNK, CHUNK - 1) if i == 0 else (1 << i, (1 << i) // 2 - 1)
                v = bh.rearrange("p (c t) -> p c t", t=w)
                if i >= 2:
                    dve.wait_ge(s["ex_r"], NL * g + i - 1)
                dve.tensor_tensor(arg[:, i % 2].rearrange("p (c t) -> p c t", t=w), v,
                                  v[:, :, c:c + 1].broadcast_to([P, SEQ // w, w]), ALU.subtract).then_inc(s["arg_r"], 1)

            for u in range(6):
                q = Panel(N_GLA, 12, 0, u)
                if u:
                    dve_split(dve, q.next())
                if u == 0:
                    exponent(0, 0)
                    exponent(0, 1)
                if u >= 2:
                    evac(0, 0, u, q)

            def body(hp2, e, front):
                h = 2 * hp2 + e
                gate, yb = head_in[e][:, 4:6], head_in[e][:, 2:4]

                def q(u):
                    return Panel(N_GLA, 12, hp2, 6 * (e + 1) + u)

                exponent(h, 2)
                dve.wait_ge(s["slev"], NL * h + 1)
                dve.tensor_tensor(a_t, tiles(b[0][:]), mask(0), ALU.mult).then_inc(s["at_r"], 1)
                dve_split(dve, q(1))
                for lv in range(LEVELS):
                    if lv + 3 <= LEVELS:
                        exponent(h, lv + 3)
                    dve.wait_ge(s["slev"], NL * h + lv + 2)
                    if lv >= 2:
                        dve.wait_ge(s["at_r"], NL * h + lv)
                    dve.tensor_tensor(tiles(sm[:, lv % 2]), tiles(b[(lv + 1) % 2][:]), mask(lv + 1),
                                      ALU.mult).then_inc(s["sm_r"], 1)
                    if front and lv % 2 == 0:
                        dve_split(dve, q(2 + lv // 2))
                if front:
                    evac(h + 1, e + 1, 2, q(2))
                    dve_split(dve, q(5))
                    evac(h + 1, e + 1, 3, q(3))
                for c in range(NCH - 1):
                    dve.wait_ge(s["u_ps"], h + 1)
                    u = u_at(c)
                    if c == 0:
                        dve.wait_ge(s["eb_r"], h + 1)
                        dve.tensor_copy(state[:, 1], u).then_inc(s["st_r"], 1)
                    else:
                        dve.wait_ge(s["st_r"], (NCH - 1) * h + c)
                        e1 = CHUNK * (c + 1) - 1
                        dve.scalar_tensor_tensor(state[:, c + 1], state[:, c], eb[:, e1:e1 + 1], u,
                                                 ALU.mult, ALU.add).then_inc(s["st_r"], 1)
                if front:
                    evac(h + 1, e + 1, 4, q(4))
                    dve_split(dve, q(6))
                dve.wait_ge(s["osq_r"], 2 * h + 2)
                dve.tensor_tensor(osq[:, 0], osq[:, 0], osq[:, 1], ALU.add).then_inc(s["osum"], 1)
                for xh in range(2):
                    dve.scalar_tensor_tensor(yb[:, xh], b[2 + xh][:], gains[:, G_ON + xh:G_ON + xh + 1],
                                             gate[:, xh], ALU.mult, ALU.mult).then_inc(s["y1"], 1)
                if front:
                    exponent(h + 1, 0)
                    exponent(h + 1, 1)
                dve.wait_ge(s["or_r"], h + 1)
                dve.wait_ge(s["y1"], 2 * h + 4)
                for xh in range(2):
                    dve.tensor_tensor(yb[:, xh], yb[:, xh], rb, ALU.mult).then_inc(s["y2"], 1)
                if front:
                    evac(h + 1, e + 1, 5, q(5))
                for xh in range(2):
                    dve.wait_ge(s["y_hi"], 2 * h + xh + 1)
                    i = bass.ds(2 * h + xh, 1)
                    last = dve.tensor_tensor(m_lo[:, i].rearrange("p a t -> p (a t)"), yb[:, xh],
                                             m_hi[:, i].rearrange("p a t -> p (a t)").bitcast(F32), ALU.subtract)
                last.then_inc(s["gla_done"], 1)

            dve.sem_inc(s["y1"], 2)
            gla_heads(dve, body)

        def pool_gla(pool):
            with pool.Fori(0, GLA_H // 2) as hp2:
                for e in range(2):
                    h = 2 * hp2 + e
                    qf, kf = head_in[e][:, 0], head_in[e][:, 1]

                    def add(lv):
                        pool.wait_ge(s["sm_r"], LEVELS * h + lv + 1)
                        pool.wait_ge(s["at_r"], NL * h + lv + 1)
                        pool.tensor_tensor(a_t, a_t, tiles(sm[:, lv % 2]), ALU.add).then_inc(s["at_r"], 1)

                    pool.wait_ge(s["q_in"], h + 1)
                    pool.wait_ge(s["k_in"], h + 1)
                    pool.wait_ge(s["ex_r"], NL * h + 1)
                    pool.tensor_tensor(kd, kf, ex[:, 0], ALU.mult).then_inc(s["kd_r"], 1)
                    for lv in range(LEVELS):
                        w = 1 << lv
                        pool.wait_ge(s["ex_r"], NL * h + lv + 2)
                        if lv >= 2:
                            pool.wait_ge(s["slev"], NL * h + lv)

                        def half(ap, i):
                            return ap.rearrange("p (c i t) -> p c i t", i=2, t=w)[:, :, i, :]

                        ev = ex[:, (lv + 1) % 2]
                        pool.tensor_tensor(half(mlev[:, lv % 2], 0), half(kf, 0), half(ev, 0), ALU.mult)
                        pool.tensor_tensor(half(mlev[:, lv % 2], 1), half(qf, 1), half(ev, 1), ALU.mult).then_inc(s["mlev_r"], 1)
                        if lv >= 2:
                            add(lv - 2)
                    add(LEVELS - 2)
                    add(LEVELS - 1)
                    pool.wait_ge(s["eb_r"], h + 1)
                    pool.tensor_tensor(qe, qf, eb, ALU.mult).then_inc(s["qe_r"], 1)

        sems("w_sq w_acc w_ss w_ln w_r w_hi")

        def sp_panels(sp, base, w):
            with sp.Fori(0, KT // 2) as m:
                for u in range(2):
                    load(sp, Panel(base, 2, m, u), [(w[:, :, bass.ds(2 * P * m + P * u, P)], 0)])

        def pe_wout(pe, base, i, done):
            for u in range(2):
                for k in range(done, KT):
                    pe_eighth(pe, Panel(base, 0, 0, u), k, m_hi, m_lo)
            with pe.Fori(0, KT // 2 - 1) as m:
                for u in range(2):
                    pe_panel(pe, Panel(base + 2, 2, m, u), m_hi, m_lo)
            pe.wait_ge(s["w_acc"], KT * (i + 1))
            pe.matmul(b[0][:], ones[:], mlp_acc, start=True, stop=True).then_inc(s["w_ss"], 1)

        def act_wout(act, base, i, gain):
            for k in range(KT):
                q = Panel(base, 0, 0, k)
                if k:
                    act_split(act, q.next())
                act.wait_ge(bank_free[q.par], q.k + 2)
                act.activation(h_hi[:, k], x[:, k], ACT.Copy, scale=gains[:, gain + k:gain + k + 1]).then_inc(s["w_hi"], 1)
                if k >= 2:
                    act.wait_ge(s["w_acc"], KT * i + k - 1)
                act.activation(mlp_sq[:, k % 2], x[:, k], ACT.Square).then_inc(s["w_sq"], 1)
            act.wait_ge(s["w_ss"], i + 1)
            act.activation(r_sqr, b[0][:], ACT.Ln, scale=1.0 / D, bias=eps[:]).then_inc(s["w_ln"], 1)
            act.wait_ge(s["w_ln"], i + 1)
            act.activation(r_sqr, r_sqr, ACT.Exp, scale=-1.0).then_inc(s["w_r"], 1)

        def dve_wout(dve, base, i, gain):
            for k in range(KT):
                q = Panel(base, 0, 0, k)
                if k:
                    dve_split(dve, q.next())
                wait_panel(dve, q)
                dve.tensor_tensor(x[:, k], x[:, k], g_bank[q.par][:], ALU.add).then_inc(bank_free[q.par], 1)
                dve.wait_ge(s["w_hi"], KT * i + k + 1)
                dve.scalar_tensor_tensor(h_lo[:, k], x[:, k], gains[:, gain + k:gain + k + 1], h_hi[:, k].bitcast(F32),
                                         ALU.mult, ALU.subtract).then_inc(s["h_ready"], 1)
                dve.wait_ge(s["w_sq"], KT * i + k + 1)
                if k == 0:
                    dve.tensor_copy(mlp_acc, mlp_sq[:, 0]).then_inc(s["w_acc"], 1)
                else:
                    dve.wait_ge(s["w_acc"], KT * i + k)
                    dve.tensor_tensor(mlp_acc, mlp_acc, mlp_sq[:, k % 2], ALU.add).then_inc(s["w_acc"], 1)

        sems("rl sqr hid_hi hid_ready down_done dn x_fin f_sq f_acc f_ss f_ln f_r f_t f_x f_h f_hi y_ps y_sb")

        def sp_mlp(sp, base, w1, w2):
            with sp.Fori(0, GROUPS) as g:
                for u in range(8):
                    load(sp, Panel(base, 16, g, u), [(rows(w1)[:, :, bass.ds(D * g + P * u, P)], 0)])
                w2g = w2.rearrange("(g k p) c -> p (g k) c", p=P, k=KT)
                for u in range(8):
                    load(sp, Panel(base, 16, g, 8 + u), [(w2g[:, bass.ds(KT * g, KT), P * u:P * (u + 1)], 0)])

        def pe_mlp(pe, base, i, first):
            def group(g, last_mlp):
                for u in range(8):
                    pe_panel(pe, Panel(base, 16, g, u), h_hi, h_lo, s["h_ready"] if u == 0 else None, first)
                for u in range(8):
                    pe_panel(pe, Panel(base, 16, g, 8 + u), m_hi, m_lo, s["hid_ready"] if u == 0 else None,
                             KT * GROUPS * i + KT * g + 2)
                    if last_mlp and u >= 1:
                        pe_out(pe, u - 1)

            with pe.Fori(0, GROUPS - 1) as g:
                group(g, False)
            group(GROUPS - 1, i == 1)

        def act_mlp(act, base, i):
            n = KT * GROUPS * i

            def group(g, last):
                for u in range(16):
                    q = Panel(base, 16, g, u)
                    if not (last and i == 1 and u == 15):
                        act_split(act, q.next())
                    if u < 8:
                        wait_panel(act, q)
                        act.wait_ge(s["hid_ready"], n + KT * g + u + 1)
                        act.activation(rl[:, u % 2], g_bank[q.par][:], ACT.Relu).then_inc(s["rl"], 1)
                        if u == 0:
                            act.wait_ge(s["down_done"], GROUPS * i + g + 1)
                        act.wait_ge(s["sqr"], n + KT * g + u + 1)
                        act.copy(m_hi[:, u], sq[:, u % 2]).then_inc(s["hid_hi"], 1)
                    elif last and i == 0:
                        act_squares(act, u - 8)
                    elif last and u >= 9:
                        act_out(act, u - 9)

            with act.Fori(0, GROUPS - 1) as g:
                group(g, False)
            group(GROUPS - 1, True)

        def dve_mlp(dve, base, i):
            n = KT * GROUPS * i

            def group(g, last):
                for u in range(16):
                    q = Panel(base, 16, g, u)
                    if not (last and i == 1 and u == 15):
                        dve_split(dve, q.next())
                    if u < 8:
                        dve.wait_ge(s["rl"], n + KT * g + u + 1)
                        dve.tensor_tensor(sq[:, u % 2], rl[:, u % 2], rl[:, u % 2], ALU.mult).then_inc(s["sqr"], 1)
                        dve.sem_inc(bank_free[q.par], 1)
                        dve.wait_ge(s["sqr"], n + KT * g + u + 1)
                        dve.wait_ge(s["hid_hi"], n + KT * g + u + 1)
                        dve.tensor_tensor(m_lo[:, u], sq[:, u % 2], m_hi[:, u].bitcast(F32),
                                          ALU.subtract).then_inc(s["hid_ready"], 1)
                    else:
                        if u == 8:
                            dve.wait_ge(s["w_r"], i + 1)
                        wait_panel(dve, q)
                        dve.tensor_tensor(down[:, u % 2], g_bank[q.par][:], r_sqr, ALU.mult).then_inc(s["dn"], 1)
                        dve.wait_ge(s["dn"], n + KT * g + u - 7)
                        dve.sem_inc(bank_free[q.par], 1)
                        add = dve.tensor_tensor(x[:, u - 8], x[:, u - 8], down[:, u % 2], ALU.add)
                        if last:
                            add.then_inc(s["x_fin"], 1)
                dve.sem_inc(s["down_done"], 1)

            with dve.Fori(0, GROUPS - 1) as g:
                group(g, False)
            group(GROUPS - 1, True)

        def act_squares(act, k):
            act.wait_ge(s["x_fin"], k + 1)
            if k >= 2:
                act.wait_ge(s["f_acc"], 2 * k - 2)
            act.activation(f_sq[:, 2 * (k % 2)], x[:, k], ACT.Square).then_inc(s["f_sq"], 1)
            act.activation(f_sq[:, 2 * (k % 2) + 1], x[:, k], ACT.Square,
                           scale=gains[:, G_FINAL + k:G_FINAL + k + 1]).then_inc(s["f_sq"], 1)

        def pool_squares(pool):
            for k in range(KT):
                for j in range(2):
                    pool.wait_ge(s["f_sq"], 2 * k + j + 1)
                    if k == 0:
                        pool.tensor_copy(f_sum[:, j], f_sq[:, j]).then_inc(s["f_acc"], 1)
                    else:
                        pool.wait_ge(s["f_acc"], 2 * k + j - 1)
                        pool.tensor_tensor(f_sum[:, j], f_sum[:, j], f_sq[:, 2 * (k % 2) + j], ALU.add).then_inc(s["f_acc"], 1)

        def pe_two_norms(pe):
            for j in range(2):
                pe.wait_ge(s["f_acc"], 2 * KT - 1 + j)
                pe.matmul(b[j][:], ones[:], f_sum[:, j], start=True, stop=True).then_inc(s["f_ss"], 1)

        def act_two_norms(act):
            act.wait_ge(s["f_ss"], 1)
            act.activation(rf, b[0][:], ACT.Ln, scale=1.0 / D, bias=eps[:]).then_inc(s["f_ln"], 1)
            act.wait_ge(s["f_ln"], 1)
            act.activation(rf, rf, ACT.Exp, scale=-0.5).then_inc(s["f_r"], 1)
            act.wait_ge(s["f_t"], 2)
            act.activation(r1, r1, ACT.Ln, scale=1.0 / D, bias=eps[:]).then_inc(s["f_ln"], 1)
            act.wait_ge(s["f_ln"], 2)
            act.activation(r1, r1, ACT.Exp, scale=-0.5).then_inc(s["f_r"], 1)
            for k in range(KT):
                act.wait_ge(s["f_h"], k + 1)
                act.copy(h_hi[:, k], f_hb[:, k % 2]).then_inc(s["f_hi"], 1)

        def dve_two_norms(dve):
            dve.wait_ge(s["f_r"], 1)
            dve.wait_ge(s["f_ss"], 2)
            dve.tensor_tensor(r1, b[1][:], rf, ALU.mult).then_inc(s["f_t"], 1)
            dve.wait_ge(s["f_t"], 1)
            dve.tensor_tensor(r1, r1, rf, ALU.mult).then_inc(s["f_t"], 1)
            for k in range(KT):
                dve.scalar_tensor_tensor(x[:, k], x[:, k], gains[:, G_FINAL + k:G_FINAL + k + 1], rf,
                                         ALU.mult, ALU.mult).then_inc(s["f_x"], 1)
            dve.wait_ge(s["f_r"], 2)

            def low(k):
                dve.wait_ge(s["f_hi"], k + 1)
                dve.tensor_tensor(h_lo[:, k], f_hb[:, k % 2], h_hi[:, k].bitcast(F32), ALU.subtract).then_inc(s["h_ready"], 1)

            for k in range(KT):
                dve.wait_ge(s["f_x"], k + 1)
                if k >= 2:
                    dve.wait_ge(s["h_ready"], 2 * KT + k - 1)
                dve.scalar_tensor_tensor(f_hb[:, k % 2], x[:, k], gains[:, G_MIX1 + k:G_MIX1 + k + 1], r1,
                                         ALU.mult, ALU.mult).then_inc(s["f_h"], 1)
                if k >= 1:
                    low(k - 1)
            low(KT - 1)

        def pe_out(pe, k):
            pe.wait_ge(s["x_fin"], KT + k + 1)
            if k >= 2:
                pe.wait_ge(s["y_sb"], k - 1)
            for tt in range(TT):
                last = pe.transpose(b[2 + k % 2][:, tt * P:(tt + 1) * P], x[:, k, tt * P:(tt + 1) * P], ident[:])
            last.then_inc(s["y_ps"], 1)

        def act_out(act, k):
            act.wait_ge(s["y_ps"], k + 1)
            act.copy(y_tok[:, :, k * P:(k + 1) * P], tiles(b[2 + k % 2][:])).then_inc(s["y_sb"], 1)

        def sp_out(sp):
            ov = out.rearrange("b (t p) d -> p (b t) d", p=P)
            for k in range(KT):
                sp.wait_ge(s["y_sb"], k + 1)
                sp.dma_start(ov[:, :, k * P:(k + 1) * P], y_tok[:, :, k * P:(k + 1) * P]).then_inc(s["out_done"], 16)
            sp.wait_ge(s["out_done"], 16 * KT)

        at[0] = 22400 - (SEQ + TT * 40 + ATT_H * SEQ)
        kept0 = at[0]
        gb = take(SEQ)
        gb_tok = take(TT, 40)
        o_att = take(ATT_H, SEQ)

        at[0] = 0
        ca, sa = take(SEQ), take(SEQ)
        ci_si_keep = take(3 * SEQ)
        ci, si, keep2 = (ci_si_keep[:, i * SEQ:(i + 1) * SEQ] for i in range(3))
        ak = take(2, SEQ)
        ms = [None, ci_si_keep[:, 0:1280]]
        v_key = [take(TT, P) for _ in range(ATT_KV)]
        sel = take(1280)
        r0 = at[0]
        ms[0] = take(1280)
        p_t = take(1280)
        aq = take(2, SEQ)
        r_end, at[0] = at[0], r0
        iqs = take(4, SEQ)
        at[0] = r0
        norms0 = r0
        f_sq, f_sum = take(4, SEQ), take(2, SEQ)
        rf, r1, f_hb = take(SEQ), take(SEQ), take(2, SEQ)
        at[0] = r_end
        rp_c, rp_s = take(SEQ), take(SEQ)
        r128, sq128 = take(SEQ), take(SEQ)
        w_tok = take(TT, IDX_H)
        n_max, r_sum = take(2 * TT), take(TT)
        hp = take(4)
        small = take(SEQ)
        ik = take(SEQ)
        sc = take(1152)
        av = take(2, SEQ)
        gtmp = take(3, SEQ)
        lg = gtmp[:, 0:2]
        top8 = take(3, 8)
        assert at[0] <= kept0, (at[0], kept0)
        off = [0, 128, 384, 768]
        koff = [0, 512, 896, 1152]

        sems("t_in in1 z_ga z_ge z_gl z_gt z_mx z_sp z_g z_gb z_ea z_b wt_ps wt_sb gbt_ps gbt_sb "
             "r_sq r_ss r_ln r_r r_y rp_ps rp_cc rp_ss rp_out av_ps av_sb lg_ps lg_r lg_a sc_m sel_r zsel "
             "aq_in gtb_in s_ps ms_r nm_r nms ex_a rs_r pn_r pt_ps pt_sb pv_ps att_done")

        def sp_in1(sp):
            w = rows(t["w_in_2"][0])
            first = Panel(N_IN1, 0, 0, 0)
            load(sp, first, [(w[:, :, c:c + 32], d) for c, d in ((GA0, 0), (GB0, 32), (IW0, 64), (GTA0, 96))])
            load(sp, Panel(N_IN1, 0, 0, 1), [(w[:, :, IK0:IK0 + IDX_D], 0), (w[:, :, IK0:IK0 + IDX_D], IDX_D)])
            cols = [IQ0 + P * i for i in range(4)] + [AK0, AK0 + P, AV0, AV0 + P] + [c + P * i for c in (GTB0, AQ0) for i in range(ATT_H)]
            for i, c in enumerate(cols):
                load(sp, Panel(N_IN1, 0, 0, 2 + i), [(w[:, :, c:c + P], 0)])
                if i == 0:
                    sp.wait_ge(s["phase_done"], 12)
                    for j, dst in enumerate((ca, sa, ci, si, keep2)):
                        sp.dma_start(dst, const_wide[j]).then_inc(s["t_in"], 16)
                    for j, n in enumerate(("dt_bias_2", "a_log_2")):
                        sp.dma_start(hp[0:GDN_H, j:j + 1], t[n].rearrange("a d -> d a")).then_inc(s["t_in"], 16)

        def pe_rms(pe, c, bk):
            pe.wait_ge(s["r_sq"], c + 1)
            pe.matmul(bk[:], ones[:], sq128, start=True, stop=True).then_inc(s["r_ss"], 1)

        def act_rms(act, c, src, bk):
            if isinstance(c, int) and c == 0:
                pass
            else:
                act.wait_ge(s["r_ss"], c)
                act.wait_ge(s["r_y"], c)
            act.activation(sq128, src, ACT.Square).then_inc(s["r_sq"], 1)
            act.wait_ge(s["r_ss"], c + 1)
            act.activation(r128, bk[:], ACT.Ln, scale=1.0 / P, bias=eps[:]).then_inc(s["r_ln"], 1)
            act.wait_ge(s["r_ln"], c + 1)
            act.activation(r128, r128, ACT.Exp, scale=-0.5).then_inc(s["r_r"], 1)

        def dve_rms(dve, c, src, gain):
            dve.wait_ge(s["r_r"], c + 1)
            dve.scalar_tensor_tensor(src, src, gains[:, gain:gain + 1], r128, ALU.mult, ALU.mult).then_inc(s["r_y"], 1)

        def pe_rope(pe, c, src, swap):
            if not (isinstance(c, int) and c == 0):
                pe.wait_ge(s["rp_ss"], c)
            pe.matmul(b[5][:], swap[:], src, start=True, stop=True).then_inc(s["rp_ps"], 1)

        def pool_rope(pool, c, src, cos):
            if not (isinstance(c, int) and c == 0):
                pool.wait_ge(s["rp_out"], c)
            pool.tensor_tensor(rp_c, src, cos, ALU.mult).then_inc(s["rp_cc"], 1)

        def dve_rope(dve, c, src, sin):
            if not (isinstance(c, int) and c == 0):
                dve.wait_ge(s["rp_out"], c)
            dve.wait_ge(s["rp_ps"], c + 1)
            dve.tensor_tensor(rp_s, b[5][:], sin, ALU.mult).then_inc(s["rp_ss"], 1)
            dve.wait_ge(s["rp_cc"], c + 1)
            dve.wait_ge(s["rp_ss"], c + 1)
            dve.tensor_tensor(src, rp_c, rp_s, ALU.add).then_inc(s["rp_out"], 1)

        idx_ropes = [(0, ik)] + [(1 + j, iqs[:, j]) for j in range(4)]

        def pe_in1(pe):
            for u in range(10):
                pe_panel(pe, Panel(N_IN1, 0, 0, u), h_hi, h_lo, s["h_ready"] if u == 0 else None, 2 * KT)
                if u == 1:
                    pe.wait_ge(s["in1"], 1)
                    for tt in range(TT):
                        last = pe.transpose(b[0][:, tt * P:(tt + 1) * P], small[:, tt * P:(tt + 1) * P], ident[:])
                    last.then_inc(s["wt_ps"], 1)
            pe.wait_ge(s["z_gb"], 2)
            pe.wait_ge(s["z_b"], 2)
            for tt in range(TT):
                last = pe.transpose(b[1][:, tt * 40:(tt + 1) * 40], gb[0:40, tt * P:(tt + 1) * P], ident[0:40, 0:40])
            last.then_inc(s["gbt_ps"], 1)
            pe.wait_ge(s["t_in"], 16 * 7)
            pe.wait_ge(s["consts_in"], 48)
            pe.wait_ge(s["in1"], 6)
            for c, src in idx_ropes:
                pe_rope(pe, c, src, swap_i)
            for i in range(2):
                pe_rms(pe, i, b[4])
            for i in range(2):
                pe.wait_ge(s["r_y"], i + 1)
                pe_rope(pe, 5 + i, ak[:, i], swap_a)
            for i in range(2):
                pe.wait_ge(s["in1"], 9 + i)
                for tt in range(TT):
                    last = pe.transpose(b[2 + i][:, tt * P:(tt + 1) * P], av[:, i, tt * P:(tt + 1) * P], ident[:])
                last.then_inc(s["av_ps"], 1)
            pe.wait_ge(s["wt_sb"], 1)
            pe.wait_ge(s["rp_out"], 5)
            i = 0
            for q in range(1, TT):
                for hh in range(IDX_H):
                    if i >= 2:
                        pe.wait_ge(s["lg_r"], i - 1)
                    else:
                        pe.wait_ge(s["gbt_sb"], 1)
                    r = slice(IDX_D * (hh % 2), IDX_D * (hh % 2) + IDX_D)
                    pe.matmul(b[i % 2][:, 0:P * (q + 1)], iqs[r, hh // 2, q * P:(q + 1) * P], ik[r, 0:P * (q + 1)],
                              start=True, stop=True).then_inc(s["lg_ps"], 1)
                    pe_part(pe, Panel(N_IN1, 0, 0, 10 + i // 4), i % 4)
                    i += 1
            for u in range(10 + i // 4, 10 + ATT_H):
                pe_panel(pe, Panel(N_IN1, 0, 0, u), h_hi, h_lo)
            for h in range(ATT_H + 1):
                if h < ATT_H:
                    pe_panel(pe, Panel(N_IN1, 0, 0, 10 + ATT_H + h), h_hi, h_lo)
                if h >= 1:
                    pe.wait_ge(s["r_sq"], h + 2)
                    if h >= 3:
                        pe.wait_ge(s["r_ln"], h)
                    pe.matmul(b[4 + h % 2][:], ones[:], q_sq[:, h - 1], start=True, stop=True).then_inc(s["r_ss"], 1)

        def act_in1(act):
            dst = [small, ik] + [iqs[:, j] for j in range(4)] + [ak[:, 0], ak[:, 1], av[:, 0], av[:, 1]]
            for u in range(10):
                q = Panel(N_IN1, 0, 0, u)
                act_split(act, q.next())
                wait_panel(act, q)
                act.copy(dst[u], g_bank[q.par][:]).then_inc(s["in1"], 1)
                act.wait_ge(s["in1"], u + 1)
                act.sem_inc(bank_free[q.par], 1)
                if u == 1:
                    act.wait_ge(s["wt_ps"], 1)
                    act.mul(w_tok, tiles(b[0][:])[:, :, 64:64 + IDX_H], (IDX_H * IDX_D) ** -0.5).then_inc(s["wt_sb"], 1)
                    act.wait_ge(s["t_in"], 16 * 7)
                    g = gtmp[0:GDN_H, 0]
                    act.activation(g, small[0:GDN_H, :], ACT.Abs, bias=hp[0:GDN_H, 0:1]).then_inc(s["z_ga"], 1)
                    act.activation(hp[0:GDN_H, 2:3], hp[0:GDN_H, 1:2], ACT.Exp).then_inc(s["z_ea"], 1)
                    act.wait_ge(s["z_ga"], 1)
                    act.activation(g, g, ACT.Exp, scale=-1.0).then_inc(s["z_ge"], 1)
                    act.wait_ge(s["z_ge"], 1)
                    act.activation(g, g, ACT.Ln, bias=1.0).then_inc(s["z_gl"], 1)
                    act.wait_ge(s["z_b"], 1)
                    act.activation(gb[32:32 + GDN_H, :], small[32:32 + GDN_H, :], ACT.Tanh, scale=0.5).then_inc(s["z_gt"], 1)
            act.wait_ge(s["gbt_ps"], 1)
            act.copy(gb_tok, b[1][:, 0:TT * 40].rearrange("p (t c) -> p t c", t=TT)).then_inc(s["gbt_sb"], 1)
            for i in range(2):
                act_rms(act, i, ak[:, i], b[4])
            for i in range(2):
                act.wait_ge(s["av_ps"], i + 1)
                act.copy(v_key[i], tiles(b[2 + i][:])).then_inc(s["av_sb"], 1)
            for h in range(ATT_H):
                q = Panel(N_IN1, 0, 0, 10 + h)
                act_split(act, q.next())
                wait_panel(act, q)
                act.activation(o_att[:, h], g_bank[q.par][:], ACT.Tanh, scale=0.5).then_inc(s["gtb_in"], 1)
                act.wait_ge(s["gtb_in"], h + 1)
                act.sem_inc(bank_free[q.par], 1)
            for h in range(ATT_H + 1):
                if h < ATT_H:
                    q = Panel(N_IN1, 0, 0, 10 + ATT_H + h)
                    act_split(act, q.next())
                    wait_panel(act, q)
                    act.copy(q_all[:, h], g_bank[q.par][:]).then_inc(s["aq_in"], 1)
                    act.wait_ge(s["aq_in"], h + 1)
                    act.sem_inc(bank_free[q.par], 1)
                    act.activation(q_sq[:, h], q_all[:, h], ACT.Square).then_inc(s["r_sq"], 1)
                if h >= 1:
                    act.wait_ge(s["r_ss"], h + 2)
                    act.activation(q_sq[:, h - 1], b[4 + h % 2][:], ACT.Ln, scale=1.0 / P, bias=eps[:]).then_inc(s["r_ln"], 1)
            for h in range(ATT_H):
                act.wait_ge(s["r_ln"], h + 3)
                act.activation(q_sq[:, h], q_sq[:, h], ACT.Exp, scale=-0.5).then_inc(s["r_r"], 1)

        def dve_in1(dve):
            dve.memset(gb[0:64, :], 0.0).then_inc(s["z_b"], 1)
            for u in range(10):
                dve_split(dve, Panel(N_IN1, 0, 0, u).next())
                if u == 1:
                    g, m = gtmp[0:GDN_H, 0], gtmp[0:GDN_H, 1]
                    dve.wait_ge(s["in1"], 1)
                    dve.wait_ge(s["t_in"], 16 * 7)
                    dve.tensor_scalar(m, small[0:GDN_H, :], hp[0:GDN_H, 0:1], 0.0, ALU.add, ALU.max).then_inc(s["z_mx"], 1)
                    dve.wait_ge(s["z_mx"], 1)
                    dve.wait_ge(s["z_gl"], 1)
                    dve.tensor_tensor(m, m, g, ALU.add).then_inc(s["z_sp"], 1)
                    dve.wait_ge(s["z_sp"], 1)
                    dve.wait_ge(s["z_ea"], 1)
                    dve.tensor_scalar(m, m, hp[0:GDN_H, 2:3], -1.0, ALU.mult, ALU.mult).then_inc(s["z_g"], 1)
                    dve.wait_ge(s["z_g"], 1)
                    dve.wait_ge(s["z_b"], 1)
                    dve.tensor_tensor_scan(gb[0:GDN_H, :], keep2[0:GDN_H, :], m, 0.0, ALU.mult, ALU.add).then_inc(s["z_gb"], 1)
                    dve.wait_ge(s["z_gt"], 1)
                    bt = gb[32:32 + GDN_H, :]
                    dve.tensor_scalar(bt, bt, 1.0, 0.5, ALU.add, ALU.mult).then_inc(s["z_gb"], 1)
                    dve.sem_inc(s["z_b"], 1)
            for c, src in idx_ropes:
                dve_rope(dve, c, src, si)
            for i in range(2):
                dve_rms(dve, i, ak[:, i], G_KN)
            for i in range(2):
                dve_rope(dve, 5 + i, ak[:, i], sa)
            sco = [None, 0, 256, 640]
            dve.wait_ge(s["wt_sb"], 1)
            i = 0
            for q in range(1, TT):
                n = P * (q + 1)
                acc = sc[:, sco[q]:sco[q] + n]
                for hh in range(IDX_H):
                    dve.wait_ge(s["lg_ps"], i + 1)
                    w = w_tok[:, q, hh:hh + 1]
                    if hh == 0:
                        dve.tensor_scalar(acc, b[i % 2][:, 0:n], 0.0, w, ALU.max, ALU.mult).then_inc(s["lg_r"], 1)
                        dve.wait_ge(s["lg_r"], i + 1)
                        if i:
                            dve.wait_ge(s["lg_a"], i)
                        dve.sem_inc(s["lg_a"], 1)
                    else:
                        lgt = lg[:, i % 2, 0:n]
                        dve.tensor_scalar(lgt, b[i % 2][:, 0:n], 0.0, w, ALU.max, ALU.mult).then_inc(s["lg_r"], 1)
                        dve.wait_ge(s["lg_r"], i + 1)
                        dve.wait_ge(s["lg_a"], i)
                        dve.tensor_tensor(acc, acc, lgt, ALU.add).then_inc(s["lg_a"], 1)
                    i += 1
            dve.wait_ge(s["sc_m"], 3)
            with dve.Fori(0, TOPK // 8):
                for q in range(1, TT):
                    dve.max(out=top8[:, q - 1], in_=sc[:, sco[q]:sco[q] + P * (q + 1)])
                dve.drain()
                for q in range(1, TT):
                    acc = sc[:, sco[q]:sco[q] + P * (q + 1)]
                    dve.match_replace(out=acc, in_to_replace=top8[:, q - 1], in_values=acc, imm_value=TAKEN)
                dve.drain()
            for q in range(1, TT):
                n = P * (q + 1)
                dve.tensor_scalar(sel[:, off[q]:off[q] + n], sc[:, sco[q]:sco[q] + n], TAKEN, 1.0,
                                  ALU.is_equal, ALU.subtract).then_inc(s["sel_r"], 1)
            dve.wait_ge(s["sel_r"], 3)
            dve.wait_ge(s["zsel"], 2)

        def pool_in1(pool):
            pool.wait_ge(s["t_in"], 16 * 7)
            pool.wait_ge(s["in1"], 6)
            for c, src in idx_ropes:
                pool_rope(pool, c, src, ci)
            for i in range(2):
                pool.wait_ge(s["r_y"], i + 1)
                pool_rope(pool, 5 + i, ak[:, i], ca)
            pool.memset(sel[:, 0:P], 0.0).then_inc(s["zsel"], 1)
            pool.wait_ge(s["zsel"], 1)
            pool.affine_select(out=sel[:, 0:P], in_=sel[:, 0:P], compare_op=ALU.is_ge, fill=-1.0, base=0,
                               pattern=[[-1, P]], channel_multiplier=1).then_inc(s["zsel"], 1)
            sco = [None, 0, 256, 640]
            for q in range(1, TT):
                for u in range(3 * q + 8, min(3 * q + 11, 18)):
                    pool_split(pool, Panel(N_IN1, 0, 0, u))
                pool.wait_ge(s["lg_a"], IDX_H * q)
                d = sc[:, sco[q] + P * q:sco[q] + P * (q + 1)]
                pool.affine_select(out=d, in_=d, compare_op=ALU.is_ge, fill=NOT_CAUSAL, base=0,
                                   pattern=[[-1, P]], channel_multiplier=1).then_inc(s["sc_m"], 1)
            for u in range(18, 10 + 2 * ATT_H + 1):
                pool_split(pool, Panel(N_IN1, 0, 0, u))

        HPK = ATT_H // ATT_KV
        S_ORDER = (3, 1, 0, 2)
        s_at = {3: (b[0], 0), 1: (b[2], 0), 0: (b[1], 0), 2: (b[1], P)}
        K_ORDER = (0, 2, 3, 1)
        t_at = {0: (b[3], 0), 2: (g_bank[1], 0), 3: (g_bank[0], 0), 1: (g_bank[0], P)}

        def att_steps(eng, body):
            with eng.Fori(0, HPK - 1) as j:
                body(j, 0, True)
                body(j, 1, True)
            body(HPK - 1, 0, True)
            body(HPK - 1, 1, False)

        def pe_att(pe):
            def front(i, e):
                pe.wait_ge(s["r_y"], i + 3)
                pe_rope(pe, i + 7, aq[:, e], swap_a)
                pe.wait_ge(s["rp_out"], i + 8)
                for q in S_ORDER:
                    bk, o = s_at[q]
                    last = pe.matmul(bk[:, o:o + P * (q + 1)], aq[:, e, q * P:(q + 1) * P], ak[:, e, 0:P * (q + 1)],
                                     start=True, stop=True)
                    if q != 0:
                        last.then_inc(s["s_ps"], 1)

            def body(j, e, more):
                i = 2 * j + e
                if more:
                    pe.wait_ge(s["ms_r"], TT * i + TT)
                    front(i + 1, 1 - e)
                pe.wait_ge(s["pn_r"], TT * i + TT)
                for k in K_ORDER:
                    bk, o = t_at[k]
                    for q in range(k, TT):
                        last = pe.transpose(bk[:, o + (q - k) * P:o + (q - k + 1) * P],
                                            ms[e][:, off[q] + k * P:off[q] + (k + 1) * P], ident[:])
                    if k != 3:
                        last.then_inc(s["pt_ps"], 1)
                pe.wait_ge(s["att_done"], i + 1)
                for n, k in enumerate(K_ORDER):
                    pe.wait_ge(s["pt_sb"], TT * i + n + 1)
                    last = pe.matmul(b[4][:, k * P:SEQ], v_key[e][:, k, :], p_t[:, koff[k]:koff[k] + SEQ - k * P],
                                     start=(n == 0), stop=(n == TT - 1), skip_group_check=True)
                last.then_inc(s["pv_ps"], 1)

            front(0, 0)
            att_steps(pe, body)

        def act_att(act):
            def body(j, e, more):
                i = 2 * j + e
                act.wait_ge(s["nms"], i + 1)
                for q in S_ORDER:
                    m = ms[e][:, off[q]:off[q] + P * (q + 1)]
                    act.activation(m, m, ACT.Exp, scale=P ** -0.5, bias=n_max[:, 4 * e + q:4 * e + q + 1],
                                   accum_out=r_sum[:, q:q + 1]).then_inc(s["ex_a"], 1)
                for n, k in enumerate(K_ORDER):
                    act.wait_ge(s["pt_ps"], (TT - 1) * i + (1, 2, 3, 3)[n])
                    bk, o = t_at[k]
                    act.copy(p_t[:, koff[k]:koff[k] + SEQ - k * P], bk[:, o:o + SEQ - k * P]).then_inc(s["pt_sb"], 1)

            att_steps(act, body)

        def dve_att(dve):
            def queries(j, e):
                i, h = 2 * j + e, j + HPK * e
                dve.wait_ge(s["r_r"], h + 3)
                dve.scalar_tensor_tensor(aq[:, e], q_all[:, bass.ds(h, 1)].rearrange("p a t -> p (a t)"),
                                         gains[:, G_QN:G_QN + 1], q_sq[:, bass.ds(h, 1)].rearrange("p a t -> p (a t)"),
                                         ALU.mult, ALU.mult).then_inc(s["r_y"], 1)

            def output(j, e):
                i, h = 2 * j + e, j + HPK * e
                dve.wait_ge(s["pv_ps"], i + 1)
                o = o_att[:, bass.ds(h, 1)].rearrange("p a t -> p (a t)")
                dve.scalar_tensor_tensor(o, o, 1.0, b[4][:], ALU.add, ALU.mult).then_inc(s["att_done"], 1)

            def scores(i, e):
                for n, q in enumerate(S_ORDER):
                    dve.wait_ge(s["s_ps"], (TT - 1) * i + (1, 2, 3, 3)[n])
                    w = P * (q + 1)
                    bk, o = s_at[q]
                    dve.scalar_tensor_tensor(ms[e][:, off[q]:off[q] + w], sel[:, off[q]:off[q] + w], BIG, bk[:, o:o + w],
                                             ALU.mult, ALU.add).then_inc(s["ms_r"], 1)
                for n, q in enumerate(S_ORDER):
                    dve.wait_ge(s["ms_r"], TT * i + n + 1)
                    dve.tensor_reduce(n_max[:, 4 * e + q:4 * e + q + 1], ms[e][:, off[q]:off[q] + P * (q + 1)], AX.X, ALU.max,
                                      negate=True).then_inc(s["nm_r"], 1)
                dve.wait_ge(s["nm_r"], TT * i + TT)
                nm = n_max[:, 4 * e:4 * e + 4]
                dve.tensor_scalar(nm, nm, P ** -0.5, None, ALU.mult).then_inc(s["nms"], 1)

            def body(j, e, more):
                i = 2 * j + e
                if more:
                    queries(j + e, 1 - e)
                    dve_rope(dve, i + 8, aq[:, 1 - e], sa)
                dve.wait_ge(s["ex_a"], TT * i + TT)
                dve.reciprocal(r_sum, r_sum).then_inc(s["rs_r"], 1)
                dve.wait_ge(s["rs_r"], i + 1)
                for q in S_ORDER:
                    m = ms[e][:, off[q]:off[q] + P * (q + 1)]
                    dve.tensor_scalar(m, m, r_sum[:, q:q + 1], None, ALU.mult).then_inc(s["pn_r"], 1)
                if more:
                    scores(i + 1, 1 - e)
                output(j, e)

            queries(0, 0)
            dve_rope(dve, 7, aq[:, 0], sa)
            scores(0, 0)
            att_steps(dve, body)

        def pool_att(pool):
            with pool.Fori(0, HPK) as j:
                for e in range(2):
                    i = 2 * j + e
                    pool.wait_ge(s["r_y"], i + 3)
                    pool_rope(pool, i + 7, aq[:, e], ca)

        at[0] = 0
        ub = take(SEQ + CONV)
        qkv = take(2 * 3, SEQ)
        tz = take(2, SEQ)
        zg = take(2, SEQ)
        kbe, q_dec = take(SEQ), take(SEQ)
        pick = take(2, P)
        gc_b, be_b, eg_b = take(SEQ), take(SEQ), take(SEQ)
        sq2 = take(2, SEQ)
        kb = take(SEQ)
        dec = take(TT, P)
        ek = take(SEQ)
        a_tr = take(TT, P)
        a_lv = take(2, SEQ)
        t_all = take(2 * TT, P)
        y_m = take(TT, P)
        rr = take(2, SEQ)
        vb_tok, kbe_tok = tiles(rr[:, 0]), tiles(rr[:, 1])
        kdec_tok = take(TT, P)
        u_m, w_t, v_new = take(TT, P), take(SEQ), take(TT, P)
        st = take(2, P)
        assert at[0] <= kept0, (at[0], kept0)
        o_sq, r_o, y_o = sq2[:, 0], rr[:, 0], sq2[:, 1]
        NT = 4 + 2 * (LEVELS - 1)

        def t_m(tt):
            return t_all[:, 4 * (tt // 2) + tt % 2, :]

        def t_t(tt):
            return t_all[:, 4 * (tt // 2) + 2 + tt % 2, :]

        cleared += gla_sems + gate_sems
        sems("c_chain oo_c ub0 c_in c_y c_s tz_t tz_d pick_r bc_ps bc_sb eg_r l_sq l_ss l_ln l_r l_y kb_r vb_r "
             "dm_a dm_b dm_c dec_r ek_a ek_b ek_c kk_ps kk_r qk_ps qk_r kbe_r qd_r tok_ps tok_sb al_r yy_ps y_sb2 "
             "z_ps t_r u_ps2 u_sb ws_ps vn_r kv_ps st2 oo_ps oo_sq oo_ss oo_ln oo_r oo_y1 oo_y2 oo_y3 oo_y4 oo_hi "
             "gdn_done", reuse=True)

        def sp_gdn(sp):
            w = rows(t["w_in_2"][0])
            with sp.Fori(0, GDN_H // 2) as hp2:
                for e in range(2):
                    for u, c in enumerate((QKV0, QKV0 + 1024, QKV0 + 2048, Z0, GTA0)):
                        load(sp, Panel(N_GDN, 10, hp2, 5 * e + u), [(w[:, :, bass.ds(c + P * e + 2 * P * hp2, P)], 0)])

        def gdn_heads(eng, body):
            with eng.Fori(0, GDN_H // 2 - 1) as hp2:
                body(hp2, 0, True)
                body(hp2, 1, True)
            body(GDN_H // 2 - 1, 0, True)
            body(GDN_H // 2 - 1, 1, False)

        def pe_bcast(pe, g, i, bk):
            pe.wait_ge(s["pick_r"], 2 * g + 2)
            pe.matmul(bk[:], pick[0:40, i], gb[0:40, :], start=True, stop=True).then_inc(s["bc_ps"], 1)

        def pe_l2(pe, g, i, bk):
            pe.wait_ge(s["l_sq"], 2 * g + i + 1)
            pe.matmul(bk[:], ones[:], sq2[:, i], start=True, stop=True).then_inc(s["l_ss"], 1)

        def pe_gdn(pe):
            for u in range(3):
                pe_panel(pe, Panel(N_GDN, 10, 0, u), h_hi, h_lo)
            pe_bcast(pe, 0, 0, b[5])
            pe_bcast(pe, 0, 1, b[4])
            pe_panel(pe, Panel(N_GDN, 10, 0, 3), h_hi, h_lo)
            pe_l2(pe, 0, 0, b[3])
            pe.wait_ge(s["bc_sb"], 2)
            pe_l2(pe, 0, 1, b[4])
            pe_panel(pe, Panel(N_GDN, 10, 0, 4), h_hi, h_lo)

            def products(g, e):
                kn, qn = qkv[:, 3 * e + 1], qkv[:, 3 * e]
                pe.wait_ge(s["kb_r"], g + 1)
                for bk, rhs, done in ((b[4], kb, s["kk_ps"]), (b[5], qn, s["qk_ps"])):
                    if rhs is qn:
                        pe.wait_ge(s["l_y"], 2 * g + 2)
                    for tt in range(TT):
                        c = slice(tt * P, (tt + 1) * P)
                        last = pe.matmul(bk[:, c], kn[:, c], rhs[:, c], start=True, stop=True)
                    last.then_inc(done, 1)

            products(0, 0)

            def body(hp2, e, front):
                h = 2 * hp2 + e

                def part(j):
                    eighth(2 * j)
                    eighth(2 * j + 1)

                def eighth(j):
                    k = (j - 16) // 2
                    if front:
                        pe_eighth(pe, Panel(N_GDN, 10, hp2, 5 * (e + 1) + j // 8), j % 8)
                    elif 0 <= k < GDN_H - 1:
                        if j == 16:
                            pe.wait_ge(s["gdn_done"], GDN_H)
                        pe_eighth(pe, Panel(N_WO1, 0, 0, j % 2), k, m_hi, m_lo)

                def token_major(i, src, ready, bk):
                    pe.wait_ge(ready, h + 1)
                    for tt in range(TT):
                        c = slice(tt * P, (tt + 1) * P)
                        last = pe.transpose(bk[:, c], src[:, c], ident[:])
                    last.then_inc(s["tok_ps"], 1)

                vn = qkv[:, 3 * e + 2]
                part(0)
                part(1)
                part(2)
                pe.wait_ge(s["oo_ln"], h + 1)
                for lv in range(LEVELS):
                    pe.wait_ge(s["al_r"], LEVELS * h + lv + 1)
                    al = a_lv[:, lv % 2]
                    for f in range(2):
                        bk = b[2 * f]
                        if lv >= 1:
                            pe.wait_ge(s["t_r"], NT * h + (3 if lv == 1 else 4 + 2 * (lv - 2) + 1) + f)
                        for i in range(2):
                            c = slice((2 * f + i) * P, (2 * f + i + 1) * P)
                            o = bk[:, i * P:(i + 1) * P]
                            if lv == 0:
                                last = pe.transpose(o, al[:, c], ident[:])
                            else:
                                last = pe.matmul(o, al[:, c], t_m(2 * f + i), start=True, stop=True)
                        last.then_inc(s["yy_ps"], 1)
                    if lv == 0:
                        pe.wait_ge(s["kk_r"], h + 1)
                        token_major(0, vn, s["vb_r"], b[4])
                        continue
                    if lv < LEVELS - 1:
                        eighth((6, 8, 10, 13)[lv - 1])
                    for f in range(2):
                        pe.wait_ge(s["y_sb2"], 2 * (LEVELS - 1) * h + 2 * (lv - 1) + f + 1)
                        for side in ((0, 1) if lv < LEVELS - 1 else (1,)):
                            for i in range(2):
                                tt = 2 * f + i
                                o = b[2 * f + 1][:, (2 * side + i) * P:(2 * side + i + 1) * P]
                                if side == 0:
                                    last = pe.matmul(o, t_t(tt), y_m[:, tt, :], start=True, stop=True)
                                else:
                                    last = pe.matmul(o, y_m[:, tt, :], t_t(tt), start=True, stop=True)
                        last.then_inc(s["z_ps"], 1)
                    if lv < LEVELS - 1:
                        for j in ((7,), (9,), (11, 12), ())[lv - 1]:
                            eighth(j)
                    if lv == 1:
                        pe.wait_ge(s["qk_r"], h + 1)
                        token_major(1, kbe, s["kbe_r"], b[5])
                    if lv == 2:
                        pe.wait_ge(s["tok_sb"], 3 * h + 1)
                        token_major(2, ek, s["ek_c"], b[4])
                    if lv == 3 and front:
                        pe.wait_ge(s["tok_sb"], 3 * h + 2)
                        pe_bcast(pe, h + 1, 0, b[5])
                    if lv == 4 and front:
                        pe.wait_ge(s["tok_sb"], 3 * h + 3)
                        pe_bcast(pe, h + 1, 1, b[4])
                pe.wait_ge(s["tok_sb"], 3 * h + 3)
                if front:
                    pe.wait_ge(s["bc_sb"], 2 * h + 4)
                for f in range(2):
                    pe.wait_ge(s["t_r"], NT * (h + 1) - 1 + f)
                    for tt in (2 * f, 2 * f + 1):
                        c = slice(tt * P, (tt + 1) * P)
                        pe.matmul(b[2 * f + 1][:, c], t_t(tt), vb_tok[:, tt, :], start=True, stop=True)
                        last = pe.matmul(b[4][:, c], kbe_tok[:, tt, :], t_t(tt), start=True, stop=True)
                last.then_inc(s["u_ps2"], 1)
                eighth(14)
                eighth(15)
                for c in range(NCH):
                    r = slice(CHUNK * (c % 2), CHUNK * (c % 2) + CHUNK)
                    cc = slice(CHUNK * c, CHUNK * (c + 1))
                    if c:
                        pe.wait_ge(s["st2"], (NCH - 1) * h + c)
                        pe.matmul(b[5][r, 0:P], w_t[:, cc], st[:, c % 2], start=True, stop=True).then_inc(s["ws_ps"], 1)
                        if c == 1:
                            pe.wait_ge(s["qd_r"], h + 1)
                        pe.matmul(b[1 + c % 2][:, (c // 2) * P:(c // 2) * P + CHUNK], st[:, c % 2], q_dec[:, cc],
                                  start=True, stop=True, skip_group_check=True)
                    if c == 5 and front:
                        pe_l2(pe, h + 1, 0, b[3])
                    if c == 6 and front:
                        pe_l2(pe, h + 1, 1, b[4])
                    eighth(16 + 2 * c)
                    if c < NCH - 1:
                        pe.wait_ge(s["vn_r"], NCH * h + c + 1)
                        pe.matmul(b[0][:, 0:P], kdec_tok[r, c // 2, :], v_new[r, c // 2, :],
                                  start=True, stop=True).then_inc(s["kv_ps"], 1)
                    eighth(17 + 2 * c)
                pe.wait_ge(s["vn_r"], NCH * (h + 1))
                pe.wait_ge(s["qk_r"], h + 1)
                if front:
                    pe.wait_ge(s["l_ln"], 2 * h + 3)
                for tt in range(TT):
                    last = pe.matmul(b[3][:, tt * P:(tt + 1) * P], v_new[:, tt, :], dec[:, tt, :],
                                     start=True, stop=True)
                last.then_inc(s["oo_ps"], 1)
                for j in range(16, 20):
                    part(j)
                if front:
                    products(h + 1, 1 - e)
                pe.wait_ge(s["oo_sq"], h + 1)
                pe.matmul(b[0][:], ones[:], o_sq, start=True, stop=True).then_inc(s["oo_ss"], 1)

            gdn_heads(pe, body)

        def act_conv_in(act, g, q, u):
            wait_panel(act, q)
            act.wait_ge(s["ub0"], 3 * g + u + 1)
            act.copy(ub[:, CONV - 1:CONV - 1 + SEQ], g_bank[q.par][:]).then_inc(s["c_in"], 1)
            act.wait_ge(s["c_in"], 3 * g + u + 1)
            act.sem_inc(bank_free[q.par], 1)

        def act_tanh(act, i, par, src):
            if not (isinstance(i, int) and i < 2):
                act.wait_ge(s["tz_d"], i - 1)
            act.activation(tz[:, par], src, ACT.Tanh, scale=0.5).then_inc(s["tz_t"], 1)

        def act_l2(act, g, banks):
            for i in range(2):
                act.wait_ge(s["l_ss"], 2 * g + i + 1)
                act.activation(rr[:, i], banks[i][:], ACT.Ln, scale=0.25, bias=eps[:]).then_inc(s["l_ln"], 1)
            for i in range(2):
                act.wait_ge(s["l_ln"], 2 * g + i + 1)
                act.activation(rr[:, i], rr[:, i], ACT.Exp, scale=-0.5).then_inc(s["l_r"], 1)

        def act_bcast(act, g, i, bk):
            act.wait_ge(s["bc_ps"], 2 * g + i + 1)
            act.copy(gc_b if i == 0 else be_b, bk[:]).then_inc(s["bc_sb"], 1)

        def act_gdn(act):
            for u in range(5):
                q = Panel(N_GDN, 10, 0, u)
                act_split(act, q.next())
                if u < 3:
                    act_conv_in(act, 0, q, u)
                    act.wait_ge(s["c_y"], u + 1)
                    act_tanh(act, u, u % 2, qkv[:, u])
                else:
                    wait_panel(act, q)
                    act_tanh(act, u, u % 2, g_bank[q.par][:])
                if u == 2:
                    act_bcast(act, 0, 0, b[5])
                    act_bcast(act, 0, 1, b[4])
                    for i in range(2):
                        act.wait_ge(s["c_s"], i + 1)
                        act.activation(sq2[:, i], qkv[:, i], ACT.Square).then_inc(s["l_sq"], 1)
                if u == 3:
                    act_l2(act, 0, (b[3], b[4]))
            act_decays(act, 0)
            act.wait_ge(s["ek_a"], 1)
            act.activation(ek, ek, ACT.Exp, scale=-1.0).then_inc(s["ek_b"], 1)
            act.sem_inc(s["oo_ln"], 1)
            act_split(act, Panel(N_GDN, 10, 0, 6))

            def body(hp2, e, front):
                h = 2 * hp2 + e
                g = h + 1
                o = 3 * (1 - e)

                def q(u):
                    return Panel(N_GDN, 10, hp2, 5 * (e + 1) + u)

                def tanh(u, src):
                    act_tanh(act, 10 * hp2 + 5 * (e + 1) + u, (e + 1 + u) % 2, src)

                def tok(i):
                    act.wait_ge(s["tok_ps"], 3 * h + i + 1)
                    act.copy((vb_tok, kbe_tok, kdec_tok)[i], tiles(b[(4, 5, 4)[i]][:])).then_inc(s["tok_sb"], 1)

                def level(lv):
                    for f in range(2):
                        act.wait_ge(s["yy_ps"], 2 * LEVELS * h + 2 * lv + f + 1)
                        act.copy(y_m[:, 2 * f:2 * f + 2], b[2 * f][:, 0:2 * P].rearrange("p (t c) -> p t c", t=2)
                                 ).then_inc(s["y_sb2"], 1)

                level(1)
                tok(0)
                if front:
                    act_conv_in(act, g, q(0), 0)
                level(2)
                tok(1)
                if front:
                    act_split(act, q(2))
                level(3)
                tok(2)
                level(4)
                if front:
                    act_bcast(act, g, 0, b[5])
                level(5)
                if front:
                    act_bcast(act, g, 1, b[4])
                    act.wait_ge(s["c_y"], 3 * g + 1)
                    tanh(0, qkv[:, o])
                act.wait_ge(s["u_ps2"], h + 1)
                for f in range(2):
                    act.copy(u_m[:, 2 * f:2 * f + 2], tiles(b[2 * f + 1][:])[:, 2 * f:2 * f + 2]).then_inc(s["u_sb"], 1)
                act.copy(w_t, b[4][:]).then_inc(s["u_sb"], 1)
                if front:
                    act_conv_in(act, g, q(1), 1)
                    act_split(act, q(3))
                    act.wait_ge(s["c_s"], 3 * g + 1)
                    act.activation(sq2[:, 0], qkv[:, o], ACT.Square).then_inc(s["l_sq"], 1)
                    act.wait_ge(s["c_y"], 3 * g + 2)
                    tanh(1, qkv[:, o + 1])
                    act.wait_ge(s["c_s"], 3 * g + 2)
                    act.activation(sq2[:, 1], qkv[:, o + 1], ACT.Square).then_inc(s["l_sq"], 1)
                    act_conv_in(act, g, q(2), 2)
                    act_split(act, q(4))
                    act_l2(act, g, (b[3], b[4]))
                    act.wait_ge(s["c_y"], 3 * g + 3)
                    tanh(2, qkv[:, o + 2])
                    act.wait_ge(s["st2"], (NCH - 1) * (h + 1))
                    act_decays(act, g)
                    act_split(act, q(5))
                    wait_panel(act, q(3))
                    tanh(3, g_bank[q(3).par][:])
                act.wait_ge(s["oo_y1"], h + 1)
                act.activation(o_sq, y_m.rearrange("p t c -> p (t c)"), ACT.Square).then_inc(s["oo_sq"], 1)
                if front:
                    act.wait_ge(s["ek_a"], g + 1)
                    act.activation(ek, ek, ACT.Exp, scale=-1.0).then_inc(s["ek_b"], 1)
                act.wait_ge(s["oo_ss"], h + 1)
                act.activation(r_o, b[0][:], ACT.Ln, scale=1.0 / P, bias=eps[:]).then_inc(s["oo_ln"], 1)
                act.wait_ge(s["oo_ln"], h + 2)
                act.activation(r_o, r_o, ACT.Exp, scale=-0.5).then_inc(s["oo_r"], 1)
                if front:
                    wait_panel(act, q(4))
                    tanh(4, g_bank[q(4).par][:])
                if front:
                    act_split(act, q(6))
                act.wait_ge(s["oo_y4"], h + 1)
                act.mul(m_hi[:, bass.ds(h, 1)].rearrange("p a t -> p (a t)"), y_o, 0.5).then_inc(s["oo_hi"], 1)

            gdn_heads(act, body)

        def act_decays(act, g):
            act.wait_ge(s["dm_b"], g + 1)
            act.activation(dec, dec, ACT.Exp).then_inc(s["dm_c"], 1)
            act.activation(eg_b, gc_b, ACT.Exp).then_inc(s["eg_r"], 1)

        def dve_gdn(dve):
            dve.memset(ub[:, 0:CONV - 1], 0.0).then_inc(s["memsets"], 1)
            dve.sem_inc(s["ub0"], 1)
            dve.sem_inc(s["gdn_done"], 1)
            dve.wait_ge(s["memsets"], 4)

            def head(hp2, e):
                g = 2 * hp2 + e
                o = 3 * (e % 2)

                def picks():
                    for i in range(2):
                        dve.tensor_copy(pick[0:40, i], ident[0:40, bass.ds(32 * i + g, 1)].broadcast_to([40, P])
                                        ).then_inc(s["pick_r"], 1)

                def conv(u, steps):
                    y = qkv[:, o + u]
                    for jj in steps:
                        w = conv_w[:, bass.ds(jj * 24 + u * 8 + g, 1)]
                        if jj == 0:
                            dve.wait_ge(s["c_in"], 3 * g + u + 1)
                            dve.tensor_scalar(y, ub[:, 0:SEQ], w, None, ALU.mult).then_inc(s["c_chain"], 1)
                        else:
                            dve.wait_ge(s["c_chain"], 9 * g + 3 * u + jj)
                            dve.scalar_tensor_tensor(y, ub[:, jj:jj + SEQ], w, y, ALU.mult, ALU.add
                                                     ).then_inc(s["c_chain"] if jj < CONV - 1 else s["c_y"], 1)
                        if jj == CONV - 1:
                            dve.wait_ge(s["c_y"], 3 * g + u + 1)
                            dve.sem_inc(s["ub0"], 1)

                def tanh_in(u):
                    i = 10 * hp2 + 5 * e + u
                    dve.wait_ge(s["tz_t"], i + 1)
                    return tz[:, (5 * e + u) % 2], i

                def silu(u):
                    y = qkv[:, o + u]
                    th, i = tanh_in(u)
                    dve.scalar_tensor_tensor(y, th, 1.0, y, ALU.add, ALU.mult).then_inc(s["c_s"], 1)
                    dve.wait_ge(s["c_s"], 3 * g + u + 1)
                    dve.sem_inc(s["tz_d"], 1)

                def gate_z(q):
                    th, i = tanh_in(3)
                    dve.scalar_tensor_tensor(zg[:, e % 2], th, 1.0, g_bank[q.par][:], ALU.add, ALU.mult).then_inc(s["tz_d"], 1)
                    dve.wait_ge(s["tz_d"], i + 1)
                    dve.sem_inc(bank_free[q.par], 1)

                def gate_a(q):
                    th, i = tanh_in(4)
                    dve.sem_inc(bank_free[q.par], 1)
                    dve.wait_ge(s["tz_d"], i)
                    dve.scalar_tensor_tensor(zg[:, e % 2], th, 1.0, zg[:, e % 2], ALU.add, ALU.mult).then_inc(s["tz_d"], 1)

                def decays():
                    dve.wait_ge(s["bc_sb"], 2 * g + 2)
                    g_tok = gb_tok[:, :, bass.ds(g, 1)].broadcast_to([P, TT, P])
                    dve.tensor_tensor(dec, tiles(gc_b), g_tok, ALU.subtract).then_inc(s["dm_a"], 1)
                    dve.wait_ge(s["dm_a"], g + 1)
                    dve.tensor_scalar(dec, dec, 0.0, None, ALU.min).then_inc(s["dm_b"], 1)

                def to_end():
                    ends = gc_b.rearrange("p (c t) -> p c t", t=CHUNK)
                    dve.tensor_tensor(ek.rearrange("p (c t) -> p c t", t=CHUNK), ends,
                                      ends[:, :, CHUNK - 1:CHUNK].broadcast_to([P, NCH, CHUNK]), ALU.subtract).then_inc(s["ek_a"], 1)

                def l2(i):
                    f = (0.5 * P ** -0.5, 0.5)[i]
                    dve.wait_ge(s["l_r"], 2 * g + 2)
                    dve.scalar_tensor_tensor(qkv[:, o + i], qkv[:, o + i], f, rr[:, i], ALU.mult, ALU.mult).then_inc(s["l_y"], 1)

                def beta_k():
                    dve.wait_ge(s["l_y"], 2 * g + 1)
                    dve.tensor_tensor(kb, qkv[:, o + 1], be_b, ALU.mult).then_inc(s["kb_r"], 1)

                def beta_v():
                    dve.scalar_tensor_tensor(qkv[:, o + 2], qkv[:, o + 2], 0.5, be_b, ALU.mult, ALU.mult).then_inc(s["vb_r"], 1)

                return picks, conv, silu, gate_z, gate_a, decays, to_end, l2, beta_k, beta_v

            def products(g):
                dve.wait_ge(s["kk_ps"], g + 1)
                dve.wait_ge(s["dec_r"], g + 1)
                dve.tensor_tensor(a_tr, tiles(b[4][:]), dec, ALU.mult).then_inc(s["kk_r"], 1)
                dve.wait_ge(s["kk_r"], g + 1)
                dve.wait_ge(s["qk_ps"], g + 1)
                dve.tensor_tensor(dec, tiles(b[5][:]), dec, ALU.mult).then_inc(s["qk_r"], 1)

            def first_level(g):
                eye = ident[:].unsqueeze(1).broadcast_to([P, 2, P])
                dve.wait_ge(s["al_r"], LEVELS * g + 1)
                for f in range(2):
                    dve.tensor_tensor(t_all[:, 4 * f + 2:4 * f + 4], eye, tiles(a_lv[:, 0])[:, 2 * f:2 * f + 2],
                                      ALU.subtract).then_inc(s["t_r"], 1)
                for f in range(2):
                    dve.wait_ge(s["yy_ps"], 2 * LEVELS * g + f + 1)
                    dve.tensor_tensor(t_all[:, 4 * f:4 * f + 2], eye, b[2 * f][:, 0:2 * P].rearrange("p (t c) -> p t c", t=2),
                                      ALU.subtract).then_inc(s["t_r"], 1)

            picks, conv, silu, gate_z, gate_a, decays, to_end, l2, beta_k, beta_v = head(0, 0)
            picks()
            dve.wait_ge(s["w_ready"], N_GDN + 3)
            for u in range(5):
                q0 = Panel(N_GDN, 10, 0, u)
                dve_split(dve, q0.next())
                if u < 3:
                    conv(u, range(CONV))
                    silu(u)
                if u == 2:
                    decays()
                    to_end()
                if u == 3:
                    gate_z(q0)
                    l2(1)
                    beta_k()
                    l2(0)
                    beta_v()
                if u == 4:
                    gate_a(q0)
            products(0)
            first_level(0)
            dve_split(dve, Panel(N_GDN, 10, 0, 6))

            def body(hp2, e, front):
                h = 2 * hp2 + e
                picks, conv, silu, gate_z, gate_a, decays, to_end, l2, beta_k, beta_v = head(hp2, e + 1)

                def q(u):
                    return Panel(N_GDN, 10, hp2, 5 * (e + 1) + u)

                if front:
                    dve.wait_ge(s["bc_ps"], 2 * h + 2)
                    picks()
                for lv in range(1, LEVELS):
                    for f in range(2):
                        dve.wait_ge(s["z_ps"], 2 * (LEVELS - 1) * h + 2 * (lv - 1) + f + 1)
                        dve.wait_ge(s["t_r"], NT * h + 4 + 2 * (lv - 1) + (f if lv > 1 else 0))
                        o = 0 if lv < LEVELS - 1 else 2
                        dve.tensor_tensor(t_all[:, 4 * f + o:4 * f + 4], t_all[:, 4 * f + o:4 * f + 4],
                                          tiles(b[2 * f + 1][:])[:, o:], ALU.subtract).then_inc(s["t_r"], 1)
                    if front:
                        if lv >= 2:
                            conv(0, (lv - 2,))
                        if lv == 3:
                            dve_split(dve, q(2))
                if front:
                    silu(0)
                dve.wait_ge(s["u_sb"], 3 * h + 3)
                for c in range(NCH):
                    r = slice(CHUNK * (c % 2), CHUNK * (c % 2) + CHUNK)
                    if c == 0:
                        dve.tensor_copy(v_new[r, 0], u_m[r, 0]).then_inc(s["vn_r"], 1)
                    else:
                        dve.wait_ge(s["ws_ps"], (NCH - 1) * h + c)
                        dve.tensor_tensor(v_new[r, c // 2], u_m[r, c // 2], b[5][r, 0:P], ALU.subtract).then_inc(s["vn_r"], 1)
                    if front:
                        if c in (1, 2):
                            conv(1, (2 * c - 1,))
                        elif c == 3:
                            silu(1)
                        elif c in (4, 5):
                            conv(2, (2 * (c - 4),))
                    if c < NCH - 1:
                        dve.wait_ge(s["kv_ps"], (NCH - 1) * h + c + 1)
                        e1 = CHUNK * (c + 1) - 1
                        if c == 0:
                            dve.tensor_copy(st[:, 1], b[0][:, 0:P]).then_inc(s["st2"], 1)
                        else:
                            dve.wait_ge(s["st2"], (NCH - 1) * h + c)
                            dve.scalar_tensor_tensor(st[:, (c + 1) % 2], st[:, c % 2], eg_b[:, e1:e1 + 1], b[0][:, 0:P],
                                                     ALU.mult, ALU.add).then_inc(s["st2"], 1)
                    if front:
                        if c < 2:
                            conv(1, (2 * c,))
                        elif c == 2:
                            dve_split(dve, q(3))
                        elif c in (4, 5):
                            conv(2, (2 * (c - 4) + 1,))
                        elif c == 6:
                            dve_split(dve, q(4))
                dve.wait_ge(s["oo_ps"], h + 1)
                if front:
                    decays()
                    l2(1)
                    beta_k()
                    l2(0)
                    dve_split(dve, q(5))
                dve.tensor_copy(y_m, tiles(b[3][:])).then_inc(s["oo_c"], 1)
                dve.wait_ge(s["oo_c"], 3 * h + 1)
                yv = y_m.rearrange("p t (e c) -> p t e c", e=2)
                dve.tensor_tensor(yv[:, 1:, 0], yv[:, 1:, 0], tiles(b[1][:])[:, 1:, 0:CHUNK], ALU.add).then_inc(s["oo_c"], 1)
                dve.tensor_tensor(yv[:, :, 1], yv[:, :, 1], tiles(b[2][:])[:, :, 0:CHUNK], ALU.add).then_inc(s["oo_c"], 1)
                dve.wait_ge(s["oo_c"], 3 * h + 3)
                dve.sem_inc(s["oo_y1"], 1)
                if front:
                    silu(2)
                    gate_z(q(3))
                    to_end()
                    beta_v()
                dve.wait_ge(s["tz_d"], 10 * hp2 + 5 * e + 5)
                dve.scalar_tensor_tensor(y_o, y_m.rearrange("p t c -> p (t c)"), gains[:, G_GDN:G_GDN + 1], zg[:, e],
                                         ALU.mult, ALU.mult).then_inc(s["oo_y2"], 1)
                if front:
                    products(h + 1)
                    first_level(h + 1)
                dve.wait_ge(s["oo_y2"], h + 1)
                dve.wait_ge(s["oo_r"], h + 1)
                dve.tensor_tensor(y_o, y_o, r_o, ALU.mult).then_inc(s["oo_y3"], 1)
                dve.wait_ge(s["oo_y3"], h + 1)
                dve.tensor_tensor(y_o, y_o, o_att[:, bass.ds(h, 1)].rearrange("p a t -> p (a t)"), ALU.add).then_inc(s["oo_y4"], 1)
                dve.wait_ge(s["oo_y4"], h + 1)
                if front:
                    gate_a(q(4))
                if front:
                    dve_split(dve, q(6))
                dve.wait_ge(s["oo_hi"], h + 1)
                dve.scalar_tensor_tensor(m_lo[:, bass.ds(h, 1)].rearrange("p a t -> p (a t)"), y_o, 0.5,
                                         m_hi[:, bass.ds(h, 1)].rearrange("p a t -> p (a t)").bitcast(F32),
                                         ALU.mult, ALU.subtract).then_inc(s["gdn_done"], 1)

            gdn_heads(dve, body)

        def pool_gdn(pool):
            with pool.Fori(0, GDN_H // 2) as hp2:
                for e in range(2):
                    h = 2 * hp2 + e
                    qn, kn = qkv[:, 3 * e], qkv[:, 3 * e + 1]
                    pool.wait_ge(s["dm_c"], h + 1)
                    pool.tensor_tensor(dec, dec, mask(LEVELS + 1), ALU.mult).then_inc(s["dec_r"], 1)
                    for lv in range(LEVELS):
                        pool.wait_ge(s["kk_r"], h + 1)
                        if lv >= 2:
                            pool.wait_ge(s["yy_ps"], 2 * LEVELS * h + 2 * lv - 2)
                            if lv == 2:
                                pool.wait_ge(s["t_r"], NT * h + 2)
                        pool.tensor_tensor(tiles(a_lv[:, lv % 2]), a_tr, mask(lv + 1), ALU.mult).then_inc(s["al_r"], 1)
                        if lv == 1:
                            pool.wait_ge(s["kb_r"], h + 1)
                            pool.wait_ge(s["eg_r"], h + 1)
                            pool.tensor_tensor(kbe, kb, eg_b, ALU.mult).then_inc(s["kbe_r"], 1)
                        if lv == 2:
                            pool.wait_ge(s["ek_b"], h + 1)
                            pool.wait_ge(s["l_y"], 2 * h + 2)
                            pool.tensor_tensor(ek, ek, kn, ALU.mult).then_inc(s["ek_c"], 1)
                    pool.tensor_tensor(q_dec, qn, eg_b, ALU.mult).then_inc(s["qd_r"], 1)

        at[0] = 0
        rl, sq, down = take(2, SEQ), take(2, SEQ), take(2, SEQ)
        mlp_sq, mlp_acc, r_sqr = take(2, SEQ), take(SEQ), take(SEQ)
        assert at[0] <= norms0
        at[0] = norms0
        y_tok = take(TT, D)

        block = ctx.enter_context(nc.Block())

        @block.sync
        def _(sp):
            sp_start(sp)
            sp_gla(sp)
            sp_panels(sp, N_WO0, rows(t["l0_w_out"]))
            sp_mlp(sp, N_FF0, t["l0_w_ff1"], t["l0_w_ff2"])
            sp_in1(sp)
            sp_gdn(sp)
            sp_panels(sp, N_WO1, rows(t["w_out_2"][0]))
            sp_mlp(sp, N_FF1, t["w_mlp_up_2"][0], t["w_mlp_down_2"][0])
            sp_out(sp)

        @block.tensor
        def _(pe):
            pe_start(pe)
            pe_norm(pe)
            pe.wait_ge(s["memsets"], 3)
            fence(pe, 1)
            pe_gates(pe)
            pe_gla(pe)
            pe.wait_ge(s["gla_done"], GLA_H + 1)
            fence(pe, 2)
            pe_wout(pe, N_WO0, 0, 2 * (GLA_H - 1))
            pe_mlp(pe, N_FF0, 0, KT)
            fence(pe, 3)
            pe_two_norms(pe)
            pe_in1(pe)
            pe_att(pe)
            fence(pe, 4)
            pe_gdn(pe)
            pe.wait_ge(s["gdn_done"], GDN_H + 1)
            fence(pe, 5)
            pe_wout(pe, N_WO1, 1, GDN_H - 1)
            pe_mlp(pe, N_FF1, 1, 3 * KT)
            pe_out(pe, KT - 1)

        @block.scalar
        def _(act):
            act_start(act)
            act_split(act, Panel(N_GK, 0, 0, 0))
            fence(act, 1)
            act_norm(act)
            act_gates(act)
            act_gla(act)
            fence(act, 2)
            act_wout(act, N_WO0, 0, G_FFN0)
            act_mlp(act, N_FF0, 0)
            fence(act, 3)
            act_two_norms(act)
            act_in1(act)
            act_att(act)
            fence(act, 4)
            act_gdn(act)
            fence(act, 5)
            act_wout(act, N_WO1, 1, G_MLP1)
            act_mlp(act, N_FF1, 1)
            act_out(act, KT - 1)

        @block.vector
        def _(dve):
            dve_start(dve)
            dve_split(dve, Panel(N_GK, 0, 0, 0))
            fence(dve, 1)
            dve_norm(dve)
            dve_gates(dve)
            dve_gla(dve)
            fence(dve, 2)
            for done in gla_sems + gate_sems:
                dve.sem_clear(done)
            dve.sem_inc(s["hid_ready"], 2)
            dve.sem_inc(s["down_done"], 1)
            dve_wout(dve, N_WO0, 0, G_FFN0)
            dve_mlp(dve, N_FF0, 0)
            fence(dve, 3)
            dve.sem_inc(s["att_done"], 1)
            dve_two_norms(dve)
            dve_in1(dve)
            dve_att(dve)
            fence(dve, 4)
            dve_gdn(dve)
            fence(dve, 5)
            dve_wout(dve, N_WO1, 1, G_MLP1)
            dve_mlp(dve, N_FF1, 1)

        @block.gpsimd
        def _(pool):
            fence(pool, 1)
            pool_gla(pool)
            fence(pool, 2)
            pool_squares(pool)
            fence(pool, 3)
            pool_in1(pool)
            pool_att(pool)
            fence(pool, 4)
            pool_gdn(pool)
            fence(pool, 5)


NAMES = ["x", "l0_norm_mix", "l0_w_in", "l0_w_gk_up", "l0_b_gk", "l0_g_onorm", "l0_w_out", "l0_norm_ffn",
         "l0_w_ff1", "l0_w_ff2", "final_norm", "norm_mix_g_2", "w_in_2", "conv_w_2", "a_log_2", "dt_bias_2",
         "gdn_norm_g_2", "q_norm_g_2", "k_norm_g_2", "w_out_2", "norm_mlp_g_2", "w_mlp_up_2", "w_mlp_down_2"]


def kernel(**inputs):
    import concourse.bacc as bacc
    from concourse.bass_utils import run_bass_kernel_spmd

    nc = bacc.Bacc("TRN2", target_bir_lowering=False, num_devices=1)
    arrays = {f"in_{n}": np.ascontiguousarray(inputs[n]) for n in NAMES}
    square, wide = host_constants()
    arrays["const_square"], arrays["const_wide"] = square, wide
    aps = {k: nc.dram_tensor(k, a.shape, mybir.dt.from_np(a.dtype), kind="ExternalInput").ap()
           for k, a in arrays.items()}
    out = nc.dram_tensor("out", (1, SEQ, D), F32, kind="ExternalOutput").ap()
    build(nc, {n: aps[f"in_{n}"] for n in NAMES}, out, aps["const_square"], aps["const_wide"])
    r = run_bass_kernel_spmd(nc, [arrays], core_ids=[0])
    return r.results[0]["out"]
```
